# Optimizing a Trainium2 kernel written in Bass

```python
import jax, jax.numpy as jnp
from jax import lax
import numpy as np

D_MODEL = 1024
BATCH = 1
SEQ = 256
DEPTH = 2
DEC_BATCH = 8
DEC_SEQ = 8
PAST_LEN = 2048
PAGE_SIZE = 128

N_MIXERS = 2
N_RWKV = (DEPTH + 1) // 2
N_CONV = DEPTH // 2
N_META = 16
HEAD_DIM = 64
N_HEADS = D_MODEL // HEAD_DIM
D_DECAY_LORA = 64
D_AAA_LORA = 64
D_GATE_LORA = 160
D_FF = 2816
CONV_W = 3
RMS_EPS = 1e-6
GN_EPS = 64e-5

kernel_name = "rwkv7_shortconv_macaron_hybrid_step"

def _rmsnorm(x, g):
    x32 = x.astype(jnp.float32)
    y = x32 * lax.rsqrt(jnp.mean(x32 * x32, axis=-1, keepdims=True) + RMS_EPS)
    return (y * g.astype(jnp.float32)).astype(x.dtype)

def _swiglu(x, w_gu, w_down):
    gate, up = jnp.split(x @ w_gu, 2, axis=-1)
    return (jax.nn.silu(gate) * up) @ w_down

def _rwkv7_time_mix(h, wkv0, shift0, mu, w_rkv, w0, w1, w2, a0, a1, a2, g1, g2,
                    k_k, k_a, r_k, ln_w, ln_b, w_o):
    bsz, t_len, _ = h.shape
    f32 = jnp.float32
    prev = jnp.concatenate([shift0[:, None, :].astype(h.dtype), h[:, :-1]], axis=1)
    xx = prev - h
    xr, xw, xk, xv, xa, xg = [h + xx * mu[c] for c in range(6)]
    r = xr @ w_rkv[0]
    k = xk @ w_rkv[1]
    v = xv @ w_rkv[2]
    w = -jax.nn.softplus(-(w0 + jnp.tanh(xw @ w1) @ w2)) - 0.5
    decay = jnp.exp(-jnp.exp(w.astype(f32)))
    a = jax.nn.sigmoid(a0 + (xa @ a1) @ a2)
    g = jax.nn.sigmoid(xg @ g1) @ g2
    kk = (k * k_k).astype(f32).reshape(bsz, t_len, N_HEADS, HEAD_DIM)
    kk = kk / jnp.maximum(jnp.linalg.norm(kk, axis=-1, keepdims=True), 1e-12)
    k = k * (1.0 + (a - 1.0) * k_a)

    def heads(z):
        return z.astype(f32).reshape(bsz, t_len, N_HEADS, HEAD_DIM)

    r_h, k_h, v_h, a_h, d_h = heads(r), heads(k), heads(v), heads(a), heads(decay)
    b_h = kk * a_h

    def step(S, inp):
        r_t, d_t, k_t, v_t, kk_t, b_t = inp
        S = (S * d_t[..., None, :]
             + jnp.einsum('bhij,bhj->bhi', S, -kk_t)[..., None] * b_t[..., None, :]
             + v_t[..., :, None] * k_t[..., None, :])
        return S, jnp.einsum('bhij,bhj->bhi', S, r_t)

    tm = lambda z: jnp.swapaxes(z, 0, 1)
    S_fin, ys = lax.scan(step, wkv0.astype(f32),
                         (tm(r_h), tm(d_h), tm(k_h), tm(v_h), tm(kk), tm(b_h)))
    y = tm(ys)
    mean = jnp.mean(y, axis=-1, keepdims=True)
    var = jnp.mean(jnp.square(y - mean), axis=-1, keepdims=True)
    yn = ((y - mean) * lax.rsqrt(var + GN_EPS)).reshape(bsz, t_len, D_MODEL)
    yn = yn * ln_w.astype(f32) + ln_b.astype(f32)
    bonus = jnp.sum(r_h * k_h * r_k.astype(f32), axis=-1, keepdims=True) * v_h
    o = ((yn + bonus.reshape(bsz, t_len, D_MODEL)) * g.astype(f32)).astype(h.dtype)
    return o @ w_o, S_fin.astype(wkv0.dtype), h[:, -1].astype(shift0.dtype)

def _short_conv_mix(h, conv0, w_in, conv_w, w_out):
    t_len = h.shape[1]
    gate_b, gate_c, xin = jnp.split(h @ w_in, 3, axis=-1)
    u = gate_c * xin
    pad = jnp.concatenate([conv0.astype(u.dtype), u], axis=1)
    conv = pad[:, 0:t_len] * conv_w[0] + pad[:, 1:t_len + 1] * conv_w[1] + pad[:, 2:t_len + 2] * conv_w[2]
    return (gate_b * conv) @ w_out, pad[:, -(CONV_W - 1):].astype(conv0.dtype)

def _trunk(x, wkv_in, shift_in, conv_in, p):
    new_wkv, new_shift, new_conv = [], [], []
    for i in range(DEPTH):
        x = x + 0.5 * _swiglu(_rmsnorm(x, p['ffn_norm'][i, 0]), p['ffn_w_gu'][i, 0], p['ffn_w_down'][i, 0])
        hn = _rmsnorm(x, p['mix_norm'][i])
        j = i // N_MIXERS
        if i % N_MIXERS == 0:
            out, s_wkv, s_shift = _rwkv7_time_mix(
                hn, wkv_in[j], shift_in[j], p['rk_mu'][j], p['rk_w_rkv'][j], p['rk_w0'][j],
                p['rk_w1'][j], p['rk_w2'][j], p['rk_a0'][j], p['rk_a1'][j], p['rk_a2'][j],
                p['rk_g1'][j], p['rk_g2'][j], p['rk_k_k'][j], p['rk_k_a'][j], p['rk_r_k'][j],
                p['rk_ln_w'][j], p['rk_ln_b'][j], p['rk_w_o'][j])
            new_wkv.append(s_wkv)
            new_shift.append(s_shift)
        else:
            out, s_conv = _short_conv_mix(hn, conv_in[j], p['sc_w_in'][j], p['sc_conv_w'][j], p['sc_w_out'][j])
            new_conv.append(s_conv)
        x = x + out
        x = x + 0.5 * _swiglu(_rmsnorm(x, p['ffn_norm'][i, 1]), p['ffn_w_gu'][i, 1], p['ffn_w_down'][i, 1])
    x = _rmsnorm(x, p['final_norm'])
    return x, jnp.stack(new_wkv), jnp.stack(new_shift), jnp.stack(new_conv)

def setup_inputs(seed: int = 0) -> dict:
    key = jax.random.key(seed)
    ks = iter(jax.random.split(key, 48))
    f32 = jnp.float32

    def nrm(shape, s):
        return jax.random.normal(next(ks), shape, f32) * s

    def unif(shape, lo, hi):
        return jax.random.uniform(next(ks), shape, f32, lo, hi)

    D, H, N, F = D_MODEL, N_HEADS, HEAD_DIM, D_FF
    return {
        'x_prompt': nrm((BATCH, SEQ, D), 1.0),
        'x_sample': nrm((DEC_BATCH, DEC_SEQ, D), 1.0),
        'state_wkv': nrm((N_RWKV, DEC_BATCH, H, N, N), 0.1),
        'state_shift': nrm((N_RWKV, DEC_BATCH, D), 1.0),
        'state_conv': nrm((N_CONV, DEC_BATCH, CONV_W - 1, D), 0.5),
        'meta': nrm((N_META, D), 1.0),
        'ffn_norm': 1.0 + nrm((DEPTH, 2, D), 0.01),
        'ffn_w_gu': nrm((DEPTH, 2, D, 2 * F), D ** -0.5),
        'ffn_w_down': nrm((DEPTH, 2, F, D), F ** -0.5),
        'mix_norm': 1.0 + nrm((DEPTH, D), 0.01),
        'final_norm': 1.0 + nrm((D,), 0.01),
        'rk_mu': unif((N_RWKV, 6, D), 0.0, 1.0),
        'rk_w_rkv': nrm((N_RWKV, 3, D, D), D ** -0.5),
        'rk_w0': unif((N_RWKV, D), -6.5, -1.5),
        'rk_w1': nrm((N_RWKV, D, D_DECAY_LORA), D ** -0.5),
        'rk_w2': nrm((N_RWKV, D_DECAY_LORA, D), 0.1 * D_DECAY_LORA ** -0.5),
        'rk_a0': nrm((N_RWKV, D), 0.1),
        'rk_a1': nrm((N_RWKV, D, D_AAA_LORA), D ** -0.5),
        'rk_a2': nrm((N_RWKV, D_AAA_LORA, D), 0.5 * D_AAA_LORA ** -0.5),
        'rk_g1': nrm((N_RWKV, D, D_GATE_LORA), D ** -0.5),
        'rk_g2': nrm((N_RWKV, D_GATE_LORA, D), D_GATE_LORA ** -0.5),
        'rk_k_k': 0.85 + nrm((N_RWKV, D), 0.05),
        'rk_k_a': 1.0 + nrm((N_RWKV, D), 0.05),
        'rk_r_k': -0.04 + nrm((N_RWKV, H, N), 0.05),
        'rk_ln_w': 1.0 + nrm((N_RWKV, D), 0.01),
        'rk_ln_b': nrm((N_RWKV, D), 0.01),
        'rk_w_o': nrm((N_RWKV, D, D), D ** -0.5),
        'sc_w_in': nrm((N_CONV, D, 3 * D), D ** -0.5),
        'sc_conv_w': nrm((N_CONV, CONV_W, D), CONV_W ** -0.5),
        'sc_w_out': nrm((N_CONV, D, D), D ** -0.5),
    }

def reference(x_prompt, x_sample, state_wkv, state_shift, state_conv, meta, ffn_norm, ffn_w_gu, ffn_w_down,
              mix_norm, final_norm, rk_mu, rk_w_rkv, rk_w0, rk_w1, rk_w2, rk_a0, rk_a1, rk_a2, rk_g1, rk_g2,
              rk_k_k, rk_k_a, rk_r_k, rk_ln_w, rk_ln_b, rk_w_o, sc_w_in, sc_conv_w, sc_w_out):
    p = {
        'ffn_norm': ffn_norm, 'ffn_w_gu': ffn_w_gu, 'ffn_w_down': ffn_w_down, 'mix_norm': mix_norm,
        'final_norm': final_norm, 'rk_mu': rk_mu, 'rk_w_rkv': rk_w_rkv, 'rk_w0': rk_w0, 'rk_w1': rk_w1,
        'rk_w2': rk_w2, 'rk_a0': rk_a0, 'rk_a1': rk_a1, 'rk_a2': rk_a2, 'rk_g1': rk_g1, 'rk_g2': rk_g2,
        'rk_k_k': rk_k_k, 'rk_k_a': rk_k_a, 'rk_r_k': rk_r_k, 'rk_ln_w': rk_ln_w, 'rk_ln_b': rk_ln_b,
        'rk_w_o': rk_w_o, 'sc_w_in': sc_w_in, 'sc_conv_w': sc_conv_w, 'sc_w_out': sc_w_out,
    }
    bp = x_prompt.shape[0]
    xp = jnp.concatenate([jnp.broadcast_to(meta.astype(x_prompt.dtype)[None], (bp, N_META, D_MODEL)), x_prompt], axis=1)
    wkv0 = jnp.zeros((N_RWKV, bp, N_HEADS, HEAD_DIM, HEAD_DIM), state_wkv.dtype)
    shift0 = jnp.zeros((N_RWKV, bp, D_MODEL), state_shift.dtype)
    conv0 = jnp.zeros((N_CONV, bp, CONV_W - 1, D_MODEL), state_conv.dtype)
    yp, wkv_p, shift_p, conv_p = _trunk(xp, wkv0, shift0, conv0, p)
    y_prompt = yp[:, N_META:]
    y_sample, wkv_s, shift_s, conv_s = _trunk(x_sample, state_wkv, state_shift, state_conv, p)
    return (y_prompt, y_sample, wkv_p, shift_p, conv_p, wkv_s, shift_s, conv_s)


_drawn_inputs = setup_inputs


def setup_inputs(seed=0):
    import zlib

    import numpy as np

    out = dict(_drawn_inputs(seed))
    spreads = {}
    factors = {'ffn_norm': 5.433,
     'mix_norm': 2.946,
     'final_norm': 5.824,
     'rk_w1': 8.0,
     'rk_w2': 8.0,
     'rk_ln_w': 8.0,
     'rk_ln_b': 8.0}
    for name, (base, spread) in spreads.items():
        noise = np.random.default_rng([zlib.crc32(name.encode()), seed]).standard_normal(out[name].shape)
        drawn = base * np.exp(spread * noise) if base else spread * noise
        out[name] = __import__('jax').numpy.asarray(drawn.astype(out[name].dtype))
    for name, factor in factors.items():
        out[name] = (out[name] * factor).astype(out[name].dtype)
    return out
```

```python
from contextlib import ExitStack

import concourse.bass as bass
from concourse import mybir

ALU = mybir.AluOpType
ACT = mybir.ActivationFunctionType
AX_X = mybir.AxisListType.X
F32 = mybir.dt.float32
F32R = mybir.dt.float32r

P = 128
D = 1024
KT = D // P
FF = 2816
FT = FF // P
META, SEQ, SEQS, STEPS = 16, 256, 8, 8
TP = META + SEQ
T = TP + SEQS * STEPS
HEADS, HD = 16, 64
PAIRS = HEADS // 2
C = 32
PAD = C - TP % C
TS = PAD + T
CHUNKS = TS // C
PCHUNKS = (PAD + TP) // C
SCH = CHUNKS - PCHUNKS
SPC = C // STEPS
LOADS = 5
EPS = 1e-6
GN_EPS = 64e-5
E_HALF = 0.6065306597126334
BIG, SMALL = 16, FT // 2
POOL_TILES = {BIG: 10, SMALL: 7}

V_NORM = 0
V_MIX = 4
V_FINAL = 6
V_MU = 7
V_W0, V_A0, V_KK, V_KA, V_RK, V_LNW, V_LNB = range(13, 20)
V_CONV = 20
V_OMKA = 23
NVEC = 24

K_ONES = 0
K_BLOCK = 128
K_EYE = 256
K_SEL = 320
K_SCAN = K_SEL + 16 * PAIRS
K_ZMASK = K_SCAN + TS
K_SEQCOL = K_ZMASK + CHUNKS * 2 * C
K_SEQROW = K_SEQCOL + SPC * C
K_SELT = K_SEQROW + SPC
NCONST = K_SELT + P * PAIRS


def build_program(nc, x_dram, vec_dram, const_dram, shift_dram, conv_dram, wkv_dram, gu_dram, down_dram,
                  mix_dram, wo_dram, scin_dram, scout_dram, blockeye_dram, y_out, wkvp_out, wkvs_out, shift_out,
                  convo_out, zt_dram, tt_dram):
    with ExitStack() as ctx:
        def sem(name):
            return ctx.enter_context(nc.semaphore(name))

        PS = ctx.enter_context(nc.psum_tensor("psum", [P, 8, 512], F32))

        top = [0]

        def at(name, shape, dt=F32, start=None):
            size = 4
            for n in shape[1:]:
                size *= n
            start = -(-top[0] // 32) * 32 if start is None else start
            t = nc.alloc_sbuf_tensor_at(name, shape, dt, offset=base + start)
            if start + size > top[0]:
                top[0] = start + size
            return t

        base = -(-nc.sbuf_base // 32) * 32
        x = at("x", [P, KT, T])
        raw = [at(f"w_raw{i}", [P, BIG * P]) for i in range(2)]
        whi = [at(f"w_hi{i}", [P, BIG * P], F32R) for i in range(2)]
        wlo = [at(f"w_lo{i}", [P, BIG * P], F32R) for i in range(2)]
        vec = at("vec", [P, KT, NVEC])
        con = at("con", [P, NCONST])
        cin = at("cin", [P, KT * 2 * SEQS])
        shin = at("shin", [P, KT * SEQS])
        stage = at("stage", [P, KT, 2 + 2 * SEQS])
        shst = at("shst", [P, KT, 1 + SEQS])
        e_start = -(-top[0] // 32) * 32
        tmp = [at(f"tmp{i}", [P, TS]) for i in range(8)]
        rstd = at("rstd", [P, T])
        acc = at("acc", [P, T])
        ms = at("ms", [P, T])
        x_start = -(-top[0] // 32) * 32
        xhi = at("x_hi", [P, KT, T], F32R)
        xlo = at("x_lo", [P, KT, T], F32R)
        a_start = -(-top[0] // 32) * 32
        hhi = at("h_hi", [P, FT, T], F32R)
        hlo = at("h_lo", [P, FT, T], F32R)
        f_end = top[0]
        vy = at("vy", [P, PAIRS, TS], start=a_start)
        xx = at("xx", [P, KT, T], start=a_start)
        gate = at("gate", [P, KT, T], start=a_start + 4 * PAIRS * TS)
        o1 = a_start + 4 * PAIRS * TS + 4 * KT * T
        bonus = at("bonus", [P, KT, T], start=o1)
        ar = at("ar", [P, PAIRS, 2, TS], start=o1 + 4 * KT * T)
        o2 = o1 + 4 * KT * T + 8 * PAIRS * TS
        bkh = at("bkh", [P, PAIRS, 2 * TS], start=o2)
        o3 = o2 + 8 * PAIRS * TS
        z = at("z", [P, PAIRS, CHUNKS, 2 * C], start=o3)
        hc = at("hc", [P, KT, T], start=o3)
        sw = at("sw", [P, PAIRS, TS], start=o3 + 4 * PAIRS * TS)
        o4 = o3 + 8 * PAIRS * TS
        thi = at("t_hi", [P, 2, T], F32R, start=o1)
        tlo = at("t_lo", [P, 2, T], F32R, start=o1 + 8 * T)
        ohi = at("o_hi", [P, KT, T], F32R, start=o1 + 4 * KT * T)
        olo = at("o_lo", [P, KT, T], F32R, start=o1 + 8 * KT * T)
        bkt = [at(f"bkt{i}", [P, CHUNKS, 2 * C], start=x_start + 4 * i * 2 * TS) for i in range(2)]
        gt = at("gt", [P, 2, C * C], start=x_start)
        wt = at("wt", [P, 2, C * C], start=x_start + 8 * C * C)
        outer = [at(f"outer{i}", [P, C * C // 4], start=x_start + 16 * C * C + i * C * C) for i in range(2)]
        q = x_start
        uv = [at(f"uv{i}", [P, PAIRS, HD], start=q + i * 2048) for i in range(2)]
        kv = [at(f"kv{i}", [P, PAIRS, HD], start=q + 4096 + i * 2048) for i in range(2)]
        st = [at(f"st{i}", [P, PAIRS, HD], start=q + 8192 + i * 2048) for i in range(2)]
        xs = at("xs", [P, PAIRS, HD], start=q + 12288)
        sd = at("sd", [P, PAIRS, HD], start=q + 14336)
        arm = at("arm", [P, SPC, PAIRS, C], start=q + 16384)
        assert q + 20480 <= a_start
        s0 = at("s0", [P, SPC, PAIRS, HD], start=e_start)
        ttc = [at(f"ttc{i}", [P, PAIRS, C], start=e_start + 8192 + i * 1024) for i in range(2)]
        dend = at("dend", [P, PAIRS, PCHUNKS + SEQS], start=o4)
        up = at("up", [P, KT, 2 + SEQ], start=o3)
        us = at("us", [P, KT, SEQS, 2 + STEPS], start=o3 + 4 * KT * (2 + SEQ))
        cv = at("cv", [P, KT, SEQ + SEQS * STEPS], start=a_start)
        assert base + top[0] <= nc.sbuf_usable_end, (base + top[0], nc.sbuf_usable_end)

        loaded = sem("loaded")
        raw_full = [sem(f"raw_full{i}") for i in range(2)]
        hi_ready = sem("hi_ready")
        lo_pool = sem("lo_pool")
        lo_dve = sem("lo_dve")
        slot_used = sem("slot_used")
        scaled = sem("scaled")
        gate_scaled = sem("gate_scaled")
        act_ready = sem("act_ready")
        h_ready = sem("h_ready")
        hhi_ready = sem("hhi_ready")
        hlo_ready = sem("hlo_ready")
        x_new = sem("x_new")
        sq_ready = sem("sq_ready")
        acc_done = sem("acc_done")
        xg_ready = sem("xg_ready")
        xhi_ready = sem("xhi_ready")
        xlo_ready = sem("xlo_ready")
        ss_done = sem("ss_done")
        root_ready = sem("root_ready")
        rstd_ready = sem("rstd_ready")
        stored = sem("stored")

        block = ctx.enter_context(nc.Block())

        stream = {}
        first = 0
        for name, dram, slots, tiles in (
                ("gu0", gu_dram[0], FT, BIG), ("down0", down_dram[0], 2 * KT, SMALL),
                ("mix", mix_dram, 16, BIG), ("wo", wo_dram, 4, BIG),
                ("gu1", gu_dram[1], FT, BIG), ("down1", down_dram[1], 2 * KT, SMALL),
                ("gu2", gu_dram[2], FT, BIG), ("down2", down_dram[2], 2 * KT, SMALL),
                ("scin", scin_dram, 12, BIG), ("scout", scout_dram, 4, BIG),
                ("gu3", gu_dram[3], FT, BIG), ("down3", down_dram[3], 2 * KT, SMALL)):
            stream[name] = (first, slots, tiles, dram)
            first += slots
        order = list(stream)
        MIXB = stream["mix"][0]

        def next_tiles(name):
            i = order.index(name) + 1
            return stream[order[i]][2] if i < len(order) else 0

        def used(n):
            return n + 3 - (16 if n >= MIXB + 16 else 0) if isinstance(n, int) else None

        def used_base(name):
            n = stream[name][0]
            return n + 2 - (16 if n > MIXB else 0)

        FFN = {0: dict(q=1, ver=0, c0=0, n=T, scaled=0), 1: dict(q=3, ver=7, c0=14, n=T - 14, scaled=FT),
               2: dict(q=4, ver=8, c0=14, n=T - 14, scaled=2 * FT),
               3: dict(q=6, ver=10, c0=16, n=T - 16, scaled=3 * FT + 12)}
        CONV = dict(q=5, ver=9, c0=14, n=T - 14, scaled=3 * FT)
        SPLITS = {0: (0, V_NORM + 0, 0), 2: (7, V_NORM + 1, 14), 3: (8, V_NORM + 2, 14),
                  4: (9, V_MIX + 1, 14), 5: (10, V_NORM + 3, 16)}
        RCOL = {1: 0, 2: 14, 3: 14, 4: 14, 5: 16, 6: 16}

        def passes(w_hi, w_lo, x_hi, x_lo):
            return ((w_hi, x_hi), (w_hi, x_lo), (w_lo, x_hi))

        def split_act(act, half, par, tiles, free_sem, free_value):
            act.wait_ge(raw_full[par], 16 * half + 16)
            act.wait_ge(free_sem, free_value)
            act.activation(whi[par][:, :tiles * P], raw[par][:, :tiles * P], ACT.Copy).then_inc(hi_ready, 1)

        def split_pool(pool, half, par, tiles):
            n = POOL_TILES[tiles] * P
            pool.wait_ge(hi_ready, 2 * half + par + 1)
            pool.tensor_tensor(wlo[par][:, :n], raw[par][:, :n], whi[par][:, :n].bitcast(F32),
                               ALU.subtract).then_inc(lo_pool, 1)

        def split_dve(dve, half, par, tiles):
            a, b = POOL_TILES[tiles] * P, tiles * P
            dve.wait_ge(hi_ready, 2 * half + par + 1)
            dve.tensor_tensor(wlo[par][:, a:b], raw[par][:, a:b], whi[par][:, a:b].bitcast(F32),
                              ALU.subtract).then_inc(lo_dve, 1)

        def pe_slot_wait(pe, n):
            pe.wait_ge(lo_pool, n + 3)
            pe.wait_ge(lo_dve, n + 3)

        def load_phase(sp, name, lo=0, hi=None):
            first, slots, tiles, dram = stream[name]
            with sp.Fori(lo // 2, (slots if hi is None else hi) // 2) as i:
                for par in range(2):
                    n = first + 2 * i + par
                    sp.wait_ge(lo_pool, n + 1)
                    sp.wait_ge(lo_dve, n + 1)
                    sp.dma_start(raw[par][:, :tiles * P], dram[2 * i + par]).then_inc(raw_full[par], 16)

        def res_dve(dve, q, m, par, alpha, ps, ready, split=True):
            if q:
                c = RCOL[q]
                dve.wait_ge(slot_used, ready)
                dve.scalar_tensor_tensor(out=x[:, m, c:], in0=ps[:, :T - c], scalar=alpha, in1=x[:, m, c:],
                                         op0=ALU.mult, op1=ALU.add).then_inc(x_new, 1)
            if q in SPLITS:
                ver, g, c = SPLITS[q]
                dve.wait_ge(x_new, 8 * q + m + 1 if q else 8)
                dve.tensor_scalar(tmp[4 + par][:, :T - c], x[:, m, c:], vec[:, m, g:g + 1], None,
                                  ALU.mult).then_inc(xg_ready, 1)

        def res_dve_after(dve, q, m, par, first):
            c = SPLITS[q][2] if q in SPLITS else RCOL[q]
            dve.wait_ge(sq_ready, 8 * q + m + 1)
            if first:
                dve.tensor_copy(acc[:, :T - c], tmp[6 + par][:, :T - c]).then_inc(acc_done, 1)
            else:
                dve.wait_ge(acc_done, 8 * q + m)
                dve.tensor_tensor(acc[:, :T - c], acc[:, :T - c], tmp[6 + par][:, :T - c],
                                  ALU.add).then_inc(acc_done, 1)
            if q in SPLITS:
                ver, g, c = SPLITS[q]
                dve.wait_ge(xhi_ready, 8 * ver + m + 1)
                dve.tensor_tensor(xlo[:, m, :T - c], tmp[4 + par][:, :T - c],
                                  xhi[:, m, :T - c].bitcast(F32), ALU.subtract).then_inc(xlo_ready, 1)

        def res_act(act, q, m, par, m_is_two_on=True):
            c = SPLITS[q][2] if q in SPLITS else RCOL[q]
            act.wait_ge(x_new, 8 * q + m + 1 if q else 8)
            if m_is_two_on:
                act.wait_ge(acc_done, 8 * q + m - 1)
            act.activation(tmp[6 + par][:, :T - c], x[:, m, c:], ACT.Square).then_inc(sq_ready, 1)
            if q in SPLITS:
                ver = SPLITS[q][0]
                act.wait_ge(xg_ready, 8 * ver + m + 1)
                act.activation(xhi[:, m, :T - c], tmp[4 + par][:, :T - c], ACT.Copy).then_inc(xhi_ready, 1)

        def norm_pe(pe, q, norm, n):
            pe.wait_ge(acc_done, 8 * q + 8)
            pe.matmul(PS[:, 6, :n], con[:, K_ONES:K_ONES + P], acc[:, :n], start=True, stop=True).then_inc(ss_done, 1)

        def norm_act(act, norm, n):
            act.wait_ge(ss_done, norm + 1)
            act.activation(ms[:, :n], PS[:, 6, :n], ACT.Sqrt, bias=EPS, scale=1.0 / D).then_inc(root_ready, 1)

        def norm_dve(dve, norm, n):
            dve.wait_ge(root_ready, norm + 1)
            dve.reciprocal(rstd[:, :n], ms[:, :n]).then_inc(rstd_ready, 1)
            dve.wait_ge(rstd_ready, norm + 1)

        def pe_pair(pe, par, banks, ver, n, out_sem, src=None, fresh=False):
            xh, xl = src or (xhi, xlo)
            for k in range(KT):
                if fresh:
                    pe.wait_ge(xlo_ready, 8 * ver + k + 1)
                for j in range(2):
                    for i, (w, v) in enumerate(passes(whi[par], wlo[par], xh, xl)):
                        last = pe.matmul(PS[:, banks[j], :n], w[:, (2 * k + j) * P:(2 * k + j + 1) * P], v[:, k, :n],
                                         start=(k == 0 and i == 0), stop=(k == KT - 1 and i == 2))
            last.then_inc(out_sem, 1)

        def ffn_pe(pe, f):
            d = FFN[f]
            gu, down, n = stream[f"gu{f}"][0], stream[f"down{f}"][0], d["n"]

            def gu_slot(i, par, fresh=False):
                pe_slot_wait(pe, gu + 2 * i + par)
                pe.wait_ge(scaled, d["scaled"] + 2 * i + par + 1)
                pe_pair(pe, par, (2 * par, 2 * par + 1), d["ver"], n, slot_used, fresh=fresh)

            if f in (1, 3):
                pe.wait_ge(x_new, 8 * (2 if f == 1 else 5) + 6)
            gu_slot(0, 0, fresh=True)
            norm_pe(pe, {0: 0, 1: 2, 2: 3, 3: 5}[f], 0, n)
            gu_slot(0, 1)
            with pe.Fori(1, FT // 2) as i:
                for par in range(2):
                    gu_slot(i, par)

            def down_tile(m, par, first=False):
                pe.wait_ge(x_new, 8 * d["q"] + m - 1)
                for half in range(2):
                    pe_slot_wait(pe, down + 2 * m + half)
                    for k in range(SMALL):
                        kk = half * SMALL + k
                        if first and kk in (0, FT - 2, FT - 1):
                            pe.wait_ge(hlo_ready, FT * f + max(kk + 1, FT - 2))
                        for i, (w, v) in enumerate(passes(whi[half], wlo[half], hhi, hlo)):
                            last = pe.matmul(PS[:, 4 + par, :n], w[:, k * P:(k + 1) * P], v[:, kk, :n],
                                             start=(kk == 0 and i == 0), stop=(kk == FT - 1 and i == 2))
                    last.then_inc(slot_used, 1)

            down_tile(0, 0, first=True)
            down_tile(1, 1)
            with pe.Fori(1, KT // 2) as i:
                for par in range(2):
                    down_tile(2 * i + par, par)

        def ffn_act(act, f):
            d = FFN[f]
            n, gub, dnb = d["n"], used_base(f"gu{f}"), used_base(f"down{f}")
            gu, down = stream[f"gu{f}"][0], stream[f"down{f}"][0]

            def gu_slot(i, par, tiles, first=False):
                split_act(act, gu // 2 + i + 1, par, tiles, slot_used, gub + 2 * i + par + 1)
                if first:
                    norm_act(act, {0: 0, 1: 2, 2: 3, 3: 5}[f], n)
                s = 2 * i + par
                act.wait_ge(gate_scaled, FT * f + s + 1)
                act.activation(tmp[1][:, :n], tmp[0][:, :n], ACT.Silu).then_inc(act_ready, 1)
                act.wait_ge(h_ready, FT * f + s + 1)
                act.activation(hhi[:, bass.ds(s, 1), :n], tmp[3][:, :n], ACT.Copy).then_inc(hhi_ready, 1)

            gu_slot(0, 0, BIG, first=True)
            gu_slot(0, 1, BIG)
            with act.Fori(1, FT // 2 - 1) as i:
                for par in range(2):
                    gu_slot(i, par, BIG)
            for par in range(2):
                gu_slot(FT // 2 - 1, par, SMALL)

            def down_tile(m, par, tiles, first=False, last=False):
                split_act(act, down // 2 + m + 1, 0, tiles, slot_used, dnb + 2 * m + 1) if tiles else None
                if last:
                    res_act(act, d["q"], m, par)
                if tiles:
                    split_act(act, down // 2 + m + 1, 1, tiles, slot_used, dnb + 2 * m + 2)
                if not last:
                    res_act(act, d["q"], m, par, not first)

            down_tile(0, 0, SMALL, first=True)
            down_tile(1, 1, SMALL, first=True)
            with act.Fori(1, KT // 2 - 1) as i:
                for par in range(2):
                    down_tile(2 * i + par, par, SMALL)
            down_tile(KT - 2, 0, SMALL)
            down_tile(KT - 1, 1, next_tiles(f"down{f}"), last=True)

        def ffn_dve(dve, f):
            d = FFN[f]
            n, gub, dnb = d["n"], used_base(f"gu{f}"), used_base(f"down{f}")
            gu, down = stream[f"gu{f}"][0], stream[f"down{f}"][0]

            def gu_slot(i, par, tiles, first=False):
                s = 2 * i + par
                if first:
                    norm_dve(dve, {0: 0, 1: 2, 2: 3, 3: 5}[f], n)
                dve.wait_ge(slot_used, gub + s + 1)
                dve.tensor_tensor(tmp[0][:, :n], PS[:, 2 * par, :n], rstd[:, :n], ALU.mult).then_inc(gate_scaled, 1)
                dve.tensor_tensor(tmp[2][:, :n], PS[:, 2 * par + 1, :n], rstd[:, :n], ALU.mult).then_inc(scaled, 1)
                split_dve(dve, gu // 2 + i + 1, par, tiles)
                dve.wait_ge(act_ready, FT * f + s + 1)
                dve.wait_ge(scaled, d["scaled"] + s + 3)
                dve.tensor_tensor(tmp[3][:, :n], tmp[1][:, :n], tmp[2][:, :n], ALU.mult).then_inc(h_ready, 1)
                dve.wait_ge(hhi_ready, FT * f + s + 1)
                dve.tensor_tensor(hlo[:, bass.ds(s, 1), :n], tmp[3][:, :n], hhi[:, bass.ds(s, 1), :n].bitcast(F32),
                                  ALU.subtract).then_inc(hlo_ready, 1)

            gu_slot(0, 0, BIG, first=True)
            gu_slot(0, 1, BIG)
            with dve.Fori(1, FT // 2 - 1) as i:
                for par in range(2):
                    gu_slot(i, par, BIG)
            for par in range(2):
                gu_slot(FT // 2 - 1, par, SMALL)

            def down_tile(m, par, tiles, first=False, last=False):
                if tiles:
                    split_dve(dve, down // 2 + m + 1, 0, tiles)
                res_dve(dve, d["q"], m, par, 0.5, PS[:, 4 + par, :], dnb + 2 * m + 2)
                if tiles and not last:
                    split_dve(dve, down // 2 + m + 1, 1, tiles)
                res_dve_after(dve, d["q"], m, par, first)
                if tiles and last:
                    split_dve(dve, down // 2 + m + 1, 1, tiles)

            down_tile(0, 0, SMALL, first=True)
            down_tile(1, 1, SMALL)
            with dve.Fori(1, KT // 2 - 1) as i:
                for par in range(2):
                    down_tile(2 * i + par, par, SMALL)
            down_tile(KT - 2, 0, SMALL)
            down_tile(KT - 1, 1, next_tiles(f"down{f}"), last=True)

        def split_phase_pool(pool, name):
            first, slots, tiles, _ = stream[name]
            with pool.Fori(0, slots // 2 - 1) as i:
                for par in range(2):
                    split_pool(pool, first // 2 + i + 1, par, tiles)
            if next_tiles(name):
                for par in range(2):
                    split_pool(pool, first // 2 + slots // 2, par, next_tiles(name))

        conv_u = sem("conv_u")
        o_ready = sem("o_ready")
        ohi_ready = sem("ohi_ready")
        olo_ready = sem("olo_ready")
        dve_line = sem("dve_line")
        line = [0]
        PR = 2 + SEQ

        def link(dve, ins):
            line[0] += 1
            ins.then_inc(dve_line, 1)
            dve.wait_ge(dve_line, line[0])

        def conv_pe(pe):
            d = CONV
            first = stream["scin"][0]
            for s in range(12):
                pe_slot_wait(pe, first + s)
                pe.wait_ge(scaled, d["scaled"] + s + 1)
                pe_pair(pe, s % 2, (2 * (s % 2), 2 * (s % 2) + 1), d["ver"], d["n"], slot_used, fresh=(s == 0))
                if s == 0:
                    norm_pe(pe, 4, 4, d["n"])
            project_pe(pe, "scout", 5, PR - 2 + SEQS * STEPS, KT)

        def project_pe(pe, name, q, n, olo_base):
            first = stream[name][0]
            for s in range(4):
                pe_slot_wait(pe, first + s)
                pe.wait_ge(x_new, 8 * q + 2 * s - 2)
                if s == 0:
                    pe.wait_ge(scaled, SCALED_BEFORE[name])
                    if name == "wo":
                        pe.wait_ge(mix_evac, MIX_GROUPS)
                banks = ((2 * s) % 4, (2 * s + 1) % 4)
                for k in range(KT):
                    if s == 0:
                        pe.wait_ge(olo_ready, olo_base + k + 1)
                    for j in range(2):
                        for i, (w, v) in enumerate(passes(whi[s % 2], wlo[s % 2], ohi, olo)):
                            last = pe.matmul(PS[:, banks[j], :n], w[:, (2 * k + j) * P:(2 * k + j + 1) * P], v[:, k, :n],
                                             start=(k == 0 and i == 0), stop=(k == KT - 1 and i == 2))
                last.then_inc(slot_used, 1)

        SCALED_BEFORE = {"wo": 2 + FT, "scout": 2 + 3 * FT + 12}

        def project_act(act, name, q):
            first, base_used, nxt = stream[name][0], used_base(name), next_tiles(name)
            for s in range(4):
                tiles = BIG if s < 2 else nxt
                if s < 3:
                    split_act(act, first // 2 + (s + 2) // 2, s % 2, tiles, slot_used, base_used + s + 1)
                for m in (2 * s, 2 * s + 1):
                    res_act(act, q, m, m % 2, m >= 2)
                if s == 3:
                    split_act(act, first // 2 + (s + 2) // 2, s % 2, tiles, slot_used, base_used + s + 1)

        def project_dve(dve, name, q):
            first, base_used, nxt = stream[name][0], used_base(name), next_tiles(name)
            for s in range(4):
                tiles = BIG if s < 2 else nxt
                for m in (2 * s, 2 * s + 1):
                    res_dve(dve, q, m, m % 2, 1.0, PS[:, m % 4, :], base_used + s + 1)
                    if s < 3 and m % 2 == 0:
                        split_dve(dve, first // 2 + (s + 2) // 2, s % 2, tiles)
                    res_dve_after(dve, q, m, m % 2, m == 0)
                if s == 3:
                    split_dve(dve, first // 2 + (s + 2) // 2, s % 2, tiles)

        def conv_act(act):
            d = CONV
            first, ub = stream["scin"][0], used_base("scin")
            for s in range(12):
                split_act(act, first // 2 + (s + 2) // 2, s % 2, BIG, slot_used, ub + s + 1)
                if s == 0:
                    norm_act(act, 4, d["n"])
                if s >= 8:
                    for m in (2 * (s - 8), 2 * (s - 8) + 1):
                        act.wait_ge(o_ready, KT + m + 1)
                        act.activation(ohi[:, m, :TN], tmp[2 + m % 2][:, :TN], ACT.Copy).then_inc(ohi_ready, 1)
            project_act(act, "scout", 5)

        TN = SEQ + SEQS * STEPS

        def conv_dve(dve):
            d = CONV
            first, ub, n = stream["scin"][0], used_base("scin"), d["n"]
            w = [lambda f, c=c: vec[:, f, V_CONV + c:V_CONV + c + 1] for c in range(3)]
            for s in range(12):
                if s == 0:
                    norm_dve(dve, 4, n)
                    dve.wait_ge(loaded, 16 * LOADS)
                    link(dve, dve.tensor_copy(us[:, :, :, 0:2], cin[:, :].rearrange("p (k b w) -> p k b w", k=KT, w=2)))
                dve.wait_ge(slot_used, ub + s + 1)
                if s < 8:
                    f = s
                    link(dve, dve.tensor_tensor(tmp[0][:, :n], PS[:, 2 * (s % 2), :n], rstd[:, :n], ALU.mult))
                    dve.tensor_tensor(tmp[2][:, :n], PS[:, 2 * (s % 2) + 1, :n], rstd[:, :n], ALU.mult).then_inc(scaled, 1)
                    dve.wait_ge(scaled, d["scaled"] + s + 3)
                    split_dve(dve, first // 2 + (s + 2) // 2, s % 2, BIG)
                    dve.tensor_tensor(up[:, f, :], tmp[0][:, :PR], tmp[2][:, :PR], ALU.mult)
                    link(dve, dve.tensor_tensor(
                        us[:, f, :, 2:], tmp[0][:, PR:n].rearrange("p (b t) -> p b t", t=STEPS),
                        tmp[2][:, PR:n].rearrange("p (b t) -> p b t", t=STEPS), ALU.mult))
                    cs = cv[:, f, SEQ:].rearrange("p (b t) -> p b t", t=STEPS)
                    dve.tensor_scalar(cv[:, f, :SEQ], up[:, f, 0:SEQ], w[0](f), None, ALU.mult)
                    link(dve, dve.tensor_scalar(cs, us[:, f, :, 0:STEPS], w[0](f), None, ALU.mult))
                    for c in (1, 2):
                        dve.scalar_tensor_tensor(out=cv[:, f, :SEQ], in0=up[:, f, c:c + SEQ], scalar=w[c](f),
                                                 in1=cv[:, f, :SEQ], op0=ALU.mult, op1=ALU.add)
                        link(dve, dve.scalar_tensor_tensor(out=cs, in0=us[:, f, :, c:c + STEPS], scalar=w[c](f),
                                                           in1=cs, op0=ALU.mult, op1=ALU.add))
                else:
                    ms_ = (2 * (s - 8), 2 * (s - 8) + 1)
                    link(dve, dve.tensor_tensor(tmp[0][:, :TN], PS[:, 2 * (s % 2), 2:n], rstd[:, 2:n], ALU.mult))
                    dve.tensor_tensor(tmp[1][:, :TN], PS[:, 2 * (s % 2) + 1, 2:n], rstd[:, 2:n], ALU.mult).then_inc(scaled, 1)
                    dve.wait_ge(scaled, d["scaled"] + s + 3)
                    for m in ms_:
                        dve.tensor_tensor(tmp[2 + m % 2][:, :TN], tmp[m % 2][:, :TN], cv[:, m, :],
                                          ALU.mult).then_inc(o_ready, 1)
                    split_dve(dve, first // 2 + (s + 2) // 2, s % 2, BIG)
                    for m in ms_:
                        dve.wait_ge(ohi_ready, KT + m + 1)
                        dve.tensor_tensor(olo[:, m, :TN], tmp[2 + m % 2][:, :TN], ohi[:, m, :TN].bitcast(F32),
                                          ALU.subtract).then_inc(olo_ready, 1)
                if s == 8:
                    link(dve, dve.tensor_copy(stage[:, :, 0:2], up[:, :, SEQ:]))
                    dve.tensor_copy(stage[:, :, 2:].rearrange("p k (b w) -> p k b w", w=2),
                                    us[:, :, :, STEPS:]).then_inc(conv_u, 1)
            project_dve(dve, "scout", 5)

        def final_pe(pe):
            norm_pe(pe, 6, 6, TN)

        def final_dve(dve):
            norm_dve(dve, 6, TN)
            for k in range(KT):
                dve.scalar_tensor_tensor(out=cv[:, k, :], in0=x[:, k, 16:], scalar=vec[:, k, V_FINAL:V_FINAL + 1],
                                         in1=rstd[:, :TN], op0=ALU.mult, op1=ALU.mult).then_inc(y_ready, 1)

        y_ready = sem("y_ready")

        MIX_GROUPS = 27
        LAST_GROUP = [0, 1, 2, 3, 5, 13, 14, 15, 16, 17, 18, 22, 23, 24, 25, 26]
        XK, XW, XA, XR, XG, XV = 1, 2, 3, 4, 5, 6
        MU = {XR: 0, XW: 1, XK: 2, XV: 3, XA: 4, XG: 5}
        RD = slice(PAD, TS)
        YC = PAD + 14
        NY = TS - YC

        mix_out = sem("mix_out")
        mix_evac = sem("mix_evac")
        lora_hi = sem("lora_hi")
        lora_in = sem("lora_in")
        lora_lo = sem("lora_lo")
        kk_ready = sem("kk_ready")
        kk_sq = sem("kk_sq")
        kk_ss = sem("kk_ss")
        kk_max = sem("kk_max")
        kk_root = sem("kk_root")
        kk_inv = sem("kk_inv")
        kk_spread = sem("kk_spread")
        logs_ready = sem("logs_ready")
        decays = sem("decays")
        ends_ready = sem("ends_ready")
        rk_ready = sem("rk_ready")
        rk_sum = sem("rk_sum")
        pair_ready = sem("pair_ready")
        z_done = sem("z_done")
        z_ready = sem("z_ready")
        z_stored = sem("z_stored")
        g_loaded = sem("g_loaded")
        inv_dve = sem("inv_dve")
        inv_pool = sem("inv_pool")
        inv_stored = sem("inv_stored")
        tt_loaded = [sem(f"tt_loaded{i}") for i in range(2)]
        shift_ready = sem("shift_ready")

        def mix_sp(sp):
            load_phase(sp, "mix")
            load_phase(sp, "wo")
            sp.wait_ge(shift_ready, 1)
            sp.dma_start(shift_out, shst[:].rearrange("p k n -> p (k n)")).then_inc(stored, 16)
            for p in range(PAIRS):
                sp.wait_ge(z_ready, 2 * p + 2)
                for hh in range(2):
                    rows = slice(HD * hh, HD * hh + C)
                    sp.dma_start(zt_dram[:, 2 * p + hh].rearrange("c s t -> s c t"),
                                 z[rows, p, :, 0:C]).then_inc(z_stored, 16)
            sp.wait_ge(z_stored, 16 * HEADS)
            sp.dma_start(gt[:, 0, :], zt_dram[0:8].rearrange("c h s t -> (c h) (s t)")).then_inc(g_loaded, 16)
            sp.dma_start(gt[:REST, 1, :], zt_dram[8:].rearrange("c h s t -> (c h) (s t)")).then_inc(g_loaded, 16)
            for i in range(2):
                sp.dma_start(wt[:, i, :], blockeye_dram).then_inc(g_loaded, 16)
            sp.wait_ge(inv_dve, 2 * (C - 1))
            sp.dma_start(tt_dram[0:8].rearrange("c h s t -> (c h) (s t)"), wt[:, 0, :]).then_inc(inv_stored, 16)
            sp.wait_ge(inv_pool, 2 * (C - 1))
            sp.dma_start(tt_dram[8:].rearrange("c h s t -> (c h) (s t)"), wt[:REST, 1, :]).then_inc(inv_stored, 16)
            sp.wait_ge(inv_stored, 32)

            def load_inverses(c):
                if c >= 2:
                    sp.wait_ge(u_done, 2 * (c - 1))
                for hh in range(2):
                    sp.dma_start(ttc[c % 2][HD * hh:HD * hh + C, :, :],
                                 tt_dram[c].rearrange("(p two) s t -> two s p t", two=2)[hh]).then_inc(tt_loaded[c % 2], 16)

            load_inverses(0)
            load_inverses(1)
            sp.wait_ge(pair_ready, PAIRS + 1)
            for q in range(SPC):
                sp.dma_start(s0[:, q].rearrange("p a b -> p (a b)"), wkv_dram[q]).then_inc(s0_loaded, 16)
            for c in range(2, CHUNKS):
                load_inverses(c)
                if c == PCHUNKS:
                    sp.wait_ge(st_ready, 2 * PCHUNKS + 1)
                    sp.dma_start(wkvp_out, st[PCHUNKS % 2][:].rearrange("p a b -> p (a b)")).then_inc(final_stored, 16)
            for n in range(SEQS):
                sp.wait_ge(seq_ready, n + 1)
                sp.dma_start(wkvs_out[n], s0[:, n % SPC].rearrange("p a b -> p (a b)")).then_inc(seq_stored, 16)
                if n < SPC:
                    sp.wait_ge(seq_stored, 16 * (n + 1))
                    sp.dma_start(s0[:, n].rearrange("p a b -> p (a b)"), wkv_dram[SPC + n]).then_inc(s0_loaded, 16)
            sp.wait_ge(seq_stored, 16 * SEQS)

        REST = (CHUNKS - 8) * HEADS
        MIX_STORES = 1
        s0_loaded = sem("s0_loaded")
        seq_ready = sem("seq_ready")
        seq_stored = sem("seq_stored")
        final_stored = sem("final_stored")
        x_done = sem("x_done")
        xs_dve = sem("xs_dve")
        xs_act = sem("xs_act")
        u_done = sem("u_done")
        uv_dve = sem("uv_dve")
        uv_act = sem("uv_act")
        s_done = sem("s_done")
        st_ready = sem("st_ready")
        sd_ready = sem("sd_ready")
        y_done = sem("y_done")
        y_evac = sem("y_evac")
        prep_done = sem("prep_done")
        prep_evac = sem("prep_evac")
        arm_ready = sem("arm_ready")
        kvm_ready = sem("kvm_ready")
        q_done = sem("q_done")

        def mix_pe(pe):
            norm_pe(pe, 1, 1, T)
            group = [0]

            def open_group():
                g = group[0]
                if g >= 2:
                    pe.wait_ge(mix_evac, g - 1)
                group[0] += 1
                return 2 * (g % 2)

            def project(slot, ver, fresh):
                pe_slot_wait(pe, MIXB + slot)
                b = open_group()
                pe_pair(pe, slot % 2, (b, b + 1), ver, T, mix_out, fresh=fresh)

            def lora_out(slot, first_tile, steps):
                for m in range(0, KT, 2):
                    b = open_group()
                    for j in range(2):
                        for k in range(steps):
                            tile = first_tile + KT * k + m + j
                            for i, (w, v) in enumerate(passes(whi[slot % 2], wlo[slot % 2], thi, tlo)):
                                last = pe.matmul(PS[:, b + j, :T], w[:, tile * P:(tile + 1) * P], v[:, k, :],
                                                 start=(k == 0 and i == 0), stop=(k == steps - 1 and i == 2))
                    last.then_inc(mix_out, 1)

            for s in range(4):
                project(s, XK, s == 0)
            pe_slot_wait(pe, MIXB + 4)
            for ver in (XW, XA):
                b = open_group()
                for k in range(KT):
                    pe.wait_ge(xlo_ready, 8 * ver + k + 1)
                    for i, (w, v) in enumerate(passes(whi[0], wlo[0], xhi, xlo)):
                        last = pe.matmul(PS[:, b, :T], w[:, 2 * k * P:(2 * k + 1) * P], v[:, k, :],
                                         start=(k == 0 and i == 0), stop=(k == KT - 1 and i == 2))
                last.then_inc(mix_out, 1)
            pe_slot_wait(pe, MIXB + 5)
            pe.wait_ge(lora_lo, 1)
            lora_out(5, 0, 1)
            lora_out(5, KT, 1)
            for s in range(4):
                project(6 + s, XR, s == 0)
            for p in range(PAIRS):
                pe.wait_ge(kk_sq, p + 1)
                last = pe.matmul(PS[0:HEADS, 6, :T], con[:, K_SEL + 16 * p:K_SEL + 16 * p + 16],
                                 tmp[6 + p % 2][:, RD], start=(p == 0), stop=(p == PAIRS - 1))
                last.then_inc(kk_ss, 1)
            project(10, XG, True)
            pe_slot_wait(pe, MIXB + 11)
            pe.wait_ge(lora_lo, 3)
            lora_out(11, 0, 2)
            for s in range(4):
                project(12 + s, XV, s == 0)
            pe.wait_ge(kk_inv, 1)

            def spread(p):
                if p >= 2:
                    pe.wait_ge(pair_ready, p - 1)
                pe.matmul(PS[:, 4 + p % 2, :T], con[0:HEADS, K_SELT + P * p:K_SELT + P * p + P], rstd[0:HEADS, :],
                          start=True, stop=True).then_inc(kk_spread, 1)

            spread(0)
            for p in range(PAIRS):
                if p + 1 < PAIRS:
                    spread(p + 1)
                pe.wait_ge(rk_ready, p + 1)
                pe.matmul(PS[:, 6 + p % 2, :T], con[:, K_BLOCK:K_BLOCK + P], tmp[0][:, RD],
                          start=True, stop=True).then_inc(rk_sum, 1)
                pe.wait_ge(pair_ready, p + 1)
                if p == 0:
                    pe.wait_ge(mix_evac, MIX_GROUPS)
                if p >= 2:
                    pe.wait_ge(z_ready, 2 * p - 2)
                for c in range(CHUNKS):
                    for hh in range(2):
                        rows = slice(HD * hh, HD * hh + HD)
                        last = pe.matmul(PS[rows, 2 * (p % 2) + c // 8, (c % 8) * 64:(c % 8) * 64 + 64],
                                         bkt[p % 2][rows, c, :], ar[rows, p, :, c * C:c * C + C],
                                         start=True, stop=True)
                last.then_inc(z_done, 1)
            chain_pe(pe)
            pe.wait_ge(y_evac, CHUNKS)
            for p in range(PAIRS):
                if p >= 2:
                    pe.wait_ge(yc_ready, p - 1)
                pe.matmul(PS[:, p % 2, :NY], con[:, K_BLOCK:K_BLOCK + P], vy[:, p, YC:], start=True, stop=True)\
                    .then_inc(mean_done, 1)
            for p in range(PAIRS):
                pe.wait_ge(yc_sq, p + 1)
                pe.matmul(PS[0:HEADS, 6, :NY], con[:, K_SEL + 16 * p:K_SEL + 16 * p + 16],
                          tmp[6 + p % 2][:, :NY], start=(p == 0), stop=(p == PAIRS - 1)).then_inc(var_done, 1)
            pe.wait_ge(gn_inv, 1)
            for p in range(PAIRS):
                if p >= 2:
                    pe.wait_ge(gn_used, p - 1)
                pe.matmul(PS[:, 4 + p % 2, :NY], con[0:HEADS, K_SELT + P * p:K_SELT + P * p + P], rstd[0:HEADS, :NY],
                          start=True, stop=True).then_inc(gn_spread, 1)
            project_pe(pe, "wo", 2, T - 14, 0)

        mean_done = sem("mean_done")
        yc_ready = sem("yc_ready")
        yc_sq = sem("yc_sq")
        var_done = sem("var_done")
        gn_root = sem("gn_root")
        gn_inv = sem("gn_inv")
        gn_spread = sem("gn_spread")
        gn_used = sem("gn_used")

        def chain_pe(pe):
            def prep(c, g):
                k = 2 * c + g
                if k >= 1:
                    pe.wait_ge(prep_evac, k)
                else:
                    pe.wait_ge(z_ready, 2 * PAIRS)
                for p in range(4 * g, 4 * g + 4):
                    for hh in range(2):
                        rows = slice(HD * hh, HD * hh + HD)
                        a = (p - 4 * g) * HD
                        pe.matmul(PS[HD * hh + C:HD * hh + 2 * C, 6, a:a + HD], vy[rows, p, c * C:c * C + C],
                                  con[rows, K_EYE:K_EYE + HD], start=True, stop=True)
                        last = pe.matmul(PS[rows, 6, 256 + a:256 + a + HD], bkh[rows, p, 2 * C * c:2 * C * c + 2 * C],
                                         con[rows, K_EYE:K_EYE + HD], start=True, stop=True)
                last.then_inc(prep_done, 1)

            def step_x(c, g):
                pe.wait_ge(prep_evac, 2 * c + g + 1)
                if c < PCHUNKS:
                    pe.wait_ge(st_ready, 2 * c + 1 if c == 0 else 2 * c + g)
                    if c == 0:
                        pe.wait_ge(z_ready, 2 * PAIRS)
                else:
                    pe.wait_ge(arm_ready, c - PCHUNKS + 1)
                    pe.wait_ge(s0_loaded, 16 * SPC * (c - PCHUNKS + 1))
                if c >= 1:
                    pe.wait_ge(xs_dve, 2 * (c - 1) + g + 1)
                    pe.wait_ge(xs_act, 2 * (c - 1) + g + 1)
                for p in range(4 * g, 4 * g + 4):
                    for hh in range(2):
                        rows = slice(HD * hh, HD * hh + HD)
                        out = PS[HD * hh:HD * hh + C, g, (p - 4 * g) * HD:(p - 4 * g + 1) * HD]
                        if c < PCHUNKS:
                            pe.matmul(out, ar[rows, p, 0, c * C:c * C + C], st[c % 2][rows, p, :], start=True, stop=False)
                        else:
                            for q in range(SPC):
                                pe.matmul(out, arm[rows, q, p, :], s0[rows, q, p, :], start=(q == 0), stop=False)
                        rows = slice(HD * hh + C, HD * hh + 2 * C)
                        last = pe.matmul(out, z[rows, p, c, 0:C], uv[c % 2][rows, p, :], start=False, stop=True)
                last.then_inc(x_done, 1)

            def step_u(c, g):
                pe.wait_ge(tt_loaded[c % 2], 32 * (c // 2 + 1))
                pe.wait_ge(xs_dve, 2 * c + g + 1)
                pe.wait_ge(xs_act, 2 * c + g + 1)
                if c >= 1:
                    pe.wait_ge(uv_dve, 2 * (c - 1) + g + 1)
                    pe.wait_ge(uv_act, 2 * (c - 1) + g + 1)
                for p in range(4 * g, 4 * g + 4):
                    for hh in range(2):
                        rows = slice(HD * hh, HD * hh + C)
                        last = pe.matmul(PS[rows, 2 + g, (p - 4 * g) * HD:(p - 4 * g + 1) * HD],
                                         ttc[c % 2][rows, p, :], xs[rows, p, :], start=True, stop=True)
                last.then_inc(u_done, 1)

            def step_s(c, g):
                pe.wait_ge(uv_dve, 2 * c + g + 1)
                pe.wait_ge(uv_act, 2 * c + g + 1)
                if c >= 1:
                    pe.wait_ge(st_ready, 2 * c + g)
                for p in range(4 * g, 4 * g + 4):
                    for hh in range(2):
                        rows = slice(HD * hh, HD * hh + HD)
                        last = pe.matmul(PS[rows, 4 + g, (p - 4 * g) * HD:(p - 4 * g + 1) * HD],
                                         kv[c % 2][rows, p, :], uv[c % 2][rows, p, :], start=True, stop=True)
                last.then_inc(s_done, 1)

            def step_y(c):
                if c >= 1:
                    pe.wait_ge(y_evac, c)
                pe.wait_ge(uv_dve, 2 * c + 2)
                pe.wait_ge(uv_act, 2 * c + 2)
                for p in range(PAIRS):
                    for hh in range(2):
                        rows = slice(HD * hh, HD * hh + HD)
                        last = pe.matmul(PS[rows, 7, p * C:p * C + C], uv[c % 2][rows, p, :], z[rows, p, c, C:],
                                         start=True, stop=False)
                        if c < PCHUNKS:
                            last = pe.matmul(PS[rows, 7, p * C:p * C + C], st[c % 2][rows, p, :],
                                             ar[rows, p, 1, c * C:c * C + C], start=False, stop=True)
                        else:
                            for q in range(SPC):
                                a = q * STEPS
                                last = pe.matmul(PS[rows, 7, p * C + a:p * C + a + STEPS], s0[rows, q, p, :],
                                                 ar[rows, p, 1, c * C + a:c * C + a + STEPS],
                                                 start=False, stop=(q == SPC - 1))
                last.then_inc(y_done, 1)

            def step_q(c):
                for q in range(SPC):
                    k = SPC * (c - PCHUNKS) + q
                    pe.wait_ge(kvm_ready, k + 1)
                    if k >= 2:
                        pe.wait_ge(seq_ready, k - 1)
                    for p in range(PAIRS):
                        for hh in range(2):
                            rows = slice(HD * hh, HD * hh + HD)
                            last = pe.matmul(PS[rows, 4 + q % 2, p * HD:p * HD + HD], st[q % 2][rows, p, :],
                                             uv[c % 2][rows, p, :], start=True, stop=True)
                    last.then_inc(q_done, 1)

            prep(0, 0)
            prep(0, 1)
            for c in range(CHUNKS):
                step_x(c, 0)
                step_x(c, 1)
                if c + 1 < CHUNKS:
                    prep(c + 1, 0)
                step_u(c, 0)
                step_u(c, 1)
                if c + 1 < CHUNKS:
                    prep(c + 1, 1)
                if c < PCHUNKS:
                    step_s(c, 0)
                    step_s(c, 1)
                step_y(c)
                if c >= PCHUNKS:
                    step_q(c)

        def mix_act(act):
            dn = used_base("down0")
            norm_act(act, 1, T)

            def split(k):
                split_act(act, (MIXB + k) // 2, k % 2, BIG, mix_out, LAST_GROUP[k - 2] + 1)

            def x_hi(ver):
                for k in range(KT):
                    act.wait_ge(xg_ready, 8 * ver + k + 1)
                    act.activation(xhi[:, k, :], tmp[4 + k % 2][:, :T], ACT.Copy).then_inc(xhi_ready, 1)

            def evac(g, outs):
                act.wait_ge(mix_out, g + 1)
                for j, (dst, func, bias) in enumerate(outs):
                    kw = {} if bias is None else {"bias": bias}
                    last = act.activation(dst, PS[:, 2 * (g % 2) + j, :T], func, **kw)
                last.then_inc(mix_evac, 1)

            x_hi(XK)
            for s in range(4):
                split(2 + s)
                evac(s, [(bkh[:, m, TS + PAD:], ACT.Copy, None) for m in (2 * s, 2 * s + 1)])
            x_hi(XW)
            act.wait_ge(mix_out, 5)
            act.activation(tmp[0][0:HD, :T], PS[0:HD, 0, :T], ACT.Tanh).then_inc(mix_evac, 1)
            x_hi(XA)
            act.wait_ge(mix_out, 6)
            act.activation(tmp[0][HD:, :T], PS[HD:, 2, :T], ACT.Copy).then_inc(mix_evac, 1)
            act.wait_ge(mix_evac, 6)
            act.activation(thi[:, 0, :], tmp[0][:, :T], ACT.Copy).then_inc(lora_hi, 1)
            x_hi(XR)
            split(6)
            for s in range(4):
                evac(6 + s, [(sw[:, m, PAD:], ACT.Sigmoid, vec[:, m, V_W0:V_W0 + 1]) for m in (2 * s, 2 * s + 1)])
            for s in range(4):
                evac(10 + s, [(bkh[:, m, PAD:TS], ACT.Sigmoid, vec[:, m, V_A0:V_A0 + 1]) for m in (2 * s, 2 * s + 1)])
            split(7)
            for s in range(4):
                split(8 + s)
                evac(14 + s, [(ar[:, m, 1, PAD:], ACT.Copy, None) for m in (2 * s, 2 * s + 1)])
                for p in (2 * s, 2 * s + 1):
                    act.wait_ge(kk_ready, p + 1)
                    if p >= 2:
                        act.wait_ge(kk_ss, p - 1)
                    act.activation(tmp[6 + p % 2][:, RD], ar[:, p, 0, PAD:], ACT.Square).then_inc(kk_sq, 1)
            x_hi(XG)
            act.wait_ge(mix_out, 19)
            act.activation(tmp[1][:, :T], PS[:, 0, :T], ACT.Sigmoid).then_inc(lora_in, 1)
            act.activation(tmp[2][:, :T], PS[:, 1, :T], ACT.Sigmoid).then_inc(mix_evac, 1)
            act.wait_ge(mix_evac, 19)
            act.wait_ge(lora_in, 1)
            act.activation(thi[:, 0, :], tmp[1][:, :T], ACT.Copy).then_inc(lora_hi, 1)
            act.activation(thi[:, 1, :], tmp[2][:, :T], ACT.Copy).then_inc(lora_hi, 1)
            split(12)
            x_hi(XV)
            for s in range(4):
                evac(19 + s, [(gate[:, m, :], ACT.Copy, None) for m in (2 * s, 2 * s + 1)])
            split(13)
            for s in range(4):
                split(14 + s)
                evac(23 + s, [(vy[:, m, PAD:], ACT.Copy, None) for m in (2 * s, 2 * s + 1)])
            act.wait_ge(kk_max, 1)
            act.activation(ms[0:HEADS, :], ms[0:HEADS, :], ACT.Sqrt).then_inc(kk_root, 1)
            for p in range(PAIRS):
                act.wait_ge(logs_ready, p + 1)
                act.activation(tmp[6][:, RD], tmp[3][:, RD], ACT.Exp).then_inc(decays, 1)
                act.activation(tmp[7][:, RD], tmp[3][:, RD], ACT.Exp, scale=-1.0).then_inc(decays, 1)
                act.activation(tmp[4][:, RD], tmp[4][:, RD], ACT.Exp).then_inc(decays, 1)
                act.activation(tmp[5][:, RD], tmp[5][:, RD], ACT.Exp).then_inc(decays, 1)
                act.wait_ge(decays, 4 * p + 1)
                act.activation(dend[:, p, 0:PCHUNKS], tmp[6][:, C - 1:PCHUNKS * C:C], ACT.Copy).then_inc(ends_ready, 1)
                act.activation(dend[:, p, PCHUNKS:], tmp[6][:, PCHUNKS * C + STEPS - 1::STEPS], ACT.Copy).then_inc(ends_ready, 1)
            chain_act(act)
            for p in range(PAIRS):
                act.wait_ge(yc_ready, p + 1)
                if p >= 2:
                    act.wait_ge(var_done, p - 1)
                act.activation(tmp[6 + p % 2][:, :NY], vy[:, p, YC:], ACT.Square).then_inc(yc_sq, 1)
            act.wait_ge(var_done, PAIRS)
            act.activation(ms[0:HEADS, :NY], PS[0:HEADS, 6, :NY], ACT.Sqrt, bias=GN_EPS, scale=1.0 / HD)\
                .then_inc(gn_root, 1)
            for p in range(PAIRS):
                act.wait_ge(o_ready, p + 1)
                act.activation(ohi[:, p, :NY], tmp[4 + p % 2][:, :NY], ACT.Copy).then_inc(ohi_ready, 1)
            project_act(act, "wo", 2)

        def chain_act(act):
            def prep(c, g):
                act.wait_ge(prep_done, 2 * c + g + 1)
                if c >= 2:
                    act.wait_ge(y_done, c - 1)
                ps = slice(4 * g, 4 * g + 4)
                act.activation(kv[c % 2][:, ps, :], PS[:, 6, 256:512].rearrange("p (a b) -> p a b", b=HD), ACT.Copy)
                for hh in range(2):
                    rows = slice(HD * hh + C, HD * hh + 2 * C)
                    last = act.activation(uv[c % 2][rows, ps, :],
                                          PS[rows, 6, 0:256].rearrange("p (a b) -> p a b", b=HD), ACT.Copy)
                last.then_inc(prep_evac, 1)

            def odd(done, dst, bank, out_sem, c, g):
                act.wait_ge(done, 2 * c + g + 1)
                act.activation(dst[HD:HD + C, 4 * g:4 * g + 4, :],
                               PS[HD:HD + C, bank + g, 0:256].rearrange("p (a b) -> p a b", b=HD),
                               ACT.Copy).then_inc(out_sem, 1)

            act.wait_ge(inv_stored, 32)
            prep(0, 0)
            prep(0, 1)
            for c in range(CHUNKS):
                for g in range(2):
                    if c >= 1:
                        act.wait_ge(u_done, 2 * (c - 1) + g + 1)
                    odd(x_done, xs, 0, xs_act, c, g)
                if c + 1 < CHUNKS:
                    prep(c + 1, 0)
                for g in range(2):
                    odd(u_done, uv[c % 2], 2, uv_act, c, g)
                if c + 1 < CHUNKS:
                    prep(c + 1, 1)
                act.wait_ge(y_done, c + 1)
                act.activation(vy[:, :, c * C:c * C + C], PS[:, 7, 0:256].rearrange("p (a b) -> p a b", b=C),
                               ACT.Copy).then_inc(y_evac, 1)

        def mix_pool(pool):
            first = MIXB // 2
            for k in range(2, 18):
                split_pool(pool, (MIXB + k) // 2, k % 2, BIG)
            pool.wait_ge(g_loaded, 64)
            inverse(pool, 1, REST, inv_pool)
            pool.wait_ge(inv_stored, 32)
            for c in range(PCHUNKS):
                for g in range(2):
                    pool.wait_ge(st_ready, 1 if c == 0 else 2 * c + g)
                    if c >= 1:
                        pool.wait_ge(st_ready, 2 * c + g)
                    pool.tensor_tensor(sd[:, 4 * g:4 * g + 4, :], st[c % 2][:, 4 * g:4 * g + 4, :],
                                       dend[:, 4 * g:4 * g + 4, c:c + 1].to_broadcast([P, 4, HD]),
                                       ALU.mult).then_inc(sd_ready, 1)

        def inverse(eng, slot, rows, out_sem):
            g = gt[:rows, slot, :].rearrange("p (s t) -> p s t", t=C)
            w = wt[:rows, slot, :].rearrange("p (s t) -> p s t", t=C)
            done = 0
            for r in range(C - 1, 0, -1):
                n = C - r
                o = outer[slot][:rows, :r * n].rearrange("p (s t) -> p s t", t=n)
                if done:
                    eng.wait_ge(out_sem, done)
                eng.tensor_tensor(o, g[:, 0:r, r:r + 1].to_broadcast([rows, r, n]),
                                  w[:, r:r + 1, r:].to_broadcast([rows, r, n]), ALU.mult).then_inc(out_sem, 1)
                eng.wait_ge(out_sem, done + 1)
                eng.tensor_tensor(w[:, 0:r, r:], w[:, 0:r, r:], o, ALU.add).then_inc(out_sem, 1)
                done += 2

        def mix_dve(dve):
            norm_dve(dve, 1, T)
            seqs = slice(TP, T, STEPS)

            def split(k):
                split_dve(dve, (MIXB + k) // 2, k % 2, BIG)

            def mixed(ver, k):
                dve.wait_ge(xlo_ready, 8 * ver + k - 1)
                dve.scalar_tensor_tensor(out=tmp[4 + k % 2][:, :T], in0=xx[:, k, :],
                                         scalar=vec[:, k, V_MU + MU[ver]:V_MU + MU[ver] + 1], in1=hc[:, k, :],
                                         op0=ALU.mult, op1=ALU.add).then_inc(xg_ready, 1)

            def low(ver, k):
                dve.wait_ge(xhi_ready, 8 * ver + k + 1)
                dve.tensor_tensor(xlo[:, k, :], tmp[4 + k % 2][:, :T], xhi[:, k, :].bitcast(F32),
                                  ALU.subtract).then_inc(xlo_ready, 1)

            def shifted(k):
                link(dve, dve.scalar_tensor_tensor(out=hc[:, k, :], in0=x[:, k, :], scalar=vec[:, k, V_MIX:V_MIX + 1],
                                                   in1=rstd[:], op0=ALU.mult, op1=ALU.mult))
                link(dve, dve.tensor_tensor(xx[:, k, 1:], hc[:, k, :T - 1], hc[:, k, 1:], ALU.subtract))
                dve.tensor_scalar(xx[:, k, 0:1], hc[:, k, 0:1], -1.0, None, ALU.mult)
                link(dve, dve.tensor_tensor(xx[:, k, seqs], shin[:, SEQS * k:SEQS * k + SEQS], hc[:, k, seqs],
                                            ALU.subtract))

            def mix_version(ver, freed):
                dve.wait_ge(mix_out, freed)
                mixed(ver, 0)
                for k in range(KT):
                    if k + 1 < KT:
                        mixed(ver, k + 1)
                    low(ver, k)

            for k in range(KT):
                shifted(k)
                mixed(XK, k)
                if k:
                    low(XK, k - 1)
            low(XK, KT - 1)
            dve.tensor_copy(shst[:, :, 0:1], hc[:, :, TP - 1:TP])
            dve.tensor_copy(shst[:, :, 1:], hc[:, :, TP + STEPS - 1::STEPS]).then_inc(shift_ready, 1)
            for k in range(2, 6):
                split(k)
            mix_version(XW, 4)
            mix_version(XA, 5)
            dve.wait_ge(lora_hi, 1)
            dve.tensor_tensor(tlo[:, 0, :], tmp[0][:, :T], thi[:, 0, :].bitcast(F32), ALU.subtract).then_inc(lora_lo, 1)
            mix_version(XR, 6)
            split(6)
            dve.memset(ar[:, :, :, 0:PAD], 0.0)
            dve.wait_ge(mix_evac, 4)
            for p in range(PAIRS):
                dve.tensor_scalar(ar[:, p, 0, PAD:], bkh[:, p, TS + PAD:], vec[:, p, V_KK:V_KK + 1], None,
                                  ALU.mult).then_inc(kk_ready, 1)
            for k in range(7, 12):
                split(k)
            mix_version(XG, 18)
            for k in range(2):
                dve.wait_ge(lora_hi, 2 + k)
                dve.tensor_tensor(tlo[:, k, :], tmp[1 + k][:, :T], thi[:, k, :].bitcast(F32),
                                  ALU.subtract).then_inc(lora_lo, 1)
            split(12)
            mix_version(XV, 19)
            dve.wait_ge(kk_ss, PAIRS)
            dve.tensor_scalar(ms[0:HEADS, :], PS[0:HEADS, 6, :T], 1e-24, None, ALU.max).then_inc(kk_max, 1)
            for k in range(13, 18):
                split(k)
            dve.wait_ge(kk_root, 1)
            dve.reciprocal(rstd[0:HEADS, :], ms[0:HEADS, :]).then_inc(kk_inv, 1)
            for t in tmp:
                dve.memset(t[:, 0:PAD], 0.0)
            for t in bkt:
                dve.memset(t[:, 0, :], 0.0)
            link(dve, dve.tensor_scalar(vec[:, :, V_OMKA:V_OMKA + 1], vec[:, :, V_KA:V_KA + 1], -1.0, 1.0,
                                        ALU.mult, ALU.add))
            dve.wait_ge(mix_evac, MIX_GROUPS)
            dve.memset(vy[:, :, 0:PAD], 0.0)
            for p in range(PAIRS):
                scaled_pair(dve, p)
            dve.memset(acc[:, 2:3], 0.0).then_inc(pair_ready, 1)
            dve.wait_ge(g_loaded, 64)
            inverse(dve, 0, P, inv_dve)
            for p in range(PAIRS):
                dve.scalar_tensor_tensor(out=bonus[:, p, :], in0=bonus[:, p, :], scalar=vec[:, p, V_LNB:V_LNB + 1],
                                         in1=gate[:, p, :], op0=ALU.add, op1=ALU.mult)
                link(dve, dve.tensor_scalar(gate[:, p, :], gate[:, p, :], vec[:, p, V_LNW:V_LNW + 1], None, ALU.mult))
            chain_dve(dve)
            for p in range(PAIRS):
                dve.wait_ge(mean_done, p + 1)
                dve.scalar_tensor_tensor(out=vy[:, p, YC:], in0=PS[:, p % 2, :NY], scalar=-1.0 / HD, in1=vy[:, p, YC:],
                                         op0=ALU.mult, op1=ALU.add).then_inc(yc_ready, 1)
            dve.wait_ge(gn_root, 1)
            dve.reciprocal(rstd[0:HEADS, :NY], ms[0:HEADS, :NY]).then_inc(gn_inv, 1)
            dve.wait_ge(seq_stored, 16 * SEQS)
            for p in range(PAIRS):
                t = tmp[4 + p % 2][:, :NY]
                dve.wait_ge(gn_spread, p + 1)
                dve.wait_ge(yc_ready, PAIRS)
                link(dve, dve.tensor_tensor(t, PS[:, 4 + p % 2, :NY], vy[:, p, YC:], ALU.mult))
                dve.memset(tmp[0][:, 0:1], 0.0).then_inc(gn_used, 1)
                link(dve, dve.tensor_tensor(t, t, gate[:, p, 14:], ALU.mult))
                dve.tensor_tensor(t, t, bonus[:, p, 14:], ALU.add).then_inc(o_ready, 1)
                dve.wait_ge(ohi_ready, p + 1)
                dve.tensor_tensor(olo[:, p, :NY], t, ohi[:, p, :NY].bitcast(F32), ALU.subtract).then_inc(olo_ready, 1)
            project_dve(dve, "wo", 2)

        def scaled_pair(dve, p):
            aa, k, a, r = bkh[:, p, PAD:TS], bkh[:, p, TS + PAD:], ar[:, p, 0, PAD:], ar[:, p, 1, PAD:]
            t = [u[:, RD] for u in tmp]
            dve.wait_ge(kk_spread, p + 1)
            link(dve, dve.tensor_tensor(a, PS[:, 4 + p % 2, :T], a, ALU.mult))
            link(dve, dve.tensor_scalar(t[0], aa, vec[:, p, V_KA:V_KA + 1], vec[:, p, V_OMKA:V_OMKA + 1],
                                        ALU.mult, ALU.add))
            link(dve, dve.tensor_tensor(t[1], k, t[0], ALU.mult))
            link(dve, dve.scalar_tensor_tensor(out=t[2], in0=a, scalar=-1.0, in1=aa, op0=ALU.mult, op1=ALU.mult))
            link(dve, dve.tensor_scalar(sw[:, p, PAD:], sw[:, p, PAD:], -E_HALF, None, ALU.mult))
            link(dve, dve.tensor_tensor_scan(t[3], con[:, K_SCAN + PAD:K_SCAN + TS], sw[:, p, PAD:], 0.0,
                                             ALU.mult, ALU.add))
            dve.tensor_tensor(t[4], t[3], sw[:, p, PAD:], ALU.subtract)
            for a0, n, size in ((PAD, 1, C - PAD), (C, PCHUNKS - 1, C), (PCHUNKS * C, SEQS, STEPS)):
                src = tmp[3][:, a0:a0 + n * size].rearrange("p (n s) -> p n s", s=size)
                dst = tmp[5][:, a0:a0 + n * size].rearrange("p (n s) -> p n s", s=size)
                last = dve.tensor_tensor(dst, src[:, :, size - 1:size].to_broadcast([P, n, size]), src, ALU.subtract)
            last.then_inc(logs_ready, 1)
            link(dve, dve.scalar_tensor_tensor(out=t[0], in0=r, scalar=vec[:, p, V_RK:V_RK + 1], in1=t[1],
                                               op0=ALU.mult, op1=ALU.mult))
            dve.memset(acc[:, 0:1], 0.0).then_inc(rk_ready, 1)
            dve.wait_ge(decays, 4 * p + 4)
            dve.tensor_tensor(a, a, t[4], ALU.mult)
            dve.tensor_tensor(r, r, t[6], ALU.mult)
            if p >= 2:
                dve.wait_ge(z_done, p - 1)
            chunks = [u[:].rearrange("p (c t) -> p c t", t=C) for u in tmp]
            hat = bkh[:, p, :].rearrange("p (c t) -> p c t", t=2 * C)
            dve.tensor_tensor(bkt[p % 2][:, :, 0:C], chunks[2], chunks[7], ALU.mult)
            dve.tensor_tensor(bkt[p % 2][:, :, C:], chunks[1], chunks[7], ALU.mult)
            dve.tensor_tensor(hat[:, :, 0:C], chunks[2], chunks[5], ALU.mult)
            dve.tensor_tensor(hat[:, :, C:], chunks[1], chunks[5], ALU.mult)
            dve.wait_ge(rk_sum, p + 1)
            dve.wait_ge(ends_ready, 2 * p + 2)
            link(dve, dve.tensor_tensor(bonus[:, p, :], PS[:, 6 + p % 2, :T], vy[:, p, PAD:], ALU.mult))
            dve.memset(acc[:, 1:2], 0.0).then_inc(pair_ready, 1)
            dve.wait_ge(z_done, p + 1)
            for i, (c0, c1) in enumerate(((0, 8), (8, CHUNKS))):
                n = (c1 - c0) * 2 * C
                dve.tensor_tensor(z[:, p, c0:c1, :].rearrange("p c t -> p (c t)"), PS[:, 2 * (p % 2) + i, :n],
                                  con[:, K_ZMASK + c0 * 2 * C:K_ZMASK + c1 * 2 * C], ALU.mult).then_inc(z_ready, 1)

        def chain_dve(dve):
            def even(done, dst, bank, out_sem, c, g):
                dve.wait_ge(done, 2 * c + g + 1)
                dve.tensor_copy(dst[0:C, 4 * g:4 * g + 4, :],
                                PS[0:C, bank + g, 0:256].rearrange("p (a b) -> p a b", b=HD)).then_inc(out_sem, 1)

            dve.wait_ge(inv_stored, 32)
            dve.memset(st[0][:], 0.0).then_inc(st_ready, 1)
            for c in range(CHUNKS):
                if c >= PCHUNKS:
                    n = c - PCHUNKS
                    seq = con[:, K_SEQCOL:K_SEQCOL + SPC * C].rearrange("p (q t) -> p q t", t=C)
                    if n:
                        dve.wait_ge(x_done, 2 * c)
                    for q in range(SPC):
                        last = dve.tensor_tensor(arm[:, q], ar[:, :, 0, c * C:c * C + C],
                                                 seq[:, q:q + 1, :].to_broadcast([P, PAIRS, C]), ALU.mult)
                    last.then_inc(arm_ready, 1)
                for g in range(2):
                    if c >= 1:
                        dve.wait_ge(u_done, 2 * (c - 1) + g + 1)
                    even(x_done, xs, 0, xs_dve, c, g)
                for g in range(2):
                    even(u_done, uv[c % 2], 2, uv_dve, c, g)
                if c < PCHUNKS:
                    for g in range(2):
                        dve.wait_ge(s_done, 2 * c + g + 1)
                        dve.wait_ge(sd_ready, 2 * c + g + 1)
                        if c >= 1:
                            dve.wait_ge(y_done, c)
                        dve.tensor_tensor(st[(c + 1) % 2][:, 4 * g:4 * g + 4, :], sd[:, 4 * g:4 * g + 4, :],
                                          PS[:, 4 + g, 0:256].rearrange("p (a b) -> p a b", b=HD),
                                          ALU.add).then_inc(st_ready, 1)
                    continue
                if c == PCHUNKS:
                    dve.wait_ge(final_stored, 16)
                    dve.wait_ge(y_done, c)
                for q in range(SPC):
                    k = SPC * (c - PCHUNKS) + q
                    if k >= 2:
                        dve.wait_ge(q_done, k - 1)
                    dve.tensor_scalar(st[q % 2][:], kv[c % 2][:], con[:, K_SEQROW + q:K_SEQROW + q + 1], None,
                                      ALU.mult).then_inc(kvm_ready, 1)
                    if q >= 1:
                        new_state(dve, c, q - 1)
                new_state(dve, c, SPC - 1)

        def new_state(dve, c, q):
            k = SPC * (c - PCHUNKS) + q
            dve.wait_ge(y_done, c + 1)
            link(dve, dve.tensor_tensor(s0[:, q], s0[:, q],
                                        dend[:, :, PCHUNKS + k:PCHUNKS + k + 1].to_broadcast([P, PAIRS, HD]), ALU.mult))
            dve.wait_ge(q_done, k + 1)
            dve.tensor_tensor(s0[:, q], s0[:, q], PS[:, 4 + q % 2, :].rearrange("p (a b) -> p a b", b=HD),
                              ALU.add).then_inc(seq_ready, 1)

        @block.sync
        def _(sp):
            sp.dma_start(x[:], x_dram).then_inc(loaded, 16)
            sp.dma_start(vec[:], vec_dram).then_inc(loaded, 16)
            sp.dma_start(con[:], const_dram).then_inc(loaded, 16)
            sp.dma_start(cin[:], conv_dram).then_inc(loaded, 16)
            sp.dma_start(shin[:], shift_dram).then_inc(loaded, 16)
            load_phase(sp, "gu0")
            load_phase(sp, "down0")
            mix_sp(sp)
            for name in order[4:]:
                load_phase(sp, name)
            sp.wait_ge(conv_u, 1)
            sp.dma_start(convo_out, stage[:]).then_inc(stored, 16)
            for k in range(KT):
                sp.wait_ge(y_ready, k + 1)
                sp.dma_start(y_out[k], cv[:, k, :]).then_inc(stored, 16)
            sp.wait_ge(stored, 16 * (KT + 1 + MIX_STORES))

        @block.gpsimd
        def _(pool):
            for par in range(2):
                split_pool(pool, 0, par, BIG)
            for name in order:
                if name == "mix":
                    mix_pool(pool)
                else:
                    split_phase_pool(pool, name)

        @block.scalar
        def _(act):
            for par in range(2):
                split_act(act, 0, par, BIG, slot_used, 2)
            for m in range(KT):
                res_act(act, 0, m, m % 2, m >= 2)
            ffn_act(act, 0)
            mix_act(act)
            ffn_act(act, 1)
            ffn_act(act, 2)
            conv_act(act)
            ffn_act(act, 3)
            norm_act(act, 6, TN)

        @block.vector
        def _(dve):
            dve.memset(tmp[7][:, 0:1], 0.0).then_inc(slot_used, 2)
            dve.memset(tmp[7][:, 1:2], 0.0).then_inc(scaled, 2)
            dve.memset(tmp[7][:, 2:3], 0.0).then_inc(lo_pool, 2)
            dve.memset(tmp[7][:, 3:4], 0.0).then_inc(lo_dve, 2)
            dve.wait_ge(loaded, 16 * LOADS)
            dve.memset(tmp[7][:, 4:5], 0.0).then_inc(x_new, 8)
            dve.wait_ge(x_new, 8)
            for par in range(2):
                split_dve(dve, 0, par, BIG)
            for m in range(KT):
                res_dve(dve, 0, m, m % 2, None, None, None)
                res_dve_after(dve, 0, m, m % 2, m == 0)
            ffn_dve(dve, 0)
            mix_dve(dve)
            ffn_dve(dve, 1)
            ffn_dve(dve, 2)
            conv_dve(dve)
            ffn_dve(dve, 3)
            final_dve(dve)

        @block.tensor
        def _(pe):
            pe.wait_ge(loaded, 16 * LOADS)
            ffn_pe(pe, 0)
            mix_pe(pe)
            ffn_pe(pe, 1)
            ffn_pe(pe, 2)
            conv_pe(pe)
            ffn_pe(pe, 3)
            final_pe(pe)


def _slots(w, pairs):
    import numpy as np
    w = np.asarray(w).reshape(KT, P, -1, P)
    return np.stack([np.stack([w[:, :, m] for m in pair], 2).transpose(1, 0, 2, 3).reshape(P, -1) for pair in pairs])


def _constants():
    import numpy as np
    c = np.zeros((P, NCONST), np.float32)
    head = np.arange(P) // HD
    c[:, K_ONES:K_ONES + P] = 1.0
    c[:, K_BLOCK:K_BLOCK + P] = head[:, None] == head[None, :]
    c[:, K_EYE:K_EYE + HD] = (np.arange(P) % HD)[:, None] == np.arange(HD)[None, :]
    for p in range(PAIRS):
        c[:, K_SEL + 16 * p:K_SEL + 16 * p + 16] = (2 * p + head)[:, None] == np.arange(16)[None, :]
        c[:HEADS, K_SELT + P * p:K_SELT + P * p + P] = np.arange(HEADS)[:, None] == (2 * p + head)[None, :]
    col = np.arange(TS)
    starts = (col % C == 0) | ((col >= PCHUNKS * C) & (col % STEPS == 0))
    c[:, K_SCAN:K_SCAN + TS] = ~starts
    s, t = (np.arange(P) % C)[:, None], np.arange(C)[None, :]
    z = c[:, K_ZMASK:K_ZMASK + CHUNKS * 2 * C].reshape(P, CHUNKS, 2, C)
    for n in range(CHUNKS):
        same = (s // STEPS == t // STEPS) | (n < PCHUNKS)
        z[:, n, 0] = (s < t) & same
        z[:, n, 1] = (s <= t) & same
    c[:, K_SEQCOL:K_SEQCOL + SPC * C] = (np.arange(C)[None, :] // STEPS == np.arange(SPC)[:, None]).reshape(1, -1)
    c[:, K_SEQROW:K_SEQROW + SPC] = s // STEPS == np.arange(SPC)[None, :]
    return c


_INPUTS = ("x", "vec", "const", "shift", "conv", "wkv", "gu", "down", "mix", "wo", "scin", "scout", "eye")
_OUTPUTS = {"y": (KT, P, SEQ + SEQS * STEPS), "wkvp": (P, PAIRS * HD), "wkvs": (SEQS, P, PAIRS * HD),
            "shifto": (P, KT * (1 + SEQS)), "convo": (P, KT * (2 + 2 * SEQS))}


def kernel(**a):
    import numpy as np
    import concourse.bacc as bacc
    from concourse.bass_utils import run_bass_kernel_spmd

    a = {k: np.asarray(v) for k, v in a.items()}
    f32 = np.float32

    def tiles(v):
        return v.reshape(-1, KT, P).transpose(2, 1, 0)

    tokens = np.concatenate([a["meta"], a["x_prompt"][0], a["x_sample"].reshape(SEQS * STEPS, D)], 0)
    vectors = np.concatenate([
        a["ffn_norm"].reshape(4, D), a["mix_norm"], a["final_norm"][None], a["rk_mu"][0], a["rk_w0"], a["rk_a0"],
        a["rk_k_k"], a["rk_k_a"], a["rk_r_k"].reshape(1, D), a["rk_ln_w"], a["rk_ln_b"], a["sc_conv_w"][0],
        np.zeros((1, D), f32)], 0)
    gu = a["ffn_w_gu"].reshape(4, D, 2 * FF)
    down = a["ffn_w_down"].reshape(4, 2, SMALL, P, KT, P).transpose(0, 4, 1, 3, 2, 5)
    w1a1 = np.concatenate([a["rk_w1"][0], a["rk_a1"][0]], 1)
    g1 = a["rk_g1"][0]
    gz = np.zeros((D, P - (g1.shape[1] - P)), f32)
    w1 = np.concatenate([w1a1, np.zeros((D, P), f32)], 1)
    g1 = np.concatenate([g1[:, :P], gz, g1[:, P:]], 1)
    zero = np.zeros((HD, D), f32)
    w2a2 = np.concatenate([np.concatenate([a["rk_w2"][0], zero], 0), np.concatenate([zero, a["rk_a2"][0]], 0)], 1)
    g2 = a["rk_g2"][0]
    g2 = np.concatenate([g2[:P], np.concatenate([np.zeros((2 * P - g2.shape[0], D), f32), g2[P:]], 0)], 1)
    straight = [(2 * s, 2 * s + 1) for s in range(4)]
    r, k, v = (_slots(a["rk_w_rkv"][0, i], straight) for i in range(3))
    mix = np.concatenate([k, _slots(w1, [(0, 1)]), w2a2[None], r, _slots(g1, [(0, 1)]), g2[None], v], 0)
    arrays = {
        "x": tiles(tokens),
        "vec": tiles(vectors),
        "const": _constants(),
        "shift": tiles(a["state_shift"][0]).reshape(P, -1),
        "conv": tiles(a["state_conv"][0].reshape(2 * SEQS, D)).reshape(P, -1),
        "wkv": a["state_wkv"][0].reshape(SEQS, PAIRS, 2, HD, HD).transpose(0, 2, 4, 1, 3).reshape(SEQS, P, -1),
        "gu": np.stack([_slots(gu[f], [(s, FT + s) for s in range(FT)]) for f in range(4)]),
        "down": down.reshape(4, 2 * KT, P, SMALL * P),
        "mix": mix,
        "wo": _slots(a["rk_w_o"][0], straight),
        "scin": _slots(a["sc_w_in"][0], [(KT + s, 2 * KT + s) for s in range(KT)] + straight),
        "scout": _slots(a["sc_w_out"][0], straight),
        "eye": np.broadcast_to(np.eye(C, dtype=f32).reshape(1, -1), (P, C * C)),
    }
    nc = bacc.Bacc("TRN2", target_bir_lowering=False, num_devices=1)
    arrays = {n: np.ascontiguousarray(arrays[n], dtype=f32) for n in _INPUTS}
    aps = [nc.dram_tensor(f"in_{n}", arrays[n].shape, F32, kind="ExternalInput").ap() for n in _INPUTS]
    outs = [nc.dram_tensor(f"out_{n}", s, F32, kind="ExternalOutput").ap() for n, s in _OUTPUTS.items()]
    scratch = [nc.dram_tensor(n, (CHUNKS, HEADS, C, C), F32).ap() for n in ("couplings", "inverses")]
    build_program(nc, *aps, *outs, *scratch)
    got = run_bass_kernel_spmd(nc, [{f"in_{n}": v for n, v in arrays.items()}], core_ids=[0]).results[0]
    y, wkvp, wkvs, shifto, convo = (got[f"out_{n}"] for n in _OUTPUTS)
    y = y.reshape(D, -1).T
    shifto = shifto.reshape(P, KT, -1).transpose(2, 1, 0).reshape(-1, D)
    convo = convo.reshape(P, KT, -1).transpose(2, 1, 0).reshape(-1, D)

    def states(s):
        return s.reshape(-1, 2, HD, PAIRS, HD).transpose(0, 3, 1, 4, 2).reshape(1, -1, HEADS, HD, HD)

    return (y[:SEQ].reshape(1, SEQ, D), y[SEQ:].reshape(SEQS, STEPS, D), states(wkvp), shifto[None, :1],
            convo[None, None, :2], states(wkvs), shifto[None, 1:], convo[2:].reshape(1, SEQS, 2, D))
```

```python
from contextlib import ExitStack

import concourse.bass as bass
from concourse import mybir

ALU = mybir.AluOpType
ACT = mybir.ActivationFunctionType
AX_X = mybir.AxisListType.X
F32 = mybir.dt.float32
F32R = mybir.dt.float32r

P = 128
D = 1024
KT = D // P
FF = 2816
FT = FF // P
META, SEQ, SEQS, STEPS = 16, 256, 8, 8
TP = META + SEQ
T = TP + SEQS * STEPS
HEADS, HD = 16, 64
PAIRS = HEADS // 2
C = 32
PAD = C - TP % C
TS = PAD + T
CHUNKS = TS // C
PCHUNKS = (PAD + TP) // C
SCH = CHUNKS - PCHUNKS
SPC = C // STEPS
LOADS = 5
EPS = 1e-6
GN_EPS = 64e-5
E_HALF = 0.6065306597126334
BIG, SMALL = 16, FT // 2
POOL_TILES = {BIG: 10, SMALL: 7}

V_NORM = 0
V_MIX = 4
V_FINAL = 6
V_MU = 7
V_W0, V_A0, V_KK, V_KA, V_RK, V_LNW, V_LNB = range(13, 20)
V_CONV = 20
V_OMKA = 23
NVEC = 24

K_ONES = 0
K_BLOCK = 128
K_EYE = 256
K_SEL = 320
K_SCAN = K_SEL + 16 * PAIRS
K_ZMASK = K_SCAN + TS
K_SEQCOL = K_ZMASK + CHUNKS * 2 * C
K_SEQROW = K_SEQCOL + SPC * C
K_SELT = K_SEQROW + SPC
NCONST = K_SELT + P * PAIRS


def build_program(nc, x_dram, vec_dram, const_dram, shift_dram, conv_dram, wkv_dram, gu_dram, down_dram,
                  mix_dram, wo_dram, scin_dram, scout_dram, blockeye_dram, y_out, wkvp_out, wkvs_out, shift_out,
                  convo_out, zt_dram, tt_dram):
    with ExitStack() as ctx:
        def sem(name):
            return ctx.enter_context(nc.semaphore(name))

        PS = ctx.enter_context(nc.psum_tensor("psum", [P, 8, 512], F32))

        top = [0]

        def at(name, shape, dt=F32, start=None):
            size = 4
            for n in shape[1:]:
                size *= n
            start = -(-top[0] // 32) * 32 if start is None else start
            t = nc.alloc_sbuf_tensor_at(name, shape, dt, offset=base + start)
            if start + size > top[0]:
                top[0] = start + size
            return t

        base = -(-nc.sbuf_base // 32) * 32
        x = at("x", [P, KT, T])
        raw = [at(f"w_raw{i}", [P, BIG * P]) for i in range(2)]
        whi = [at(f"w_hi{i}", [P, BIG * P], F32R) for i in range(2)]
        wlo = [at(f"w_lo{i}", [P, BIG * P], F32R) for i in range(2)]
        vec = at("vec", [P, KT, NVEC])
        con = at("con", [P, NCONST])
        cin = at("cin", [P, KT * 2 * SEQS])
        shin = at("shin", [P, KT * SEQS])
        stage = at("stage", [P, KT, 2 + 2 * SEQS])
        shst = at("shst", [P, KT, 1 + SEQS])
        e_start = -(-top[0] // 32) * 32
        tmp = [at(f"tmp{i}", [P, TS]) for i in range(8)]
        rstd = at("rstd", [P, T])
        acc_start = -(-top[0] // 32) * 32
        acc = at("acc", [P, T])
        ms = at("ms", [P, T])
        x_start = -(-top[0] // 32) * 32
        xhi = at("x_hi", [P, KT, T], F32R)
        xlo = at("x_lo", [P, KT, T], F32R)
        a_start = -(-top[0] // 32) * 32
        hhi = at("h_hi", [P, FT, T], F32R)
        hlo = at("h_lo", [P, FT, T], F32R)
        f_end = top[0]
        vy = at("vy", [P, PAIRS, TS], start=a_start)
        xx = at("xx", [P, KT, T], start=a_start)
        iv = a_start + 4 * PAIRS * TS
        gate = at("gate", [P, KT, T], start=iv)
        yb = at("yb", [P, KT, T], start=iv + 4 * KT * T)
        o1 = iv + 8 * KT * T
        ar = at("ar", [P, PAIRS, 2, TS], start=o1)
        o2 = o1 + 8 * PAIRS * TS
        bk = at("bk", [P, PAIRS, CHUNKS, 2, C], start=o2)
        o3 = o2 + 8 * PAIRS * TS
        hc = at("hc", [P, KT, T], start=o3)
        sw = at("sw", [P, PAIRS, TS], start=o3 + 4 * PAIRS * TS)
        z = at("z", [P, PAIRS, CHUNKS, 2 * C], start=o3)
        o4 = o3 + 8 * PAIRS * TS
        dend = at("dend", [P, PAIRS, PCHUNKS + SEQS], start=o4)
        rks = at("rks", [HEADS, T], start=o4 + 4 * PAIRS * (PCHUNKS + SEQS))
        ohi = at("o_hi", [P, KT, T], F32R, start=o1)
        olo = at("o_lo", [P, KT, T], F32R, start=o1 + 4 * KT * T)
        gt = at("gt", [P, 2, C * C], start=iv)
        wt = at("wt", [P, 2, C * C], start=iv + 8 * C * C)
        outer = [at(f"outer{i}", [P, C * C // 4], start=iv + 16 * C * C + i * C * C) for i in range(2)]
        thi = at("t_hi", [P, 2, T], F32R, start=acc_start)
        tlo = at("t_lo", [P, 2, T], F32R, start=iv + 18 * C * C)
        assert 18 * C * C + 8 * T <= 8 * KT * T
        q = x_start
        uv = [at(f"uv{i}", [P, PAIRS, HD], start=q + i * 2048) for i in range(2)]
        kv = [at(f"kv{i}", [P, PAIRS, HD], start=q + 4096 + i * 2048) for i in range(2)]
        st = [at(f"st{i}", [P, PAIRS, HD], start=q + 8192 + i * 2048) for i in range(2)]
        xs = at("xs", [P, PAIRS, HD], start=q + 12288)
        sd = at("sd", [P, PAIRS, HD], start=q + 14336)
        arm = at("arm", [P, SPC, PAIRS, C], start=q + 16384)
        assert q + 20480 <= a_start
        s0 = at("s0", [P, SPC, PAIRS, HD], start=e_start)
        ttc = [at(f"ttc{i}", [P, PAIRS, C], start=e_start + 8192 + i * 1024) for i in range(2)]
        up = at("up", [P, KT, 2 + SEQ], start=o3)
        us = at("us", [P, KT, SEQS, 2 + STEPS], start=o3 + 4 * KT * (2 + SEQ))
        cv = at("cv", [P, KT, SEQ + SEQS * STEPS], start=a_start)
        assert base + top[0] <= nc.sbuf_usable_end, (base + top[0], nc.sbuf_usable_end)

        loaded = sem("loaded")
        raw_full = [sem(f"raw_full{i}") for i in range(2)]
        hi_ready = sem("hi_ready")
        lo_pool = sem("lo_pool")
        lo_dve = sem("lo_dve")
        slot_used = sem("slot_used")
        scaled = sem("scaled")
        gate_scaled = sem("gate_scaled")
        act_ready = sem("act_ready")
        h_ready = sem("h_ready")
        hhi_ready = sem("hhi_ready")
        hlo_ready = sem("hlo_ready")
        x_new = sem("x_new")
        sq_ready = sem("sq_ready")
        acc_done = sem("acc_done")
        xg_ready = sem("xg_ready")
        xhi_ready = sem("xhi_ready")
        xlo_ready = sem("xlo_ready")
        ss_done = sem("ss_done")
        root_ready = sem("root_ready")
        rstd_ready = sem("rstd_ready")
        stored = sem("stored")

        block = ctx.enter_context(nc.Block())

        stream = {}
        first = 0
        for name, dram, slots, tiles in (
                ("gu0", gu_dram[0], FT, BIG), ("down0", down_dram[0], 2 * KT, SMALL),
                ("mix", mix_dram, 16, BIG), ("wo", wo_dram, 4, BIG),
                ("gu1", gu_dram[1], FT, BIG), ("down1", down_dram[1], 2 * KT, SMALL),
                ("gu2", gu_dram[2], FT, BIG), ("down2", down_dram[2], 2 * KT, SMALL),
                ("scin", scin_dram, 12, BIG), ("scout", scout_dram, 4, BIG),
                ("gu3", gu_dram[3], FT, BIG), ("down3", down_dram[3], 2 * KT, SMALL)):
            stream[name] = (first, slots, tiles, dram)
            first += slots
        order = list(stream)
        MIXB = stream["mix"][0]

        def next_tiles(name):
            i = order.index(name) + 1
            return stream[order[i]][2] if i < len(order) else 0

        def used(n):
            return n + 3 - (16 if n >= MIXB + 16 else 0) if isinstance(n, int) else None

        def used_base(name):
            n = stream[name][0]
            return n + 2 - (16 if n > MIXB else 0)

        FFN = {0: dict(q=1, ver=0, c0=0, n=T, scaled=0), 1: dict(q=3, ver=7, c0=14, n=T - 14, scaled=FT),
               2: dict(q=4, ver=8, c0=14, n=T - 14, scaled=2 * FT),
               3: dict(q=6, ver=10, c0=16, n=T - 16, scaled=3 * FT + 12)}
        CONV = dict(q=5, ver=9, c0=14, n=T - 14, scaled=3 * FT)
        SPLITS = {0: (0, V_NORM + 0, 0), 2: (7, V_NORM + 1, 14), 3: (8, V_NORM + 2, 14),
                  4: (9, V_MIX + 1, 14), 5: (10, V_NORM + 3, 16)}
        RCOL = {1: 0, 2: 14, 3: 14, 4: 14, 5: 16, 6: 16}

        def passes(w_hi, w_lo, x_hi, x_lo):
            return ((w_hi, x_hi), (w_hi, x_lo), (w_lo, x_hi))

        def split_act(act, half, par, tiles, free_sem, free_value):
            act.wait_ge(raw_full[par], 16 * half + 16)
            act.wait_ge(free_sem, free_value)
            act.activation(whi[par][:, :tiles * P], raw[par][:, :tiles * P], ACT.Copy).then_inc(hi_ready, 1)

        def split_pool(pool, half, par, tiles):
            n = POOL_TILES[tiles] * P
            pool.wait_ge(hi_ready, 2 * half + par + 1)
            pool.tensor_tensor(wlo[par][:, :n], raw[par][:, :n], whi[par][:, :n].bitcast(F32),
                               ALU.subtract).then_inc(lo_pool, 1)

        def split_dve(dve, half, par, tiles):
            a, b = POOL_TILES[tiles] * P, tiles * P
            dve.wait_ge(hi_ready, 2 * half + par + 1)
            dve.tensor_tensor(wlo[par][:, a:b], raw[par][:, a:b], whi[par][:, a:b].bitcast(F32),
                              ALU.subtract).then_inc(lo_dve, 1)

        def pe_slot_wait(pe, n):
            pe.wait_ge(lo_pool, n + 3)
            pe.wait_ge(lo_dve, n + 3)

        def load_phase(sp, name, lo=0, hi=None):
            first, slots, tiles, dram = stream[name]
            with sp.Fori(lo // 2, (slots if hi is None else hi) // 2) as i:
                for par in range(2):
                    n = first + 2 * i + par
                    sp.wait_ge(lo_pool, n + 1)
                    sp.wait_ge(lo_dve, n + 1)
                    sp.dma_start(raw[par][:, :tiles * P], dram[2 * i + par]).then_inc(raw_full[par], 16)

        def load_slot(sp, name, k):
            first, _, tiles, dram = stream[name]
            n = first + k
            sp.wait_ge(lo_pool, n + 1)
            sp.wait_ge(lo_dve, n + 1)
            sp.dma_start(raw[n % 2][:, :tiles * P], dram[k]).then_inc(raw_full[n % 2], 16)

        def res_dve(dve, q, m, par, alpha, ps, ready, split=True):
            if q:
                c = RCOL[q]
                dve.wait_ge(slot_used, ready)
                dve.scalar_tensor_tensor(out=x[:, m, c:], in0=ps[:, :T - c], scalar=alpha, in1=x[:, m, c:],
                                         op0=ALU.mult, op1=ALU.add).then_inc(x_new, 1)
            if q in SPLITS:
                ver, g, c = SPLITS[q]
                dve.wait_ge(x_new, 8 * q + m + 1 if q else 8)
                dve.tensor_scalar(tmp[4 + par][:, :T - c], x[:, m, c:], vec[:, m, g:g + 1], None,
                                  ALU.mult).then_inc(xg_ready, 1)

        def res_dve_after(dve, q, m, par, first):
            c = SPLITS[q][2] if q in SPLITS else RCOL[q]
            dve.wait_ge(sq_ready, 8 * q + m + 1)
            if first:
                dve.tensor_copy(acc[:, :T - c], tmp[6 + par][:, :T - c]).then_inc(acc_done, 1)
            else:
                dve.wait_ge(acc_done, 8 * q + m)
                dve.tensor_tensor(acc[:, :T - c], acc[:, :T - c], tmp[6 + par][:, :T - c],
                                  ALU.add).then_inc(acc_done, 1)
            if q in SPLITS:
                ver, g, c = SPLITS[q]
                dve.wait_ge(xhi_ready, 8 * ver + m + 1)
                dve.tensor_tensor(xlo[:, m, :T - c], tmp[4 + par][:, :T - c],
                                  xhi[:, m, :T - c].bitcast(F32), ALU.subtract).then_inc(xlo_ready, 1)

        def res_act(act, q, m, par, m_is_two_on=True):
            c = SPLITS[q][2] if q in SPLITS else RCOL[q]
            act.wait_ge(x_new, 8 * q + m + 1 if q else 8)
            if m_is_two_on:
                act.wait_ge(acc_done, 8 * q + m - 1)
            act.activation(tmp[6 + par][:, :T - c], x[:, m, c:], ACT.Square).then_inc(sq_ready, 1)
            if q in SPLITS:
                ver = SPLITS[q][0]
                act.wait_ge(xg_ready, 8 * ver + m + 1)
                act.activation(xhi[:, m, :T - c], tmp[4 + par][:, :T - c], ACT.Copy).then_inc(xhi_ready, 1)

        def norm_pe(pe, q, norm, n):
            pe.wait_ge(acc_done, 8 * q + 8)
            pe.matmul(PS[:, 6, :n], con[:, K_ONES:K_ONES + P], acc[:, :n], start=True, stop=True).then_inc(ss_done, 1)

        def norm_act(act, norm, n):
            act.wait_ge(ss_done, norm + 1)
            act.activation(ms[:, :n], PS[:, 6, :n], ACT.Sqrt, bias=EPS, scale=1.0 / D).then_inc(root_ready, 1)

        def norm_dve(dve, norm, n):
            dve.wait_ge(root_ready, norm + 1)
            dve.reciprocal(rstd[:, :n], ms[:, :n]).then_inc(rstd_ready, 1)
            dve.wait_ge(rstd_ready, norm + 1)

        def pe_pair(pe, par, banks, ver, n, out_sem, src=None, fresh=False):
            xh, xl = src or (xhi, xlo)
            for k in range(KT):
                if fresh:
                    pe.wait_ge(xlo_ready, 8 * ver + k + 1)
                for j in range(2):
                    for i, (w, v) in enumerate(passes(whi[par], wlo[par], xh, xl)):
                        last = pe.matmul(PS[:, banks[j], :n], w[:, (2 * k + j) * P:(2 * k + j + 1) * P], v[:, k, :n],
                                         start=(k == 0 and i == 0), stop=(k == KT - 1 and i == 2))
            last.then_inc(out_sem, 1)

        def ffn_pe(pe, f):
            d = FFN[f]
            gu, down, n = stream[f"gu{f}"][0], stream[f"down{f}"][0], d["n"]

            def gu_slot(i, par, fresh=False):
                pe_slot_wait(pe, gu + 2 * i + par)
                pe.wait_ge(scaled, d["scaled"] + 2 * i + par + 1)
                pe_pair(pe, par, (2 * par, 2 * par + 1), d["ver"], n, slot_used, fresh=fresh)

            if f in (1, 3):
                pe.wait_ge(x_new, 8 * (2 if f == 1 else 5) + 6)
            gu_slot(0, 0, fresh=True)
            norm_pe(pe, {0: 0, 1: 2, 2: 3, 3: 5}[f], 0, n)
            gu_slot(0, 1)
            with pe.Fori(1, FT // 2) as i:
                for par in range(2):
                    gu_slot(i, par)

            def down_tile(m, par, first=False):
                pe.wait_ge(x_new, 8 * d["q"] + m - 1)
                for half in range(2):
                    pe_slot_wait(pe, down + 2 * m + half)
                    for k in range(SMALL):
                        kk = half * SMALL + k
                        if first and kk in (0, FT - 2, FT - 1):
                            pe.wait_ge(hlo_ready, FT * f + max(kk + 1, FT - 2))
                        for i, (w, v) in enumerate(passes(whi[half], wlo[half], hhi, hlo)):
                            last = pe.matmul(PS[:, 4 + par, :n], w[:, k * P:(k + 1) * P], v[:, kk, :n],
                                             start=(kk == 0 and i == 0), stop=(kk == FT - 1 and i == 2))
                    last.then_inc(slot_used, 1)

            down_tile(0, 0, first=True)
            down_tile(1, 1)
            with pe.Fori(1, KT // 2) as i:
                for par in range(2):
                    down_tile(2 * i + par, par)

        def ffn_act(act, f):
            d = FFN[f]
            n, gub, dnb = d["n"], used_base(f"gu{f}"), used_base(f"down{f}")
            gu, down = stream[f"gu{f}"][0], stream[f"down{f}"][0]

            def gu_slot(i, par, tiles, first=False):
                split_act(act, gu // 2 + i + 1, par, tiles, slot_used, gub + 2 * i + par + 1)
                if first:
                    norm_act(act, {0: 0, 1: 2, 2: 3, 3: 5}[f], n)
                s = 2 * i + par
                act.wait_ge(gate_scaled, FT * f + s + 1)
                act.activation(tmp[1][:, :n], tmp[0][:, :n], ACT.Silu).then_inc(act_ready, 1)
                act.wait_ge(h_ready, FT * f + s + 1)
                act.activation(hhi[:, bass.ds(s, 1), :n], tmp[3][:, :n], ACT.Copy).then_inc(hhi_ready, 1)

            gu_slot(0, 0, BIG, first=True)
            gu_slot(0, 1, BIG)
            with act.Fori(1, FT // 2 - 1) as i:
                for par in range(2):
                    gu_slot(i, par, BIG)
            for par in range(2):
                gu_slot(FT // 2 - 1, par, SMALL)

            def down_tile(m, par, tiles, first=False, last=False):
                split_act(act, down // 2 + m + 1, 0, tiles, slot_used, dnb + 2 * m + 1) if tiles else None
                if last:
                    res_act(act, d["q"], m, par)
                if tiles:
                    split_act(act, down // 2 + m + 1, 1, tiles, slot_used, dnb + 2 * m + 2)
                if not last:
                    res_act(act, d["q"], m, par, not first)

            down_tile(0, 0, SMALL, first=True)
            down_tile(1, 1, SMALL, first=True)
            with act.Fori(1, KT // 2 - 1) as i:
                for par in range(2):
                    down_tile(2 * i + par, par, SMALL)
            down_tile(KT - 2, 0, SMALL)
            down_tile(KT - 1, 1, next_tiles(f"down{f}"), last=True)

        def ffn_dve(dve, f):
            d = FFN[f]
            n, gub, dnb = d["n"], used_base(f"gu{f}"), used_base(f"down{f}")
            gu, down = stream[f"gu{f}"][0], stream[f"down{f}"][0]

            def gu_slot(i, par, tiles, first=False):
                s = 2 * i + par
                if first:
                    norm_dve(dve, {0: 0, 1: 2, 2: 3, 3: 5}[f], n)
                dve.wait_ge(slot_used, gub + s + 1)
                dve.tensor_tensor(tmp[0][:, :n], PS[:, 2 * par, :n], rstd[:, :n], ALU.mult).then_inc(gate_scaled, 1)
                dve.tensor_tensor(tmp[2][:, :n], PS[:, 2 * par + 1, :n], rstd[:, :n], ALU.mult).then_inc(scaled, 1)
                split_dve(dve, gu // 2 + i + 1, par, tiles)
                dve.wait_ge(act_ready, FT * f + s + 1)
                dve.wait_ge(scaled, d["scaled"] + s + 3)
                dve.tensor_tensor(tmp[3][:, :n], tmp[1][:, :n], tmp[2][:, :n], ALU.mult).then_inc(h_ready, 1)
                dve.wait_ge(hhi_ready, FT * f + s + 1)
                dve.tensor_tensor(hlo[:, bass.ds(s, 1), :n], tmp[3][:, :n], hhi[:, bass.ds(s, 1), :n].bitcast(F32),
                                  ALU.subtract).then_inc(hlo_ready, 1)

            gu_slot(0, 0, BIG, first=True)
            gu_slot(0, 1, BIG)
            with dve.Fori(1, FT // 2 - 1) as i:
                for par in range(2):
                    gu_slot(i, par, BIG)
            for par in range(2):
                gu_slot(FT // 2 - 1, par, SMALL)

            def down_tile(m, par, tiles, first=False, last=False):
                if tiles:
                    split_dve(dve, down // 2 + m + 1, 0, tiles)
                res_dve(dve, d["q"], m, par, 0.5, PS[:, 4 + par, :], dnb + 2 * m + 2)
                if tiles and not last:
                    split_dve(dve, down // 2 + m + 1, 1, tiles)
                res_dve_after(dve, d["q"], m, par, first)
                if tiles and last:
                    split_dve(dve, down // 2 + m + 1, 1, tiles)

            down_tile(0, 0, SMALL, first=True)
            down_tile(1, 1, SMALL)
            with dve.Fori(1, KT // 2 - 1) as i:
                for par in range(2):
                    down_tile(2 * i + par, par, SMALL)
            down_tile(KT - 2, 0, SMALL)
            down_tile(KT - 1, 1, next_tiles(f"down{f}"), last=True)

        def split_phase_pool(pool, name):
            first, slots, tiles, _ = stream[name]
            with pool.Fori(0, slots // 2 - 1) as i:
                for par in range(2):
                    split_pool(pool, first // 2 + i + 1, par, tiles)
            if next_tiles(name):
                for par in range(2):
                    split_pool(pool, first // 2 + slots // 2, par, next_tiles(name))

        conv_u = sem("conv_u")
        o_ready = sem("o_ready")
        ohi_ready = sem("ohi_ready")
        olo_ready = sem("olo_ready")
        dve_line = sem("dve_line")
        line = [0]
        PR = 2 + SEQ

        def link(dve, ins):
            line[0] += 1
            ins.then_inc(dve_line, 1)
            dve.wait_ge(dve_line, line[0])

        def conv_pe(pe):
            d = CONV
            first = stream["scin"][0]
            for s in range(12):
                pe_slot_wait(pe, first + s)
                pe.wait_ge(scaled, d["scaled"] + s + 1)
                pe_pair(pe, s % 2, (2 * (s % 2), 2 * (s % 2) + 1), d["ver"], d["n"], slot_used, fresh=(s == 0))
                if s == 0:
                    norm_pe(pe, 4, 4, d["n"])
            project_pe(pe, "scout", 5, PR - 2 + SEQS * STEPS, KT)

        def project_pe(pe, name, q, n, olo_base):
            first = stream[name][0]
            for s in range(4):
                pe_slot_wait(pe, first + s)
                pe.wait_ge(x_new, 8 * q + 2 * s - 2)
                if s == 0:
                    pe.wait_ge(scaled, SCALED_BEFORE[name])
                    if name == "wo":
                        pe.wait_ge(mix_evac, MIX_GROUPS - 4)
                banks = ((2 * s) % 4, (2 * s + 1) % 4)
                for k in range(KT):
                    if s == 0:
                        pe.wait_ge(olo_ready, olo_base + k + 1)
                    for j in range(2):
                        for i, (w, v) in enumerate(passes(whi[s % 2], wlo[s % 2], ohi, olo)):
                            last = pe.matmul(PS[:, banks[j], :n], w[:, (2 * k + j) * P:(2 * k + j + 1) * P], v[:, k, :n],
                                             start=(k == 0 and i == 0), stop=(k == KT - 1 and i == 2))
                last.then_inc(slot_used, 1)

        SCALED_BEFORE = {"wo": 2 + FT, "scout": 2 + 3 * FT + 12}

        def project_act(act, name, q):
            first, base_used, nxt = stream[name][0], used_base(name), next_tiles(name)
            for s in range(4):
                tiles = BIG if s < 2 else nxt
                if s < 3:
                    split_act(act, first // 2 + (s + 2) // 2, s % 2, tiles, slot_used, base_used + s + 1)
                for m in (2 * s, 2 * s + 1):
                    res_act(act, q, m, m % 2, m >= 2)
                if s == 3:
                    split_act(act, first // 2 + (s + 2) // 2, s % 2, tiles, slot_used, base_used + s + 1)

        def project_dve(dve, name, q):
            first, base_used, nxt = stream[name][0], used_base(name), next_tiles(name)
            for s in range(4):
                tiles = BIG if s < 2 else nxt
                for m in (2 * s, 2 * s + 1):
                    res_dve(dve, q, m, m % 2, 1.0, PS[:, m % 4, :], base_used + s + 1)
                    if s < 3 and m % 2 == 0:
                        split_dve(dve, first // 2 + (s + 2) // 2, s % 2, tiles)
                    res_dve_after(dve, q, m, m % 2, m == 0)
                if s == 3:
                    split_dve(dve, first // 2 + (s + 2) // 2, s % 2, tiles)

        def conv_act(act):
            d = CONV
            first, ub = stream["scin"][0], used_base("scin")
            for s in range(12):
                split_act(act, first // 2 + (s + 2) // 2, s % 2, BIG, slot_used, ub + s + 1)
                if s == 0:
                    norm_act(act, 4, d["n"])
                if s >= 8:
                    for m in (2 * (s - 8), 2 * (s - 8) + 1):
                        act.wait_ge(o_ready, KT + m + 1)
                        act.activation(ohi[:, m, :TN], tmp[2 + m % 2][:, :TN], ACT.Copy).then_inc(ohi_ready, 1)
            project_act(act, "scout", 5)

        TN = SEQ + SEQS * STEPS

        def conv_dve(dve):
            d = CONV
            first, ub, n = stream["scin"][0], used_base("scin"), d["n"]
            w = [lambda f, c=c: vec[:, f, V_CONV + c:V_CONV + c + 1] for c in range(3)]
            for s in range(12):
                if s == 0:
                    norm_dve(dve, 4, n)
                    dve.wait_ge(loaded, 16 * LOADS)
                    link(dve, dve.tensor_copy(us[:, :, :, 0:2], cin[:, :].rearrange("p (k b w) -> p k b w", k=KT, w=2)))
                dve.wait_ge(slot_used, ub + s + 1)
                if s < 8:
                    f = s
                    link(dve, dve.tensor_tensor(tmp[0][:, :n], PS[:, 2 * (s % 2), :n], rstd[:, :n], ALU.mult))
                    dve.tensor_tensor(tmp[2][:, :n], PS[:, 2 * (s % 2) + 1, :n], rstd[:, :n], ALU.mult).then_inc(scaled, 1)
                    dve.wait_ge(scaled, d["scaled"] + s + 3)
                    split_dve(dve, first // 2 + (s + 2) // 2, s % 2, BIG)
                    dve.tensor_tensor(up[:, f, :], tmp[0][:, :PR], tmp[2][:, :PR], ALU.mult)
                    link(dve, dve.tensor_tensor(
                        us[:, f, :, 2:], tmp[0][:, PR:n].rearrange("p (b t) -> p b t", t=STEPS),
                        tmp[2][:, PR:n].rearrange("p (b t) -> p b t", t=STEPS), ALU.mult))
                    cs = cv[:, f, SEQ:].rearrange("p (b t) -> p b t", t=STEPS)
                    dve.tensor_scalar(cv[:, f, :SEQ], up[:, f, 0:SEQ], w[0](f), None, ALU.mult)
                    link(dve, dve.tensor_scalar(cs, us[:, f, :, 0:STEPS], w[0](f), None, ALU.mult))
                    for c in (1, 2):
                        dve.scalar_tensor_tensor(out=cv[:, f, :SEQ], in0=up[:, f, c:c + SEQ], scalar=w[c](f),
                                                 in1=cv[:, f, :SEQ], op0=ALU.mult, op1=ALU.add)
                        link(dve, dve.scalar_tensor_tensor(out=cs, in0=us[:, f, :, c:c + STEPS], scalar=w[c](f),
                                                           in1=cs, op0=ALU.mult, op1=ALU.add))
                else:
                    ms_ = (2 * (s - 8), 2 * (s - 8) + 1)
                    link(dve, dve.tensor_tensor(tmp[0][:, :TN], PS[:, 2 * (s % 2), 2:n], rstd[:, 2:n], ALU.mult))
                    dve.tensor_tensor(tmp[1][:, :TN], PS[:, 2 * (s % 2) + 1, 2:n], rstd[:, 2:n], ALU.mult).then_inc(scaled, 1)
                    dve.wait_ge(scaled, d["scaled"] + s + 3)
                    for m in ms_:
                        dve.tensor_tensor(tmp[2 + m % 2][:, :TN], tmp[m % 2][:, :TN], cv[:, m, :],
                                          ALU.mult).then_inc(o_ready, 1)
                    split_dve(dve, first // 2 + (s + 2) // 2, s % 2, BIG)
                    for m in ms_:
                        dve.wait_ge(ohi_ready, KT + m + 1)
                        dve.tensor_tensor(olo[:, m, :TN], tmp[2 + m % 2][:, :TN], ohi[:, m, :TN].bitcast(F32),
                                          ALU.subtract).then_inc(olo_ready, 1)
                if s == 8:
                    link(dve, dve.tensor_copy(stage[:, :, 0:2], up[:, :, SEQ:]))
                    dve.tensor_copy(stage[:, :, 2:].rearrange("p k (b w) -> p k b w", w=2),
                                    us[:, :, :, STEPS:]).then_inc(conv_u, 1)
            project_dve(dve, "scout", 5)

        def final_pe(pe):
            norm_pe(pe, 6, 6, TN)

        def final_dve(dve):
            norm_dve(dve, 6, TN)
            for k in range(KT):
                dve.scalar_tensor_tensor(out=cv[:, k, :], in0=x[:, k, 16:], scalar=vec[:, k, V_FINAL:V_FINAL + 1],
                                         in1=rstd[:, :TN], op0=ALU.mult, op1=ALU.mult).then_inc(y_ready, 1)

        y_ready = sem("y_ready")

        MIX_GROUPS = 27
        R_GROUP = 15
        LAST_GROUP = [0, 1, 2, 3, 9, 13, 14, 15, 16, 17, 18, 19, 20, 21, 22, 26]
        XK, XW, XA, XG, XR, XV = 1, 2, 3, 4, 5, 6
        VER_GROUP = {XK: 3, XW: 4, XA: 5, XG: 14, XR: 18}
        MU = {XR: 0, XW: 1, XK: 2, XV: 3, XA: 4, XG: 5}
        RD = slice(PAD, TS)
        YC = PAD + 14
        NY = TS - YC

        mix_out = sem("mix_out")
        mix_evac = sem("mix_evac")
        r_scaled = sem("r_scaled")
        x_used = sem("x_used")
        lora_hi = sem("lora_hi")
        lora_in = sem("lora_in")
        lora_lo = sem("lora_lo")
        kk_ready = sem("kk_ready")
        kk_sq = sem("kk_sq")
        kk_ss = sem("kk_ss")
        kk_max = sem("kk_max")
        kk_root = sem("kk_root")
        kk_inv = sem("kk_inv")
        kk_spread = sem("kk_spread")
        a_normed = sem("a_normed")
        logs_ready = sem("logs_ready")
        decays = sem("decays")
        r_decay = sem("r_decay")
        ends_ready = sem("ends_ready")
        a_scaled = sem("a_scaled")
        bk_scaled = sem("bk_scaled")
        rk_ready = sem("rk_ready")
        rk_sum = sem("rk_sum")
        rk_kept = sem("rk_kept")
        z_done = sem("z_done")
        z_ready = sem("z_ready")
        z_stored = sem("z_stored")
        g_loaded = sem("g_loaded")
        inv_dve = sem("inv_dve")
        inv_pool = sem("inv_pool")
        inv_stored = sem("inv_stored")
        tt_loaded = [sem(f"tt_loaded{i}") for i in range(2)]
        shift_ready = sem("shift_ready")

        def mix_sp(sp):
            load_phase(sp, "mix", 0, 14)
            load_slot(sp, "mix", 14)
            sp.wait_ge(shift_ready, 1)
            sp.dma_start(shift_out, shst[:].rearrange("p k n -> p (k n)")).then_inc(stored, 16)
            for i in range(2):
                sp.dma_start(wt[:, i, :], blockeye_dram).then_inc(g_loaded, 16)
            for p in range(PAIRS):
                sp.wait_ge(z_ready, 2 * p + 2)
                for hh in range(2):
                    rows = slice(HD * hh, HD * hh + C)
                    sp.dma_start(zt_dram[:, 2 * p + hh].rearrange("c s t -> s c t"),
                                 z[rows, p, :, 0:C]).then_inc(z_stored, 16)
            sp.wait_ge(z_stored, 16 * HEADS)
            sp.dma_start(gt[:, 0, :], zt_dram[0:8].rearrange("c h s t -> (c h) (s t)")).then_inc(g_loaded, 16)
            sp.dma_start(gt[:REST, 1, :], zt_dram[8:].rearrange("c h s t -> (c h) (s t)")).then_inc(g_loaded, 16)
            load_slot(sp, "mix", 15)
            load_slot(sp, "wo", 0)
            load_slot(sp, "wo", 1)
            sp.wait_ge(inv_dve, 2 * (C - 1))
            sp.dma_start(tt_dram[0:8].rearrange("c h s t -> (c h) (s t)"), wt[:, 0, :]).then_inc(inv_stored, 16)
            sp.wait_ge(inv_pool, 2 * (C - 1))
            sp.dma_start(tt_dram[8:].rearrange("c h s t -> (c h) (s t)"), wt[:REST, 1, :]).then_inc(inv_stored, 16)
            sp.wait_ge(inv_stored, 32)

            def load_inverses(c):
                if c >= 2:
                    sp.wait_ge(u_done, 2 * (c - 1))
                for hh in range(2):
                    sp.dma_start(ttc[c % 2][HD * hh:HD * hh + C, :, :],
                                 tt_dram[c].rearrange("(p two) s t -> two s p t", two=2)[hh]).then_inc(tt_loaded[c % 2], 16)

            load_inverses(0)
            load_inverses(1)
            sp.wait_ge(rk_sum, PAIRS)
            for q in range(SPC):
                sp.dma_start(s0[:, q].rearrange("p a b -> p (a b)"), wkv_dram[q]).then_inc(s0_loaded, 16)
            load_slot(sp, "wo", 2)
            load_slot(sp, "wo", 3)
            for c in range(2, CHUNKS):
                load_inverses(c)
                if c == PCHUNKS:
                    sp.wait_ge(st_ready, 2 * PCHUNKS + 1)
                    sp.dma_start(wkvp_out, st[PCHUNKS % 2][:].rearrange("p a b -> p (a b)")).then_inc(final_stored, 16)
            for n in range(SEQS):
                sp.wait_ge(seq_ready, n + 1)
                sp.dma_start(wkvs_out[n], s0[:, n % SPC].rearrange("p a b -> p (a b)")).then_inc(seq_stored, 16)
                if n < SPC:
                    sp.wait_ge(seq_stored, 16 * (n + 1))
                    sp.dma_start(s0[:, n].rearrange("p a b -> p (a b)"), wkv_dram[SPC + n]).then_inc(s0_loaded, 16)
            sp.wait_ge(seq_stored, 16 * SEQS)

        REST = (CHUNKS - 8) * HEADS
        MIX_STORES = 1
        s0_loaded = sem("s0_loaded")
        seq_ready = sem("seq_ready")
        seq_stored = sem("seq_stored")
        final_stored = sem("final_stored")
        x_done = sem("x_done")
        xs_dve = sem("xs_dve")
        xs_act = sem("xs_act")
        u_done = sem("u_done")
        uv_dve = sem("uv_dve")
        uv_act = sem("uv_act")
        s_done = sem("s_done")
        st_ready = sem("st_ready")
        y_done = sem("y_done")
        y_evac = sem("y_evac")
        prep_done = sem("prep_done")
        prep_evac = sem("prep_evac")
        arm_ready = sem("arm_ready")
        kvm_ready = sem("kvm_ready")
        q_done = sem("q_done")

        def mix_pe(pe):
            norm_pe(pe, 1, 1, T)
            group = [0]

            def open_group():
                g = group[0]
                group[0] += 1
                if g - 2 in range(R_GROUP, R_GROUP + 4):
                    pe.wait_ge(r_scaled, 2 * (g - 2 - R_GROUP) + 2)
                elif g >= 2:
                    pe.wait_ge(mix_evac, g - 1 - (4 if g - 2 >= R_GROUP else 0))
                return 2 * (g % 2)

            def project(slot, ver, fresh, final=False, shift=0):
                pe_slot_wait(pe, MIXB + slot)
                b = open_group()
                w_hi, w_lo = whi[slot % 2], wlo[slot % 2]
                for k in range(KT):
                    if fresh:
                        pe.wait_ge(xlo_ready, 8 * ver + k + 1)
                    for j in range(2):
                        for i, (w, v) in enumerate(passes(w_hi, w_lo, xhi, xlo)):
                            last = pe.matmul(PS[:, b + j, shift:shift + T], w[:, (2 * k + j) * P:(2 * k + j + 1) * P],
                                             v[:, k, :], start=(k == 0 and i == 0), stop=(k == KT - 1 and i == 2))
                    if final and k < KT - 1:
                        last.then_inc(x_used, 1)
                last.then_inc(mix_out, 1)

            def lora_inner(slot, ver):
                pe_slot_wait(pe, MIXB + slot)
                b = open_group()
                for k in range(KT):
                    pe.wait_ge(xlo_ready, 8 * ver + k + 1)
                    for i, (w, v) in enumerate(passes(whi[slot % 2], wlo[slot % 2], xhi, xlo)):
                        last = pe.matmul(PS[:, b, :T], w[:, k * P:(k + 1) * P], v[:, k, :],
                                         start=(k == 0 and i == 0), stop=(k == KT - 1 and i == 2))
                    if k < KT - 1:
                        last.then_inc(x_used, 1)
                last.then_inc(mix_out, 1)

            def lora_out(slot, first_tile, inner, shift=0):
                for m in range(0, KT, 2):
                    b = open_group()
                    for j in range(2):
                        for n, k in enumerate(inner):
                            tile = first_tile + KT * n + m + j
                            for i, (w, v) in enumerate(passes(whi[slot % 2], wlo[slot % 2], thi, tlo)):
                                last = pe.matmul(PS[:, b + j, shift:shift + T], w[:, tile * P:(tile + 1) * P], v[:, k, :],
                                                 start=(n == 0 and i == 0), stop=(n == len(inner) - 1 and i == 2))
                    last.then_inc(mix_out, 1)

            for s in range(4):
                project(s, XK, s == 0, s == 3, PAD)
            lora_inner(4, XW)
            for p in range(PAIRS):
                pe.wait_ge(kk_sq, p + 1)
                last = pe.matmul(PS[0:HEADS, 6, :T], con[:, K_SEL + 16 * p:K_SEL + 16 * p + 16],
                                 tmp[6 + p % 2][:, RD], start=(p == 0), stop=(p == PAIRS - 1))
                last.then_inc(kk_ss, 1)
            lora_inner(5, XA)
            pe.wait_ge(lora_lo, 1)
            lora_out(4, KT, (0,))
            pe.wait_ge(lora_lo, 2)
            lora_out(5, KT, (1,), PAD)
            project(6, XG, True, True)

            def spread(p):
                if p >= 2:
                    pe.wait_ge(a_normed, p - 1)
                pe.matmul(PS[:, 4 + p % 2, :T], con[0:HEADS, K_SELT + P * p:K_SELT + P * p + P], rstd[0:HEADS, :],
                          start=True, stop=True).then_inc(kk_spread, 1)

            pe.wait_ge(kk_inv, 1)
            for s in range(4):
                spread(2 * s)
                spread(2 * s + 1)
                project(7 + s, XR, s == 0, s == 3)
            pe.wait_ge(a_scaled, PAIRS)

            def sum_rk(p):
                pe.wait_ge(rk_ready, p + 1)
                if p == 0:
                    pe.wait_ge(r_scaled, PAIRS)
                pe.matmul(PS[0:HEADS, 0, :T], con[:, K_SEL + 16 * p:K_SEL + 16 * p + 16], tmp[p % 2][:, RD],
                          start=(p == 0), stop=(p == PAIRS - 1)).then_inc(rk_sum, 1)

            for p in range(PAIRS):
                pe.wait_ge(bk_scaled, p + 1)
                pe.wait_ge(r_scaled, p + 1)
                if p >= 2:
                    pe.wait_ge(z_ready, 2 * p - 2)
                for c in range(CHUNKS):
                    for hh in range(2):
                        rows = slice(HD * hh, HD * hh + HD)
                        last = pe.matmul(PS[rows, 4 + 2 * (p % 2) + c // 8, (c % 8) * 64:(c % 8) * 64 + 64],
                                         bk[rows, p, c, :, :].rearrange("p h t -> p (h t)"),
                                         ar[rows, p, :, c * C:c * C + C], start=True, stop=True)
                last.then_inc(z_done, 1)
                if p:
                    sum_rk(p - 1)
            sum_rk(PAIRS - 1)
            for s in range(4):
                if s == 1:
                    pe.wait_ge(rk_kept, 1)
                project(11 + s, XV, s == 0)
            pe_slot_wait(pe, MIXB + 15)
            pe.wait_ge(lora_lo, 4)
            lora_out(15, 0, (0, 1))
            chain_pe(pe)
            pe.wait_ge(y_evac, CHUNKS)
            for p in range(PAIRS):
                if p >= 2:
                    pe.wait_ge(yc_ready, p - 1)
                    pe.wait_ge(bonus_ready, p - 1)
                pe.matmul(PS[:, p % 2, :NY], con[:, K_BLOCK:K_BLOCK + P], yb[:, p, 14:], start=True, stop=True)\
                    .then_inc(mean_done, 1)
                pe.matmul(PS[:, 2 + p % 2, :NY], con[0:HEADS, K_SELT + P * p:K_SELT + P * p + P], rks[:, 14:],
                          start=True, stop=True).then_inc(rk_spread, 1)
            for p in range(PAIRS):
                pe.wait_ge(yc_sq, p + 1)
                pe.matmul(PS[0:HEADS, 6, :NY], con[:, K_SEL + 16 * p:K_SEL + 16 * p + 16],
                          tmp[6 + p % 2][:, :NY], start=(p == 0), stop=(p == PAIRS - 1)).then_inc(var_done, 1)
            pe.wait_ge(gn_inv, 1)
            for p in range(PAIRS):
                if p >= 2:
                    pe.wait_ge(gn_used, p - 1)
                pe.matmul(PS[:, 4 + p % 2, :NY], con[0:HEADS, K_SELT + P * p:K_SELT + P * p + P], rstd[0:HEADS, :NY],
                          start=True, stop=True).then_inc(gn_spread, 1)
            project_pe(pe, "wo", 2, T - 14, 0)

        mean_done = sem("mean_done")
        rk_spread = sem("rk_spread")
        bonus_ready = sem("bonus_ready")
        yc_ready = sem("yc_ready")
        yc_sq = sem("yc_sq")
        var_done = sem("var_done")
        gn_root = sem("gn_root")
        gn_inv = sem("gn_inv")
        gn_spread = sem("gn_spread")
        gn_used = sem("gn_used")

        def chain_pe(pe):
            def prep(c, g):
                k = 2 * c + g
                if k >= 1:
                    pe.wait_ge(prep_evac, k)
                else:
                    pe.wait_ge(z_ready, 2 * PAIRS)
                for p in range(4 * g, 4 * g + 4):
                    for hh in range(2):
                        rows = slice(HD * hh, HD * hh + HD)
                        a = (p - 4 * g) * HD
                        pe.matmul(PS[HD * hh + C:HD * hh + 2 * C, 6, a:a + HD], vy[rows, p, c * C:c * C + C],
                                  con[rows, K_EYE:K_EYE + HD], start=True, stop=True)
                        last = pe.matmul(PS[rows, 6, 256 + a:256 + a + HD], bk[rows, p, c, :, :].rearrange("p h t -> p (h t)"),
                                         con[rows, K_EYE:K_EYE + HD], start=True, stop=True)
                last.then_inc(prep_done, 1)

            def step_x(c, g):
                pe.wait_ge(prep_evac, 2 * c + g + 1)
                if c < PCHUNKS:
                    pe.wait_ge(st_ready, 2 * c + 1 if c == 0 else 2 * c + g)
                    if c == 0:
                        pe.wait_ge(z_ready, 2 * PAIRS)
                else:
                    pe.wait_ge(arm_ready, c - PCHUNKS + 1)
                    pe.wait_ge(s0_loaded, 16 * SPC * (c - PCHUNKS + 1))
                if c >= 1:
                    pe.wait_ge(xs_dve, 2 * (c - 1) + g + 1)
                    pe.wait_ge(xs_act, 2 * (c - 1) + g + 1)
                for p in range(4 * g, 4 * g + 4):
                    for hh in range(2):
                        rows = slice(HD * hh, HD * hh + HD)
                        out = PS[HD * hh:HD * hh + C, g, (p - 4 * g) * HD:(p - 4 * g + 1) * HD]
                        if c < PCHUNKS:
                            pe.matmul(out, ar[rows, p, 0, c * C:c * C + C], st[c % 2][rows, p, :], start=True, stop=False)
                        else:
                            for q in range(SPC):
                                pe.matmul(out, arm[rows, q, p, :], s0[rows, q, p, :], start=(q == 0), stop=False)
                        rows = slice(HD * hh + C, HD * hh + 2 * C)
                        last = pe.matmul(out, z[rows, p, c, 0:C], uv[c % 2][rows, p, :], start=False, stop=True)
                last.then_inc(x_done, 1)

            def step_u(c, g):
                pe.wait_ge(tt_loaded[c % 2], 32 * (c // 2 + 1))
                pe.wait_ge(xs_dve, 2 * c + g + 1)
                pe.wait_ge(xs_act, 2 * c + g + 1)
                if c >= 1:
                    pe.wait_ge(uv_dve, 2 * (c - 1) + g + 1)
                    pe.wait_ge(uv_act, 2 * (c - 1) + g + 1)
                for p in range(4 * g, 4 * g + 4):
                    for hh in range(2):
                        rows = slice(HD * hh, HD * hh + C)
                        last = pe.matmul(PS[rows, 2 + g, (p - 4 * g) * HD:(p - 4 * g + 1) * HD],
                                         ttc[c % 2][rows, p, :], xs[rows, p, :], start=True, stop=True)
                last.then_inc(u_done, 1)

            def step_s(c, g):
                pe.wait_ge(uv_dve, 2 * c + g + 1)
                pe.wait_ge(uv_act, 2 * c + g + 1)
                if c >= 1:
                    pe.wait_ge(st_ready, 2 * c + g)
                for p in range(4 * g, 4 * g + 4):
                    for hh in range(2):
                        rows = slice(HD * hh, HD * hh + HD)
                        last = pe.matmul(PS[rows, 4 + g, (p - 4 * g) * HD:(p - 4 * g + 1) * HD],
                                         kv[c % 2][rows, p, :], uv[c % 2][rows, p, :], start=True, stop=True)
                last.then_inc(s_done, 1)

            def step_y(c):
                if c >= 1:
                    pe.wait_ge(y_evac, c)
                pe.wait_ge(uv_dve, 2 * c + 2)
                pe.wait_ge(uv_act, 2 * c + 2)
                for p in range(PAIRS):
                    for hh in range(2):
                        rows = slice(HD * hh, HD * hh + HD)
                        last = pe.matmul(PS[rows, 7, p * C:p * C + C], uv[c % 2][rows, p, :], z[rows, p, c, C:],
                                         start=True, stop=False)
                        if c < PCHUNKS:
                            last = pe.matmul(PS[rows, 7, p * C:p * C + C], st[c % 2][rows, p, :],
                                             ar[rows, p, 1, c * C:c * C + C], start=False, stop=True)
                        else:
                            for q in range(SPC):
                                a = q * STEPS
                                last = pe.matmul(PS[rows, 7, p * C + a:p * C + a + STEPS], s0[rows, q, p, :],
                                                 ar[rows, p, 1, c * C + a:c * C + a + STEPS],
                                                 start=False, stop=(q == SPC - 1))
                last.then_inc(y_done, 1)

            def step_q(c):
                for q in range(SPC):
                    k = SPC * (c - PCHUNKS) + q
                    pe.wait_ge(kvm_ready, k + 1)
                    if k >= 2:
                        pe.wait_ge(seq_ready, k - 1)
                    for p in range(PAIRS):
                        for hh in range(2):
                            rows = slice(HD * hh, HD * hh + HD)
                            last = pe.matmul(PS[rows, 4 + q % 2, p * HD:p * HD + HD], st[q % 2][rows, p, :],
                                             uv[c % 2][rows, p, :], start=True, stop=True)
                    last.then_inc(q_done, 1)

            prep(0, 0)
            prep(0, 1)
            for c in range(CHUNKS):
                step_x(c, 0)
                step_x(c, 1)
                if c + 1 < CHUNKS:
                    prep(c + 1, 0)
                step_u(c, 0)
                step_u(c, 1)
                if c + 1 < CHUNKS:
                    prep(c + 1, 1)
                if c < PCHUNKS:
                    step_s(c, 0)
                    step_s(c, 1)
                step_y(c)
                if c >= PCHUNKS:
                    step_q(c)

        def mix_act(act):
            dn = used_base("down0")
            norm_act(act, 1, T)

            def split(k):
                split_act(act, (MIXB + k) // 2, k % 2, BIG, mix_out, LAST_GROUP[k - 2] + 1)

            def x_hi_tile(ver, k):
                act.wait_ge(xg_ready, 8 * ver + k + 1)
                if ver > XK:
                    if k < KT - 1:
                        act.wait_ge(x_used, (KT - 1) * (ver - 2) + k + 1)
                    else:
                        act.wait_ge(mix_out, VER_GROUP[ver - 1] + 1)
                act.activation(xhi[:, k, :], tmp[4 + k % 2][:, :T], ACT.Copy).then_inc(xhi_ready, 1)

            def x_hi(ver):
                for k in range(KT):
                    x_hi_tile(ver, k)

            def evac(g, outs):
                act.wait_ge(mix_out, g + 1)
                for j, (dst, func, bias, padded) in enumerate(outs):
                    kw = {} if bias is None else {"bias": bias}
                    src = PS[:, 2 * (g % 2) + j, :T]
                    if padded:
                        src = PS[:, 2 * (g % 2) + j, :TS].rearrange("p (c t) -> p c t", t=C)
                    last = act.activation(dst, src, func, **kw)
                last.then_inc(mix_evac, 1)

            def square_kk(p):
                act.wait_ge(kk_ready, p + 1)
                if p >= 2:
                    act.wait_ge(kk_ss, p - 1)
                act.activation(tmp[6 + p % 2][:, RD], ar[:, p, 0, PAD:], ACT.Square).then_inc(kk_sq, 1)

            def decay(p):
                act.wait_ge(logs_ready, p + 1)
                if p >= 2:
                    act.wait_ge(a_scaled, p - 1)
                    act.wait_ge(bk_scaled, p - 1)
                act.activation(tmp[2 + p % 2][:, RD], sw[:, p, PAD:], ACT.Exp, scale=-E_HALF).then_inc(decays, 1)
                act.activation(tmp[6 + p % 2][:, RD], sw[:, p, PAD:], ACT.Exp, scale=E_HALF).then_inc(decays, 1)

            def decay_r(p):
                act.wait_ge(logs_ready, p + 1)
                if p >= 2:
                    act.wait_ge(r_scaled, p - 1)
                act.activation(tmp[p % 2][:, RD], sw[:, p, PAD:], ACT.Exp, scale=-E_HALF).then_inc(r_decay, 1)

            x_hi(XK)
            for s in range(4):
                if s == 3:
                    x_hi(XW)
                split(2 + s)
                evac(s, [(bk[:, m, :, 1, :], ACT.Copy, None, True) for m in (2 * s, 2 * s + 1)])
            for k in range(KT):
                x_hi_tile(XA, k)
                square_kk(k)
            act.wait_ge(mix_out, 5)
            act.activation(tmp[0][:, :T], PS[:, 0, :T], ACT.Tanh).then_inc(mix_evac, 1)
            act.wait_ge(mix_evac, 5)
            act.activation(thi[:, 0, :], tmp[0][:, :T], ACT.Copy).then_inc(lora_hi, 1)
            for k in range(4):
                x_hi_tile(XG, k)
            act.wait_ge(mix_out, 6)
            act.activation(tmp[1][:, :T], PS[:, 2, :T], ACT.Copy).then_inc(mix_evac, 1)
            act.wait_ge(mix_evac, 6)
            act.activation(thi[:, 1, :], tmp[1][:, :T], ACT.Copy).then_inc(lora_hi, 1)
            for k in range(4, KT):
                x_hi_tile(XG, k)
            act.wait_ge(kk_max, 1)
            act.activation(tmp[3][0:HEADS, :T], tmp[3][0:HEADS, :T], ACT.Sqrt).then_inc(kk_root, 1)
            for s in range(4):
                evac(6 + s, [(sw[:, m, PAD:], ACT.Sigmoid, vec[:, m, V_W0:V_W0 + 1], False) for m in (2 * s, 2 * s + 1)])
            split(6)
            for s in range(4):
                evac(10 + s, [(bk[:, m, :, 0, :], ACT.Sigmoid, vec[:, m, V_A0:V_A0 + 1], True) for m in (2 * s, 2 * s + 1)])
            split(7)
            x_hi(XR)
            split(8)
            act.wait_ge(mix_out, 15)
            act.wait_ge(kk_inv, 1)
            act.activation(tmp[2][:, :T], PS[:, 0, :T], ACT.Sigmoid).then_inc(lora_in, 1)
            act.activation(tmp[3][:, :T], PS[:, 1, :T], ACT.Sigmoid).then_inc(mix_evac, 1)
            act.wait_ge(mix_evac, 15)
            act.wait_ge(lora_in, 1)
            act.activation(thi[:, 0, :], tmp[2][:, :T], ACT.Copy).then_inc(lora_hi, 1)
            act.activation(thi[:, 1, :], tmp[3][:, :T], ACT.Copy).then_inc(lora_hi, 1)
            for p in range(PAIRS):
                decay(p)
                if p in (3, 5, 7):
                    split(8 + p // 2)
                if p >= 1:
                    decay_r(p - 1)
            for lo, hi, first, step in ((0, PCHUNKS, C - 1, C), (PCHUNKS, PCHUNKS + SEQS, PCHUNKS * C + STEPS - 1, STEPS)):
                act.activation(dend[:, :, lo:hi], sw[:, :, first:first + (hi - lo - 1) * step + 1:step], ACT.Exp,
                               scale=-E_HALF).then_inc(ends_ready, 1)
            x_hi(XV)
            decay_r(PAIRS - 1)
            split(12)
            act.wait_ge(rk_sum, PAIRS)
            act.activation(rks[:, :], PS[0:HEADS, 0, :T], ACT.Copy).then_inc(rk_kept, 1)
            for s in range(4):
                split(13 + s)
                evac(19 + s, [(vy[:, m, PAD:], ACT.Copy, None, False) for m in (2 * s, 2 * s + 1)])
            act.wait_ge(inv_stored, 32)
            for s in range(4):
                evac(23 + s, [(gate[:, m, :], ACT.Copy, None, False) for m in (2 * s, 2 * s + 1)])
            split(17)
            chain_act(act)
            for p in range(PAIRS):
                act.wait_ge(yc_ready, p + 1)
                if p >= 2:
                    act.wait_ge(var_done, p - 1)
                act.activation(tmp[6 + p % 2][:, :NY], yb[:, p, 14:], ACT.Square).then_inc(yc_sq, 1)
            act.wait_ge(var_done, PAIRS)
            act.activation(ms[0:HEADS, :NY], PS[0:HEADS, 6, :NY], ACT.Sqrt, bias=GN_EPS, scale=1.0 / HD)\
                .then_inc(gn_root, 1)
            for p in range(PAIRS):
                act.wait_ge(o_ready, p + 1)
                act.activation(ohi[:, p, :NY], tmp[4 + p % 2][:, :NY], ACT.Copy).then_inc(ohi_ready, 1)
            project_act(act, "wo", 2)

        def chain_act(act):
            def prep(c, g):
                act.wait_ge(prep_done, 2 * c + g + 1)
                if c >= 2:
                    act.wait_ge(y_done, c - 1)
                ps = slice(4 * g, 4 * g + 4)
                act.activation(kv[c % 2][:, ps, :], PS[:, 6, 256:512].rearrange("p (a b) -> p a b", b=HD), ACT.Copy)
                for hh in range(2):
                    rows = slice(HD * hh + C, HD * hh + 2 * C)
                    last = act.activation(uv[c % 2][rows, ps, :],
                                          PS[rows, 6, 0:256].rearrange("p (a b) -> p a b", b=HD), ACT.Copy)
                last.then_inc(prep_evac, 1)

            def odd(done, dst, bank, out_sem, c, g):
                act.wait_ge(done, 2 * c + g + 1)
                act.activation(dst[HD:HD + C, 4 * g:4 * g + 4, :],
                               PS[HD:HD + C, bank + g, 0:256].rearrange("p (a b) -> p a b", b=HD),
                               ACT.Copy).then_inc(out_sem, 1)

            prep(0, 0)
            prep(0, 1)
            for c in range(CHUNKS):
                for g in range(2):
                    if c >= 1:
                        act.wait_ge(u_done, 2 * (c - 1) + g + 1)
                    odd(x_done, xs, 0, xs_act, c, g)
                if c + 1 < CHUNKS:
                    prep(c + 1, 0)
                for g in range(2):
                    odd(u_done, uv[c % 2], 2, uv_act, c, g)
                if c + 1 < CHUNKS:
                    prep(c + 1, 1)
                act.wait_ge(y_done, c + 1)
                skip = PAD if c == 0 else 0
                act.activation(yb[:, :, c * C - PAD + skip:c * C - PAD + C],
                               PS[:, 7, 0:256].rearrange("p (a b) -> p a b", b=C)[:, :, skip:], ACT.Copy).then_inc(y_evac, 1)

        def mix_pool(pool):
            def split(k):
                split_pool(pool, (MIXB + k) // 2, k % 2, BIG)

            for k in range(2, 9):
                split(k)
            for p in range(PAIRS):
                pool.wait_ge(decays, 2 * p + 2)
                pool.wait_ge(b_ready, p + 1)
                e = tmp[6 + p % 2][:].rearrange("p (c one t) -> p c one t", one=1, t=C)
                pool.tensor_tensor(bk[:, p], bk[:, p], e.to_broadcast([P, CHUNKS, 2, C]), ALU.mult).then_inc(bk_scaled, 1)
                if p in (3, 5, 7):
                    split(8 + p // 2)
            split(12)
            pool.wait_ge(g_loaded, 64)
            inverse(pool, 1, REST, inv_pool, split)
            split(17)

        def inverse(eng, slot, rows, out_sem, split):
            g = gt[:rows, slot, :].rearrange("p (s t) -> p s t", t=C)
            w = wt[:rows, slot, :].rearrange("p (s t) -> p s t", t=C)
            done = 0
            split_rows = {28: 13, 22: 14, 16: 15, 10: 16}
            for r in range(C - 1, 0, -1):
                if r in split_rows:
                    split(split_rows[r])
                n = C - r
                o = outer[slot][:rows, :r * n].rearrange("p (s t) -> p s t", t=n)
                if done:
                    eng.wait_ge(out_sem, done)
                eng.tensor_tensor(o, g[:, 0:r, r:r + 1].to_broadcast([rows, r, n]),
                                  w[:, r:r + 1, r:].to_broadcast([rows, r, n]), ALU.mult).then_inc(out_sem, 1)
                eng.wait_ge(out_sem, done + 1)
                eng.tensor_tensor(w[:, 0:r, r:], w[:, 0:r, r:], o, ALU.add).then_inc(out_sem, 1)
                done += 2

        def mix_dve(dve):
            norm_dve(dve, 1, T)
            seqs = slice(TP, T, STEPS)

            def split(k):
                split_dve(dve, (MIXB + k) // 2, k % 2, BIG)

            def mixed(ver, k):
                dve.wait_ge(xlo_ready, 8 * ver + k - 1)
                dve.scalar_tensor_tensor(out=tmp[4 + k % 2][:, :T], in0=xx[:, k, :],
                                         scalar=vec[:, k, V_MU + MU[ver]:V_MU + MU[ver] + 1], in1=hc[:, k, :],
                                         op0=ALU.mult, op1=ALU.add).then_inc(xg_ready, 1)

            def low(ver, k):
                dve.wait_ge(xhi_ready, 8 * ver + k + 1)
                dve.tensor_tensor(xlo[:, k, :], tmp[4 + k % 2][:, :T], xhi[:, k, :].bitcast(F32),
                                  ALU.subtract).then_inc(xlo_ready, 1)

            def shifted(k):
                link(dve, dve.scalar_tensor_tensor(out=hc[:, k, :], in0=x[:, k, :], scalar=vec[:, k, V_MIX:V_MIX + 1],
                                                   in1=rstd[:], op0=ALU.mult, op1=ALU.mult))
                link(dve, dve.tensor_tensor(xx[:, k, 1:], hc[:, k, :T - 1], hc[:, k, 1:], ALU.subtract))
                dve.tensor_scalar(xx[:, k, 0:1], hc[:, k, 0:1], -1.0, None, ALU.mult)
                link(dve, dve.tensor_tensor(xx[:, k, seqs], shin[:, SEQS * k:SEQS * k + SEQS], hc[:, k, seqs],
                                            ALU.subtract))

            def mix_version(ver):
                mixed(ver, 0)
                for k in range(KT):
                    if k + 1 < KT:
                        mixed(ver, k + 1)
                    low(ver, k)

            def kk(p):
                dve.wait_ge(mix_evac, p // 2 + 1)
                link(dve, dve.memset(bk[:, p, 0, 1, 0:PAD], 0.0))
                dve.tensor_scalar(ar[:, p, 0, :].rearrange("p (c t) -> p c t", t=C), bk[:, p, :, 1, :],
                                  vec[:, p, V_KK:V_KK + 1], None, ALU.mult).then_inc(kk_ready, 1)

            def lora_low(n, k):
                dve.wait_ge(lora_hi, n + 1)
                dve.tensor_tensor(tlo[:, k, :], tmp[n][:, :T], thi[:, k, :].bitcast(F32), ALU.subtract).then_inc(lora_lo, 1)

            def r_decayed(p):
                g = R_GROUP + p // 2
                dve.wait_ge(mix_out, g + 1)
                dve.wait_ge(r_decay, p + 1)
                dve.tensor_tensor(ar[:, p, 1, PAD:], PS[:, 2 * (g % 2) + p % 2, :T], tmp[p % 2][:, RD],
                                  ALU.mult).then_inc(r_scaled, 1)

            for k in range(KT):
                shifted(k)
                mixed(XK, k)
                if k:
                    low(XK, k - 1)
            low(XK, KT - 1)
            dve.tensor_copy(shst[:, :, 0:1], hc[:, :, TP - 1:TP])
            dve.tensor_copy(shst[:, :, 1:], hc[:, :, TP + STEPS - 1::STEPS]).then_inc(shift_ready, 1)
            dve.memset(ar[:, :, 1, 0:PAD], 0.0)
            for t in tmp[6:]:
                dve.memset(t[:, 0:PAD], 0.0)
            link(dve, dve.tensor_scalar(vec[:, :, V_OMKA:V_OMKA + 1], vec[:, :, V_KA:V_KA + 1], -1.0, 1.0,
                                        ALU.mult, ALU.add))
            for s in range(3):
                split(2 + s)
                kk(2 * s)
                kk(2 * s + 1)
            mix_version(XW)
            split(5)
            kk(PAIRS - 2)
            kk(PAIRS - 1)
            mix_version(XA)
            lora_low(0, 0)
            mixed(XG, 0)
            for k in range(KT):
                if k + 1 < KT:
                    mixed(XG, k + 1)
                low(XG, k)
                if k == 4:
                    lora_low(1, 1)
            dve.wait_ge(kk_ss, PAIRS)
            dve.tensor_scalar(tmp[3][0:HEADS, :T], PS[0:HEADS, 6, :T], 1e-24, None, ALU.max).then_inc(kk_max, 1)
            split(6)
            dve.wait_ge(kk_root, 1)
            dve.reciprocal(rstd[0:HEADS, :], tmp[3][0:HEADS, :T]).then_inc(kk_inv, 1)
            split(7)
            mix_version(XR)
            split(8)
            lora_low(2, 0)
            lora_low(3, 1)
            dve.wait_ge(mix_evac, 14)
            for p in range(PAIRS):
                pair_front(dve, p)
                if p:
                    pair_back(dve, p - 1)
                if p >= 3:
                    r_decayed(p - 3)
                if p in (3, 5, 7):
                    split(8 + p // 2)
            pair_back(dve, PAIRS - 1)
            r_decayed(PAIRS - 3)
            mix_version(XV)
            r_decayed(PAIRS - 2)
            r_decayed(PAIRS - 1)
            split(12)
            dve.memset(vy[:, :, 0:PAD], 0.0)
            for p in range(PAIRS):
                dve.wait_ge(bk_scaled, p + 1)
                if p >= 2:
                    dve.wait_ge(rk_sum, p - 1)
                else:
                    dve.wait_ge(r_scaled, PAIRS)
                dve.scalar_tensor_tensor(out=tmp[p % 2][:].rearrange("p (c t) -> p c t", t=C),
                                         in0=ar[:, p, 1, :].rearrange("p (c t) -> p c t", t=C),
                                         scalar=vec[:, p, V_RK:V_RK + 1], in1=bk[:, p, :, 1, :],
                                         op0=ALU.mult, op1=ALU.mult).then_inc(rk_ready, 1)
                dve.wait_ge(z_done, p + 1)
                if p == 0:
                    dve.wait_ge(ends_ready, 2)
                for i, (c0, c1) in enumerate(((0, 8), (8, CHUNKS))):
                    n = (c1 - c0) * 2 * C
                    dve.tensor_tensor(z[:, p, c0:c1, :].rearrange("p c t -> p (c t)"), PS[:, 4 + 2 * (p % 2) + i, :n],
                                      con[:, K_ZMASK + c0 * 2 * C:K_ZMASK + c1 * 2 * C], ALU.mult).then_inc(z_ready, 1)
            dve.wait_ge(g_loaded, 64)
            inverse(dve, 0, P, inv_dve, split)
            split(17)
            chain_dve(dve)
            for p in range(PAIRS):
                dve.wait_ge(mean_done, p + 1)
                dve.scalar_tensor_tensor(out=yb[:, p, 14:], in0=PS[:, p % 2, :NY], scalar=-1.0 / HD, in1=yb[:, p, 14:],
                                         op0=ALU.mult, op1=ALU.add).then_inc(yc_ready, 1)
                dve.wait_ge(rk_spread, p + 1)
                dve.tensor_tensor(vy[:, p, YC:], PS[:, 2 + p % 2, :NY], vy[:, p, YC:], ALU.mult).then_inc(bonus_ready, 1)
            dve.wait_ge(gn_root, 1)
            dve.reciprocal(rstd[0:HEADS, :NY], ms[0:HEADS, :NY]).then_inc(gn_inv, 1)
            dve.wait_ge(seq_stored, 16 * SEQS)
            for p in range(PAIRS):
                t = tmp[4 + p % 2][:, :NY]
                dve.wait_ge(gn_spread, p + 1)
                dve.wait_ge(yc_ready, PAIRS)
                dve.wait_ge(bonus_ready, PAIRS)
                dve.tensor_tensor(t, PS[:, 4 + p % 2, :NY], yb[:, p, 14:], ALU.mult).then_inc(gn_used, 1)
                dve.wait_ge(gn_used, p + 1)
                link(dve, dve.scalar_tensor_tensor(out=t, in0=t, scalar=vec[:, p, V_LNW:V_LNW + 1], in1=vy[:, p, YC:],
                                                   op0=ALU.mult, op1=ALU.add))
                dve.scalar_tensor_tensor(out=t, in0=t, scalar=vec[:, p, V_LNB:V_LNB + 1], in1=gate[:, p, 14:],
                                         op0=ALU.add, op1=ALU.mult).then_inc(o_ready, 1)
                dve.wait_ge(ohi_ready, p + 1)
                dve.tensor_tensor(olo[:, p, :NY], t, ohi[:, p, :NY].bitcast(F32), ALU.subtract).then_inc(olo_ready, 1)
            project_dve(dve, "wo", 2)

        def pair_front(dve, p):
            a = ar[:, p, 0, :].rearrange("p (c t) -> p c t", t=C)
            factor = tmp[6 + p % 2][:].rearrange("p (c t) -> p c t", t=C)
            b, k = bk[:, p, :, 0, :], bk[:, p, :, 1, :]
            if p >= 2:
                dve.wait_ge(bk_scaled, p - 1)
            dve.tensor_scalar(factor, b, vec[:, p, V_KA:V_KA + 1], vec[:, p, V_OMKA:V_OMKA + 1],
                              ALU.mult, ALU.add)
            link(dve, dve.tensor_tensor_scan(sw[:, p, PAD:], con[:, K_SCAN + PAD:K_SCAN + TS], sw[:, p, PAD:], 0.0,
                                             ALU.mult, ALU.add))
            dve.wait_ge(kk_spread, p + 1)
            dve.tensor_tensor(ar[:, p, 0, PAD:], PS[:, 4 + p % 2, :T], ar[:, p, 0, PAD:], ALU.mult).then_inc(a_normed, 1)
            dve.tensor_tensor(k, k, factor, ALU.mult).then_inc(logs_ready, 1)
            dve.wait_ge(a_normed, p + 1)
            dve.scalar_tensor_tensor(out=b, in0=a, scalar=-1.0, in1=b, op0=ALU.mult, op1=ALU.mult).then_inc(b_ready, 1)

        def pair_back(dve, p):
            dve.wait_ge(decays, 2 * p + 1)
            dve.wait_ge(b_ready, p + 1)
            for a0, n, size in ((PAD, 1, C - PAD), (C, PCHUNKS - 1, C), (PCHUNKS * C, SEQS, STEPS)):
                e = tmp[2 + p % 2][:, a0:a0 + n * size].rearrange("p (n s) -> p n s", s=size)
                a = ar[:, p, 0, a0:a0 + n * size].rearrange("p (n s) -> p n s", s=size)
                last = dve.tensor_tensor(a[:, :, 1:], a[:, :, 1:], e[:, :, :size - 1], ALU.mult)
            last.then_inc(a_scaled, 1)

        b_ready = sem("b_ready")

        def chain_dve(dve):
            def even(done, dst, bank, out_sem, c, g):
                dve.wait_ge(done, 2 * c + g + 1)
                dve.tensor_copy(dst[0:C, 4 * g:4 * g + 4, :],
                                PS[0:C, bank + g, 0:256].rearrange("p (a b) -> p a b", b=HD)).then_inc(out_sem, 1)

            dve.wait_ge(inv_stored, 32)
            dve.memset(st[0][:], 0.0).then_inc(st_ready, 1)
            for c in range(CHUNKS):
                if c >= PCHUNKS:
                    n = c - PCHUNKS
                    seq = con[:, K_SEQCOL:K_SEQCOL + SPC * C].rearrange("p (q t) -> p q t", t=C)
                    if n:
                        dve.wait_ge(x_done, 2 * c)
                    for q in range(SPC):
                        last = dve.tensor_tensor(arm[:, q], ar[:, :, 0, c * C:c * C + C],
                                                 seq[:, q:q + 1, :].to_broadcast([P, PAIRS, C]), ALU.mult)
                    last.then_inc(arm_ready, 1)
                for g in range(2):
                    if c >= 1:
                        dve.wait_ge(u_done, 2 * (c - 1) + g + 1)
                    even(x_done, xs, 0, xs_dve, c, g)
                for g in range(2):
                    even(u_done, uv[c % 2], 2, uv_dve, c, g)
                if c < PCHUNKS:
                    for g in range(2):
                        dve.wait_ge(s_done, 2 * c + g + 1)
                        if c >= 1:
                            dve.wait_ge(y_done, c)
                        ps = slice(4 * g, 4 * g + 4)
                        link(dve, dve.tensor_tensor(sd[:, ps, :], st[c % 2][:, ps, :],
                                                    PS[:, 4 + g, 0:256].rearrange("p (a b) -> p a b", b=HD), ALU.add))
                        dve.tensor_tensor(st[(c + 1) % 2][:, ps, :], sd[:, ps, :],
                                          dend[:, ps, c:c + 1].to_broadcast([P, 4, HD]), ALU.mult).then_inc(st_ready, 1)
                    continue
                if c == PCHUNKS:
                    dve.wait_ge(final_stored, 16)
                    dve.wait_ge(y_done, c)
                for q in range(SPC):
                    k = SPC * (c - PCHUNKS) + q
                    if k >= 2:
                        dve.wait_ge(q_done, k - 1)
                    dve.tensor_scalar(st[q % 2][:], kv[c % 2][:], con[:, K_SEQROW + q:K_SEQROW + q + 1], None,
                                      ALU.mult).then_inc(kvm_ready, 1)
                    if q >= 1:
                        new_state(dve, c, q - 1)
                new_state(dve, c, SPC - 1)

        def new_state(dve, c, q):
            k = SPC * (c - PCHUNKS) + q
            dve.wait_ge(y_done, c + 1)
            dve.wait_ge(q_done, k + 1)
            link(dve, dve.tensor_tensor(s0[:, q], s0[:, q], PS[:, 4 + q % 2, :].rearrange("p (a b) -> p a b", b=HD),
                                        ALU.add))
            dve.tensor_tensor(s0[:, q], s0[:, q], dend[:, :, PCHUNKS + k:PCHUNKS + k + 1].to_broadcast([P, PAIRS, HD]),
                              ALU.mult).then_inc(seq_ready, 1)

        @block.sync
        def _(sp):
            sp.dma_start(x[:], x_dram).then_inc(loaded, 16)
            sp.dma_start(vec[:], vec_dram).then_inc(loaded, 16)
            sp.dma_start(con[:], const_dram).then_inc(loaded, 16)
            sp.dma_start(cin[:], conv_dram).then_inc(loaded, 16)
            sp.dma_start(shin[:], shift_dram).then_inc(loaded, 16)
            load_phase(sp, "gu0")
            load_phase(sp, "down0")
            mix_sp(sp)
            for name in order[4:]:
                load_phase(sp, name)
            sp.wait_ge(conv_u, 1)
            sp.dma_start(convo_out, stage[:]).then_inc(stored, 16)
            for k in range(KT):
                sp.wait_ge(y_ready, k + 1)
                sp.dma_start(y_out[k], cv[:, k, :]).then_inc(stored, 16)
            sp.wait_ge(stored, 16 * (KT + 1 + MIX_STORES))

        @block.gpsimd
        def _(pool):
            for par in range(2):
                split_pool(pool, 0, par, BIG)
            for name in order:
                if name == "mix":
                    mix_pool(pool)
                else:
                    split_phase_pool(pool, name)

        @block.scalar
        def _(act):
            for par in range(2):
                split_act(act, 0, par, BIG, slot_used, 2)
            for m in range(KT):
                res_act(act, 0, m, m % 2, m >= 2)
            ffn_act(act, 0)
            mix_act(act)
            ffn_act(act, 1)
            ffn_act(act, 2)
            conv_act(act)
            ffn_act(act, 3)
            norm_act(act, 6, TN)

        @block.vector
        def _(dve):
            dve.memset(tmp[7][:, 0:1], 0.0).then_inc(slot_used, 2)
            dve.memset(tmp[7][:, 1:2], 0.0).then_inc(scaled, 2)
            dve.memset(tmp[7][:, 2:3], 0.0).then_inc(lo_pool, 2)
            dve.memset(tmp[7][:, 3:4], 0.0).then_inc(lo_dve, 2)
            dve.wait_ge(loaded, 16 * LOADS)
            dve.memset(tmp[7][:, 4:5], 0.0).then_inc(x_new, 8)
            dve.wait_ge(x_new, 8)
            for par in range(2):
                split_dve(dve, 0, par, BIG)
            for m in range(KT):
                res_dve(dve, 0, m, m % 2, None, None, None)
                res_dve_after(dve, 0, m, m % 2, m == 0)
            ffn_dve(dve, 0)
            mix_dve(dve)
            ffn_dve(dve, 1)
            ffn_dve(dve, 2)
            conv_dve(dve)
            ffn_dve(dve, 3)
            final_dve(dve)

        @block.tensor
        def _(pe):
            pe.wait_ge(loaded, 16 * LOADS)
            ffn_pe(pe, 0)
            mix_pe(pe)
            ffn_pe(pe, 1)
            ffn_pe(pe, 2)
            conv_pe(pe)
            ffn_pe(pe, 3)
            final_pe(pe)


def _slots(w, pairs):
    import numpy as np
    w = np.asarray(w).reshape(KT, P, -1, P)
    return np.stack([np.stack([w[:, :, m] for m in pair], 2).transpose(1, 0, 2, 3).reshape(P, -1) for pair in pairs])


def _constants():
    import numpy as np
    c = np.zeros((P, NCONST), np.float32)
    head = np.arange(P) // HD
    c[:, K_ONES:K_ONES + P] = 1.0
    c[:, K_BLOCK:K_BLOCK + P] = head[:, None] == head[None, :]
    c[:, K_EYE:K_EYE + HD] = (np.arange(P) % HD)[:, None] == np.arange(HD)[None, :]
    for p in range(PAIRS):
        c[:, K_SEL + 16 * p:K_SEL + 16 * p + 16] = (2 * p + head)[:, None] == np.arange(16)[None, :]
        c[:HEADS, K_SELT + P * p:K_SELT + P * p + P] = np.arange(HEADS)[:, None] == (2 * p + head)[None, :]
    col = np.arange(TS)
    starts = (col % C == 0) | ((col >= PCHUNKS * C) & (col % STEPS == 0))
    c[:, K_SCAN:K_SCAN + TS] = ~starts
    s, t = (np.arange(P) % C)[:, None], np.arange(C)[None, :]
    z = c[:, K_ZMASK:K_ZMASK + CHUNKS * 2 * C].reshape(P, CHUNKS, 2, C)
    for n in range(CHUNKS):
        same = (s // STEPS == t // STEPS) | (n < PCHUNKS)
        z[:, n, 0] = (s < t) & same
        z[:, n, 1] = (s <= t) & same
    c[:, K_SEQCOL:K_SEQCOL + SPC * C] = (np.arange(C)[None, :] // STEPS == np.arange(SPC)[:, None]).reshape(1, -1)
    c[:, K_SEQROW:K_SEQROW + SPC] = s // STEPS == np.arange(SPC)[None, :]
    return c


_INPUTS = ("x", "vec", "const", "shift", "conv", "wkv", "gu", "down", "mix", "wo", "scin", "scout", "eye")
_OUTPUTS = {"y": (KT, P, SEQ + SEQS * STEPS), "wkvp": (P, PAIRS * HD), "wkvs": (SEQS, P, PAIRS * HD),
            "shifto": (P, KT * (1 + SEQS)), "convo": (P, KT * (2 + 2 * SEQS))}


def kernel(**a):
    import numpy as np
    import concourse.bacc as bacc
    from concourse.bass_utils import run_bass_kernel_spmd

    a = {k: np.asarray(v) for k, v in a.items()}
    f32 = np.float32

    def tiles(v):
        return v.reshape(-1, KT, P).transpose(2, 1, 0)

    tokens = np.concatenate([a["meta"], a["x_prompt"][0], a["x_sample"].reshape(SEQS * STEPS, D)], 0)
    vectors = np.concatenate([
        a["ffn_norm"].reshape(4, D), a["mix_norm"], a["final_norm"][None], a["rk_mu"][0], a["rk_w0"], a["rk_a0"],
        a["rk_k_k"], a["rk_k_a"], a["rk_r_k"].reshape(1, D), a["rk_ln_w"], a["rk_ln_b"], a["sc_conv_w"][0],
        np.zeros((1, D), f32)], 0)
    gu = a["ffn_w_gu"].reshape(4, D, 2 * FF)
    down = a["ffn_w_down"].reshape(4, 2, SMALL, P, KT, P).transpose(0, 4, 1, 3, 2, 5)
    g1, g2 = a["rk_g1"][0], a["rk_g2"][0]
    gz = np.zeros((D, 2 * P - g1.shape[1]), f32)
    g1 = np.concatenate([g1[:, :P], gz, g1[:, P:]], 1)
    g2 = np.concatenate([g2[:P], np.concatenate([np.zeros((2 * P - g2.shape[0], D), f32), g2[P:]], 0)], 1)

    def lora(w_in, w_out):
        w_in = np.concatenate([w_in, np.zeros((D, P - w_in.shape[1]), f32)], 1)
        w_out = np.concatenate([w_out, np.zeros((P - w_out.shape[0], D), f32)], 0)
        return np.concatenate([w_in.reshape(KT, P, P).transpose(1, 0, 2).reshape(P, -1), w_out], 1)[None]

    straight = [(2 * s, 2 * s + 1) for s in range(4)]
    r, k, v = (_slots(a["rk_w_rkv"][0, i], straight) for i in range(3))
    mix = np.concatenate([k, lora(a["rk_w1"][0], a["rk_w2"][0]), lora(a["rk_a1"][0], a["rk_a2"][0]),
                          _slots(g1, [(0, 1)]), r, v, g2[None]], 0)
    arrays = {
        "x": tiles(tokens),
        "vec": tiles(vectors),
        "const": _constants(),
        "shift": tiles(a["state_shift"][0]).reshape(P, -1),
        "conv": tiles(a["state_conv"][0].reshape(2 * SEQS, D)).reshape(P, -1),
        "wkv": a["state_wkv"][0].reshape(SEQS, PAIRS, 2, HD, HD).transpose(0, 2, 4, 1, 3).reshape(SEQS, P, -1),
        "gu": np.stack([_slots(gu[f], [(s, FT + s) for s in range(FT)]) for f in range(4)]),
        "down": down.reshape(4, 2 * KT, P, SMALL * P),
        "mix": mix,
        "wo": _slots(a["rk_w_o"][0], straight),
        "scin": _slots(a["sc_w_in"][0], [(KT + s, 2 * KT + s) for s in range(KT)] + straight),
        "scout": _slots(a["sc_w_out"][0], straight),
        "eye": np.broadcast_to(np.eye(C, dtype=f32).reshape(1, -1), (P, C * C)),
    }
    nc = bacc.Bacc("TRN2", target_bir_lowering=False, num_devices=1)
    arrays = {n: np.ascontiguousarray(arrays[n], dtype=f32) for n in _INPUTS}
    aps = [nc.dram_tensor(f"in_{n}", arrays[n].shape, F32, kind="ExternalInput").ap() for n in _INPUTS]
    outs = [nc.dram_tensor(f"out_{n}", s, F32, kind="ExternalOutput").ap() for n, s in _OUTPUTS.items()]
    scratch = [nc.dram_tensor(n, (CHUNKS, HEADS, C, C), F32).ap() for n in ("couplings", "inverses")]
    build_program(nc, *aps, *outs, *scratch)
    got = run_bass_kernel_spmd(nc, [{f"in_{n}": v for n, v in arrays.items()}], core_ids=[0]).results[0]
    y, wkvp, wkvs, shifto, convo = (got[f"out_{n}"] for n in _OUTPUTS)
    y = y.reshape(D, -1).T
    shifto = shifto.reshape(P, KT, -1).transpose(2, 1, 0).reshape(-1, D)
    convo = convo.reshape(P, KT, -1).transpose(2, 1, 0).reshape(-1, D)

    def states(s):
        return s.reshape(-1, 2, HD, PAIRS, HD).transpose(0, 3, 1, 4, 2).reshape(1, -1, HEADS, HD, HD)

    return (y[:SEQ].reshape(1, SEQ, D), y[SEQ:].reshape(SEQS, STEPS, D), states(wkvp), shifto[None, :1],
            convo[None, None, :2], states(wkvs), shifto[None, 1:], convo[2:].reshape(1, SEQS, 2, D))
```

```python
from contextlib import ExitStack

import concourse.bass as bass
from concourse import mybir

ALU = mybir.AluOpType
ACT = mybir.ActivationFunctionType
AX_X = mybir.AxisListType.X
F32 = mybir.dt.float32
F32R = mybir.dt.float32r

P = 128
D = 1024
KT = D // P
FF = 2816
FT = FF // P
META, SEQ, SEQS, STEPS = 16, 256, 8, 8
TP = META + SEQ
T = TP + SEQS * STEPS
HEADS, HD = 16, 64
PAIRS = HEADS // 2
C = 32
PAD = C - TP % C
TS = PAD + T
CHUNKS = TS // C
PCHUNKS = (PAD + TP) // C
SCH = CHUNKS - PCHUNKS
SPC = C // STEPS
EPS = 1e-6
GN_EPS = 64e-5
E_HALF = 0.6065306597126334
BIG, SMALL = 16, FT // 2
POOL_TILES = {BIG: 10, SMALL: 7}

V_NORM = 0
V_MIX = 4
V_FINAL = 6
V_MU = 7
V_W0, V_A0, V_KK, V_KA, V_RK, V_LNW, V_LNB = range(13, 20)
V_CONV = 20
V_OMKA = 23
NVEC = 24

K_ONES = 0
K_BLOCK = 128
K_EYE = 256
K_SEL = 320
K_SCAN = K_SEL + 16 * PAIRS
K_ZMASK = K_SCAN + TS
K_SEQCOL = K_ZMASK + CHUNKS * 2 * C
K_SEQROW = K_SEQCOL + SPC * C
K_SELT = K_SEQROW + SPC
NCONST = K_SELT + P * PAIRS


def build_program(nc, x_dram, vec_dram, const_dram, shift_dram, conv_dram, wkv_dram, gu_dram, down_dram,
                  mix_dram, wo_dram, scin_dram, scout_dram, blockeye_dram, y_out, wkvp_out, wkvs_out, shift_out,
                  convo_out, zt_dram, tt_dram):
    with ExitStack() as ctx:
        def sem(name):
            return ctx.enter_context(nc.semaphore(name))

        PS = ctx.enter_context(nc.psum_tensor("psum", [P, 8, 512], F32))

        top = [0]

        def at(name, shape, dt=F32, start=None):
            size = 4
            for n in shape[1:]:
                size *= n
            start = -(-top[0] // 32) * 32 if start is None else start
            t = nc.alloc_sbuf_tensor_at(name, shape, dt, offset=base + start)
            if start + size > top[0]:
                top[0] = start + size
            return t

        base = -(-nc.sbuf_base // 32) * 32
        x = at("x", [P, KT, T])
        raw_start = -(-top[0] // 32) * 32
        raw = [at(f"w_raw{i}", [P, BIG * P]) for i in range(2)]
        whi = [at(f"w_hi{i}", [P, BIG * P], F32R) for i in range(2)]
        wlo = [at(f"w_lo{i}", [P, BIG * P], F32R) for i in range(2)]
        vec = at("vec", [P, KT, NVEC])
        con = at("con", [P, NCONST])
        cin = at("cin", [P, KT * 2 * SEQS])
        shin = at("shin", [P, KT * SEQS])
        stage = at("stage", [P, KT, 2 + 2 * SEQS])
        shst = at("shst", [P, KT, 1 + SEQS])
        e_start = -(-top[0] // 32) * 32
        tmp = [at(f"tmp{i}", [P, TS]) for i in range(8)]
        rstd = at("rstd", [P, T])
        acc_start = -(-top[0] // 32) * 32
        acc = at("acc", [P, T])
        ms = at("ms", [P, T])
        x_start = -(-top[0] // 32) * 32
        xhi = at("x_hi", [P, KT, T], F32R)
        xlo = at("x_lo", [P, KT, T], F32R)
        a_start = -(-top[0] // 32) * 32
        hhi = at("h_hi", [P, FT, T], F32R)
        hlo = at("h_lo", [P, FT, T], F32R)
        vy = at("vy", [P, PAIRS, TS], start=a_start)
        xx = at("xx", [P, KT, T], start=a_start)
        iv = a_start + 4 * PAIRS * TS
        gate = at("gate", [P, KT, T], start=iv)
        yb = at("yb", [P, KT, T], start=iv + 4 * KT * T)
        o1 = iv + 8 * KT * T
        ar = at("ar", [P, PAIRS, 2, TS], start=o1)
        o2 = o1 + 8 * PAIRS * TS
        bk = at("bk", [P, PAIRS, CHUNKS, 2, C], start=o2)
        o3 = o2 + 8 * PAIRS * TS
        hc = at("hc", [P, KT, T], start=o3)
        sw = at("sw", [P, PAIRS, TS], start=o3 + 4 * PAIRS * TS)
        z = at("z", [P, PAIRS, CHUNKS, 2 * C], start=o3)
        o4 = o3 + 8 * PAIRS * TS
        dend = at("dend", [P, PAIRS, PCHUNKS + SEQS], start=o4)
        rks = at("rks", [HEADS, T], start=o4 + 4 * PAIRS * (PCHUNKS + SEQS))
        ohi = at("o_hi", [P, KT, T], F32R, start=o1)
        olo = at("o_lo", [P, KT, T], F32R, start=o1 + 4 * KT * T)
        blk = 9 * C * C
        ivs = (iv, iv + 8 * KT * T - blk)
        gt = [at(f"gt{i}", [P, C * C], start=ivs[i]) for i in range(2)]
        wt = [at(f"wt{i}", [P, C * C], start=ivs[i] + 4 * C * C) for i in range(2)]
        outer = [at(f"outer{i}", [P, C * C // 4], start=ivs[i] + 8 * C * C) for i in range(2)]
        thi = at("t_hi", [P, 2, T], F32R, start=acc_start)
        tlo = at("t_lo", [P, 2, T], F32R, start=iv + blk)
        assert blk <= 4 * KT * T and 2 * blk + 8 * T <= 8 * KT * T
        q = x_start
        uv = [at(f"uv{i}", [P, PAIRS, HD], start=q + i * 2048) for i in range(2)]
        kv = [at(f"kv{i}", [P, PAIRS, HD], start=q + 4096 + i * 2048) for i in range(2)]
        st = [at(f"st{i}", [P, PAIRS, HD], start=q + 8192 + i * 2048) for i in range(2)]
        xs = at("xs", [P, PAIRS, HD], start=q + 12288)
        sd = at("sd", [P, PAIRS, HD], start=q + 14336)
        y0 = at("y0", [P, PAIRS, C], start=q + 20480)
        arm = at("arm", [P, SPC, PAIRS, C], start=q + 16384)
        assert q + 21504 <= a_start
        s0s = [at(f"s0_{i}", [P, SPC, PAIRS, HD], start=(e_start, raw_start)[i]) for i in range(2)]
        ttc = [at(f"ttc{i}", [P, PAIRS, C], start=e_start + 8192 + i * 1024) for i in range(2)]
        rm = at("rm", [P, SPC, PAIRS, C], start=e_start + 10240)
        up = at("up", [P, KT, 2 + SEQ], start=o3)
        us = at("us", [P, KT, SEQS, 2 + STEPS], start=o3 + 4 * KT * (2 + SEQ))
        cv = at("cv", [P, KT, SEQ + SEQS * STEPS], start=a_start)
        assert base + top[0] <= nc.sbuf_usable_end, (base + top[0], nc.sbuf_usable_end)

        loaded = sem("loaded")
        con_loaded = sem("con_loaded")
        raw_full = [sem(f"raw_full{i}") for i in range(2)]
        hi_ready = sem("hi_ready")
        lo_pool = sem("lo_pool")
        lo_dve = sem("lo_dve")
        slot_used = sem("slot_used")
        scaled = sem("scaled")
        gate_scaled = sem("gate_scaled")
        act_ready = sem("act_ready")
        h_ready = sem("h_ready")
        hhi_ready = sem("hhi_ready")
        hlo_ready = sem("hlo_ready")
        x_new = sem("x_new")
        sq_ready = sem("sq_ready")
        acc_done = sem("acc_done")
        xg_ready = sem("xg_ready")
        xhi_ready = sem("xhi_ready")
        xlo_ready = sem("xlo_ready")
        ss_done = sem("ss_done")
        root_ready = sem("root_ready")
        rstd_ready = sem("rstd_ready")
        stored = sem("stored")

        block = ctx.enter_context(nc.Block())

        stream = {}
        first = 0
        for name, dram, slots, tiles in (
                ("gu0", gu_dram[0], FT, BIG), ("down0", down_dram[0], 2 * KT, SMALL),
                ("mix", mix_dram, 16, BIG), ("wo", wo_dram, 4, BIG),
                ("gu1", gu_dram[1], FT, BIG), ("down1", down_dram[1], 2 * KT, SMALL),
                ("gu2", gu_dram[2], FT, BIG), ("down2", down_dram[2], 2 * KT, SMALL),
                ("scin", scin_dram, 12, BIG), ("scout", scout_dram, 4, BIG),
                ("gu3", gu_dram[3], FT, BIG), ("down3", down_dram[3], 2 * KT, SMALL)):
            stream[name] = (first, slots, tiles, dram)
            first += slots
        order = list(stream)
        MIXB = stream["mix"][0]

        def next_tiles(name):
            i = order.index(name) + 1
            return stream[order[i]][2] if i < len(order) else 0

        def used_base(name):
            n = stream[name][0]
            return n + 2 - (16 if n > MIXB else 0)

        FFN = {0: dict(q=1, ver=0, c0=0, n=T, scaled=0), 1: dict(q=3, ver=7, c0=14, n=T - 14, scaled=FT),
               2: dict(q=4, ver=8, c0=14, n=T - 14, scaled=2 * FT),
               3: dict(q=6, ver=10, c0=16, n=T - 16, scaled=3 * FT + 12)}
        CONV = dict(q=5, ver=9, c0=14, n=T - 14, scaled=3 * FT)
        SPLITS = {0: (0, V_NORM + 0, 0), 2: (7, V_NORM + 1, 14), 3: (8, V_NORM + 2, 14),
                  4: (9, V_MIX + 1, 14), 5: (10, V_NORM + 3, 16)}
        RCOL = {1: 0, 2: 14, 3: 14, 4: 14, 5: 16, 6: 16}

        def passes(w_hi, w_lo, x_hi, x_lo):
            return ((w_hi, x_hi), (w_hi, x_lo), (w_lo, x_hi))

        def split_act(act, half, par, tiles, free_sem, free_value):
            act.wait_ge(raw_full[par], 16 * half + 16)
            act.wait_ge(free_sem, free_value)
            act.activation(whi[par][:, :tiles * P], raw[par][:, :tiles * P], ACT.Copy).then_inc(hi_ready, 1)

        def split_pool(pool, half, par, tiles, share=None):
            n = (share or POOL_TILES[tiles]) * P
            pool.wait_ge(hi_ready, 2 * half + par + 1)
            pool.tensor_tensor(wlo[par][:, :n], raw[par][:, :n], whi[par][:, :n].bitcast(F32),
                               ALU.subtract).then_inc(lo_pool, 1)

        def split_dve(dve, half, par, tiles, share=None):
            a, b = (share or POOL_TILES[tiles]) * P, tiles * P
            dve.wait_ge(hi_ready, 2 * half + par + 1)
            dve.tensor_tensor(wlo[par][:, a:b], raw[par][:, a:b], whi[par][:, a:b].bitcast(F32),
                              ALU.subtract).then_inc(lo_dve, 1)

        def pe_slot_wait(pe, n):
            pe.wait_ge(lo_pool, n + 3)
            pe.wait_ge(lo_dve, n + 3)

        def load_phase(sp, name, lo=0, hi=None):
            first, slots, tiles, dram = stream[name]
            with sp.Fori(lo // 2, (slots if hi is None else hi) // 2) as i:
                for par in range(2):
                    n = first + 2 * i + par
                    sp.wait_ge(lo_pool, n + 1)
                    sp.wait_ge(lo_dve, n + 1)
                    sp.dma_start(raw[par][:, :tiles * P], dram[2 * i + par]).then_inc(raw_full[par], 16)

        def load_slot(sp, name, k):
            first, _, tiles, dram = stream[name]
            n = first + k
            sp.wait_ge(lo_pool, n + 1)
            sp.wait_ge(lo_dve, n + 1)
            sp.dma_start(raw[n % 2][:, :tiles * P], dram[k]).then_inc(raw_full[n % 2], 16)

        def res_dve(dve, q, m, par, alpha, ps, ready, split=True):
            if q:
                c = RCOL[q]
                dve.wait_ge(slot_used, ready)
                dve.scalar_tensor_tensor(out=x[:, m, c:], in0=ps[:, :T - c], scalar=alpha, in1=x[:, m, c:],
                                         op0=ALU.mult, op1=ALU.add).then_inc(x_new, 1)
            if q in SPLITS:
                ver, g, c = SPLITS[q]
                dve.wait_ge(x_new, 8 * q + m + 1 if q else 8)
                dve.tensor_scalar(tmp[4 + par][:, :T - c], x[:, m, c:], vec[:, m, g:g + 1], None,
                                  ALU.mult).then_inc(xg_ready, 1)

        def res_dve_after(dve, q, m, par, first):
            c = SPLITS[q][2] if q in SPLITS else RCOL[q]
            dve.wait_ge(sq_ready, 8 * q + m + 1)
            if first:
                dve.tensor_copy(acc[:, :T - c], tmp[6 + par][:, :T - c]).then_inc(acc_done, 1)
            else:
                dve.wait_ge(acc_done, 8 * q + m)
                dve.tensor_tensor(acc[:, :T - c], acc[:, :T - c], tmp[6 + par][:, :T - c],
                                  ALU.add).then_inc(acc_done, 1)
            if q in SPLITS:
                ver, g, c = SPLITS[q]
                dve.wait_ge(xhi_ready, 8 * ver + m + 1)
                dve.tensor_tensor(xlo[:, m, :T - c], tmp[4 + par][:, :T - c],
                                  xhi[:, m, :T - c].bitcast(F32), ALU.subtract).then_inc(xlo_ready, 1)

        def res_act(act, q, m, par, m_is_two_on=True):
            c = SPLITS[q][2] if q in SPLITS else RCOL[q]
            act.wait_ge(x_new, 8 * q + m + 1 if q else 8)
            if m_is_two_on:
                act.wait_ge(acc_done, 8 * q + m - 1)
            act.activation(tmp[6 + par][:, :T - c], x[:, m, c:], ACT.Square).then_inc(sq_ready, 1)
            if q in SPLITS:
                ver = SPLITS[q][0]
                act.wait_ge(xg_ready, 8 * ver + m + 1)
                act.activation(xhi[:, m, :T - c], tmp[4 + par][:, :T - c], ACT.Copy).then_inc(xhi_ready, 1)

        def norm_pe(pe, q, norm, n):
            pe.wait_ge(acc_done, 8 * q + 8)
            pe.matmul(PS[:, 6, :n], con[:, K_ONES:K_ONES + P], acc[:, :n], start=True, stop=True).then_inc(ss_done, 1)

        def norm_act(act, norm, n):
            act.wait_ge(ss_done, norm + 1)
            act.activation(ms[:, :n], PS[:, 6, :n], ACT.Sqrt, bias=EPS, scale=1.0 / D).then_inc(root_ready, 1)

        def norm_dve(dve, norm, n):
            dve.wait_ge(root_ready, norm + 1)
            dve.reciprocal(rstd[:, :n], ms[:, :n]).then_inc(rstd_ready, 1)
            dve.wait_ge(rstd_ready, norm + 1)

        def pe_pair(pe, par, banks, ver, n, out_sem, src=None, fresh=False):
            xh, xl = src or (xhi, xlo)
            for k in range(KT):
                if fresh:
                    pe.wait_ge(xlo_ready, 8 * ver + k + 1)
                for j in range(2):
                    for i, (w, v) in enumerate(passes(whi[par], wlo[par], xh, xl)):
                        last = pe.matmul(PS[:, banks[j], :n], w[:, (2 * k + j) * P:(2 * k + j + 1) * P], v[:, k, :n],
                                         start=(k == 0 and i == 0), stop=(k == KT - 1 and i == 2))
            last.then_inc(out_sem, 1)

        def ffn_pe(pe, f):
            d = FFN[f]
            gu, down, n = stream[f"gu{f}"][0], stream[f"down{f}"][0], d["n"]

            def gu_slot(i, par, fresh=False):
                pe_slot_wait(pe, gu + 2 * i + par)
                pe.wait_ge(scaled, d["scaled"] + 2 * i + par + 1)
                pe_pair(pe, par, (2 * par, 2 * par + 1), d["ver"], n, slot_used, fresh=fresh)

            if f in (1, 3):
                pe.wait_ge(x_new, 8 * (2 if f == 1 else 5) + 6)
            gu_slot(0, 0, fresh=True)
            norm_pe(pe, {0: 0, 1: 2, 2: 3, 3: 5}[f], 0, n)
            gu_slot(0, 1)
            with pe.Fori(1, FT // 2) as i:
                for par in range(2):
                    gu_slot(i, par)

            def down_tile(m, par, first=False):
                pe.wait_ge(x_new, 8 * d["q"] + m - 1)
                for half in range(2):
                    pe_slot_wait(pe, down + 2 * m + half)
                    for k in range(SMALL):
                        kk = half * SMALL + k
                        if first and kk in (0, FT - 2, FT - 1):
                            pe.wait_ge(hlo_ready, FT * f + max(kk + 1, FT - 2))
                        for i, (w, v) in enumerate(passes(whi[half], wlo[half], hhi, hlo)):
                            last = pe.matmul(PS[:, 4 + par, :n], w[:, k * P:(k + 1) * P], v[:, kk, :n],
                                             start=(kk == 0 and i == 0), stop=(kk == FT - 1 and i == 2))
                    last.then_inc(slot_used, 1)

            down_tile(0, 0, first=True)
            down_tile(1, 1)
            with pe.Fori(1, KT // 2) as i:
                for par in range(2):
                    down_tile(2 * i + par, par)

        def ffn_act(act, f):
            d = FFN[f]
            n, gub, dnb = d["n"], used_base(f"gu{f}"), used_base(f"down{f}")
            gu, down = stream[f"gu{f}"][0], stream[f"down{f}"][0]

            def gu_slot(i, par, tiles, first=False):
                split_act(act, gu // 2 + i + 1, par, tiles, slot_used, gub + 2 * i + par + 1)
                if first:
                    norm_act(act, {0: 0, 1: 2, 2: 3, 3: 5}[f], n)
                s = 2 * i + par
                act.wait_ge(gate_scaled, FT * f + s + 1)
                act.activation(tmp[1][:, :n], tmp[0][:, :n], ACT.Silu).then_inc(act_ready, 1)
                act.wait_ge(h_ready, FT * f + s + 1)
                act.activation(hhi[:, bass.ds(s, 1), :n], tmp[3][:, :n], ACT.Copy).then_inc(hhi_ready, 1)

            gu_slot(0, 0, BIG, first=True)
            gu_slot(0, 1, BIG)
            with act.Fori(1, FT // 2 - 1) as i:
                for par in range(2):
                    gu_slot(i, par, BIG)
            for par in range(2):
                gu_slot(FT // 2 - 1, par, SMALL)

            def down_tile(m, par, tiles, first=False, last=False):
                split_act(act, down // 2 + m + 1, 0, tiles, slot_used, dnb + 2 * m + 1) if tiles else None
                if last:
                    res_act(act, d["q"], m, par)
                if tiles:
                    split_act(act, down // 2 + m + 1, 1, tiles, slot_used, dnb + 2 * m + 2)
                if not last:
                    res_act(act, d["q"], m, par, not first)

            down_tile(0, 0, SMALL, first=True)
            down_tile(1, 1, SMALL, first=True)
            with act.Fori(1, KT // 2 - 1) as i:
                for par in range(2):
                    down_tile(2 * i + par, par, SMALL)
            down_tile(KT - 2, 0, SMALL)
            down_tile(KT - 1, 1, next_tiles(f"down{f}"), last=True)

        def ffn_dve(dve, f):
            d = FFN[f]
            n, gub, dnb = d["n"], used_base(f"gu{f}"), used_base(f"down{f}")
            gu, down = stream[f"gu{f}"][0], stream[f"down{f}"][0]

            def gu_slot(i, par, tiles, first=False):
                s = 2 * i + par
                if first:
                    norm_dve(dve, {0: 0, 1: 2, 2: 3, 3: 5}[f], n)
                dve.wait_ge(slot_used, gub + s + 1)
                dve.tensor_tensor(tmp[0][:, :n], PS[:, 2 * par, :n], rstd[:, :n], ALU.mult).then_inc(gate_scaled, 1)
                dve.tensor_tensor(tmp[2][:, :n], PS[:, 2 * par + 1, :n], rstd[:, :n], ALU.mult).then_inc(scaled, 1)
                split_dve(dve, gu // 2 + i + 1, par, tiles)
                dve.wait_ge(act_ready, FT * f + s + 1)
                dve.wait_ge(scaled, d["scaled"] + s + 3)
                dve.tensor_tensor(tmp[3][:, :n], tmp[1][:, :n], tmp[2][:, :n], ALU.mult).then_inc(h_ready, 1)
                dve.wait_ge(hhi_ready, FT * f + s + 1)
                dve.tensor_tensor(hlo[:, bass.ds(s, 1), :n], tmp[3][:, :n], hhi[:, bass.ds(s, 1), :n].bitcast(F32),
                                  ALU.subtract).then_inc(hlo_ready, 1)

            gu_slot(0, 0, BIG, first=True)
            gu_slot(0, 1, BIG)
            with dve.Fori(1, FT // 2 - 1) as i:
                for par in range(2):
                    gu_slot(i, par, BIG)
            for par in range(2):
                gu_slot(FT // 2 - 1, par, SMALL)

            def down_tile(m, par, tiles, first=False, last=False):
                if tiles:
                    split_dve(dve, down // 2 + m + 1, 0, tiles)
                res_dve(dve, d["q"], m, par, 0.5, PS[:, 4 + par, :], dnb + 2 * m + 2)
                if tiles and not last:
                    split_dve(dve, down // 2 + m + 1, 1, tiles)
                res_dve_after(dve, d["q"], m, par, first)
                if tiles and last:
                    split_dve(dve, down // 2 + m + 1, 1, tiles)

            down_tile(0, 0, SMALL, first=True)
            down_tile(1, 1, SMALL)
            with dve.Fori(1, KT // 2 - 1) as i:
                for par in range(2):
                    down_tile(2 * i + par, par, SMALL)
            down_tile(KT - 2, 0, SMALL)
            down_tile(KT - 1, 1, next_tiles(f"down{f}"), last=True)

        def split_phase_pool(pool, name):
            first, slots, tiles, _ = stream[name]
            with pool.Fori(0, slots // 2 - 1) as i:
                for par in range(2):
                    split_pool(pool, first // 2 + i + 1, par, tiles)
            if next_tiles(name):
                for par in range(2):
                    split_pool(pool, first // 2 + slots // 2, par, next_tiles(name))

        conv_u = sem("conv_u")
        o_ready = sem("o_ready")
        ohi_ready = sem("ohi_ready")
        olo_ready = sem("olo_ready")
        dve_line = sem("dve_line")
        line = [0]
        PR = 2 + SEQ

        def link(dve, ins):
            line[0] += 1
            ins.then_inc(dve_line, 1)
            dve.wait_ge(dve_line, line[0])

        def conv_pe(pe):
            d = CONV
            first = stream["scin"][0]
            for s in range(12):
                pe_slot_wait(pe, first + s)
                pe.wait_ge(scaled, d["scaled"] + s + 1)
                pe_pair(pe, s % 2, (2 * (s % 2), 2 * (s % 2) + 1), d["ver"], d["n"], slot_used, fresh=(s == 0))
                if s == 0:
                    norm_pe(pe, 4, 4, d["n"])
            project_pe(pe, "scout", 5, PR - 2 + SEQS * STEPS, KT)

        def project_pe(pe, name, q, n, olo_base):
            first = stream[name][0]
            for s in range(4):
                pe_slot_wait(pe, first + s)
                pe.wait_ge(x_new, 8 * q + 2 * s - 2)
                if s == 0:
                    pe.wait_ge(scaled, SCALED_BEFORE[name])
                    if name == "wo":
                        pe.wait_ge(mix_evac, MIX_GROUPS - 4)
                banks = ((2 * s) % 4, (2 * s + 1) % 4)
                for k in range(KT):
                    if s == 0:
                        pe.wait_ge(olo_ready, olo_base + k + 1)
                    for j in range(2):
                        for i, (w, v) in enumerate(passes(whi[s % 2], wlo[s % 2], ohi, olo)):
                            last = pe.matmul(PS[:, banks[j], :n], w[:, (2 * k + j) * P:(2 * k + j + 1) * P], v[:, k, :n],
                                             start=(k == 0 and i == 0), stop=(k == KT - 1 and i == 2))
                last.then_inc(slot_used, 1)

        SCALED_BEFORE = {"wo": 2 + FT, "scout": 2 + 3 * FT + 12}

        def project_act(act, name, q):
            first, base_used, nxt = stream[name][0], used_base(name), next_tiles(name)
            for s in range(4):
                tiles = BIG if s < 2 else nxt
                if s < 3:
                    split_act(act, first // 2 + (s + 2) // 2, s % 2, tiles, slot_used, base_used + s + 1)
                for m in (2 * s, 2 * s + 1):
                    res_act(act, q, m, m % 2, m >= 2)
                if s == 3:
                    split_act(act, first // 2 + (s + 2) // 2, s % 2, tiles, slot_used, base_used + s + 1)

        def project_dve(dve, name, q):
            first, base_used, nxt = stream[name][0], used_base(name), next_tiles(name)
            for s in range(4):
                tiles = BIG if s < 2 else nxt
                for m in (2 * s, 2 * s + 1):
                    res_dve(dve, q, m, m % 2, 1.0, PS[:, m % 4, :], base_used + s + 1)
                    if s < 3 and m % 2 == 0:
                        split_dve(dve, first // 2 + (s + 2) // 2, s % 2, tiles)
                    res_dve_after(dve, q, m, m % 2, m == 0)
                if s == 3:
                    split_dve(dve, first // 2 + (s + 2) // 2, s % 2, tiles)

        def conv_act(act):
            d = CONV
            first, ub = stream["scin"][0], used_base("scin")
            for s in range(12):
                split_act(act, first // 2 + (s + 2) // 2, s % 2, BIG, slot_used, ub + s + 1)
                if s == 0:
                    norm_act(act, 4, d["n"])
                if s >= 8:
                    for m in (2 * (s - 8), 2 * (s - 8) + 1):
                        act.wait_ge(o_ready, KT + m + 1)
                        act.activation(ohi[:, m, :TN], tmp[2 + m % 2][:, :TN], ACT.Copy).then_inc(ohi_ready, 1)
            project_act(act, "scout", 5)

        TN = SEQ + SEQS * STEPS

        def conv_dve(dve):
            d = CONV
            first, ub, n = stream["scin"][0], used_base("scin"), d["n"]
            w = [lambda f, c=c: vec[:, f, V_CONV + c:V_CONV + c + 1] for c in range(3)]
            for s in range(12):
                if s == 0:
                    norm_dve(dve, 4, n)
                    dve.wait_ge(con_loaded, 16 * 3)
                    link(dve, dve.tensor_copy(us[:, :, :, 0:2], cin[:, :].rearrange("p (k b w) -> p k b w", k=KT, w=2)))
                dve.wait_ge(slot_used, ub + s + 1)
                if s < 8:
                    f = s
                    link(dve, dve.tensor_tensor(tmp[0][:, :n], PS[:, 2 * (s % 2), :n], rstd[:, :n], ALU.mult))
                    dve.tensor_tensor(tmp[2][:, :n], PS[:, 2 * (s % 2) + 1, :n], rstd[:, :n], ALU.mult).then_inc(scaled, 1)
                    dve.wait_ge(scaled, d["scaled"] + s + 3)
                    split_dve(dve, first // 2 + (s + 2) // 2, s % 2, BIG)
                    dve.tensor_tensor(up[:, f, :], tmp[0][:, :PR], tmp[2][:, :PR], ALU.mult)
                    link(dve, dve.tensor_tensor(
                        us[:, f, :, 2:], tmp[0][:, PR:n].rearrange("p (b t) -> p b t", t=STEPS),
                        tmp[2][:, PR:n].rearrange("p (b t) -> p b t", t=STEPS), ALU.mult))
                    cs = cv[:, f, SEQ:].rearrange("p (b t) -> p b t", t=STEPS)
                    dve.tensor_scalar(cv[:, f, :SEQ], up[:, f, 0:SEQ], w[0](f), None, ALU.mult)
                    link(dve, dve.tensor_scalar(cs, us[:, f, :, 0:STEPS], w[0](f), None, ALU.mult))
                    for c in (1, 2):
                        dve.scalar_tensor_tensor(out=cv[:, f, :SEQ], in0=up[:, f, c:c + SEQ], scalar=w[c](f),
                                                 in1=cv[:, f, :SEQ], op0=ALU.mult, op1=ALU.add)
                        link(dve, dve.scalar_tensor_tensor(out=cs, in0=us[:, f, :, c:c + STEPS], scalar=w[c](f),
                                                           in1=cs, op0=ALU.mult, op1=ALU.add))
                else:
                    ms_ = (2 * (s - 8), 2 * (s - 8) + 1)
                    link(dve, dve.tensor_tensor(tmp[0][:, :TN], PS[:, 2 * (s % 2), 2:n], rstd[:, 2:n], ALU.mult))
                    dve.tensor_tensor(tmp[1][:, :TN], PS[:, 2 * (s % 2) + 1, 2:n], rstd[:, 2:n], ALU.mult).then_inc(scaled, 1)
                    dve.wait_ge(scaled, d["scaled"] + s + 3)
                    for m in ms_:
                        dve.tensor_tensor(tmp[2 + m % 2][:, :TN], tmp[m % 2][:, :TN], cv[:, m, :],
                                          ALU.mult).then_inc(o_ready, 1)
                    split_dve(dve, first // 2 + (s + 2) // 2, s % 2, BIG)
                    for m in ms_:
                        dve.wait_ge(ohi_ready, KT + m + 1)
                        dve.tensor_tensor(olo[:, m, :TN], tmp[2 + m % 2][:, :TN], ohi[:, m, :TN].bitcast(F32),
                                          ALU.subtract).then_inc(olo_ready, 1)
                if s == 8:
                    link(dve, dve.tensor_copy(stage[:, :, 0:2], up[:, :, SEQ:]))
                    dve.tensor_copy(stage[:, :, 2:].rearrange("p k (b w) -> p k b w", w=2),
                                    us[:, :, :, STEPS:]).then_inc(conv_u, 1)
            project_dve(dve, "scout", 5)

        def final_pe(pe):
            norm_pe(pe, 6, 6, TN)

        def final_dve(dve):
            norm_dve(dve, 6, TN)
            for k in range(KT):
                dve.scalar_tensor_tensor(out=cv[:, k, :], in0=x[:, k, 16:], scalar=vec[:, k, V_FINAL:V_FINAL + 1],
                                         in1=rstd[:, :TN], op0=ALU.mult, op1=ALU.mult).then_inc(y_ready, 1)

        y_ready = sem("y_ready")

        MIX_GROUPS = 27
        R_GROUP = 15
        LAST_GROUP = [0, 1, 2, 3, 9, 13, 14, 15, 16, 17, 18, 19, 20, 21, 22, 26]
        XK, XW, XA, XG, XR, XV = 1, 2, 3, 4, 5, 6
        FEW, FEW_SLOTS = 14, (13, 14, 15, 16)
        SPLIT_ROWS = ({25: 13, 19: 14, 14: 15, 8: 16}, {30: 13, 27: 14, 23: 15, 18: 16})
        GATE_BANKS = (2, 0, 4, 6)
        BANKS = {R_GROUP + i: b for i, b in enumerate((2, 0, 6, 2))}
        BANKS.update({MIX_GROUPS - 4 + i: b for i, b in enumerate(GATE_BANKS)})
        Z_BANKS = (4, 6, 2)
        MIXED = {ver: (4, 5, 4, 5) for ver in (XK, XW, XA, XG)}
        MIXED.update({XR: (4, 5, 0, 1), XV: (4, 5, 2, 3)})
        SQUARES = (6, 7, 0, 1, 2, 3, 6, 7)
        VER_GROUP = {XK: 3, XW: 4, XA: 5, XG: 14, XR: 18}
        MU = {XR: 0, XW: 1, XK: 2, XV: 3, XA: 4, XG: 5}
        RD = slice(PAD, TS)
        YC = PAD + 14
        NY = TS - YC

        mix_out = sem("mix_out")
        mix_evac = sem("mix_evac")
        r_scaled = sem("r_scaled")
        hc_ready = sem("hc_ready")
        xx_all = sem("xx_all")
        xx_ready = sem("xx_ready")
        x_used = sem("x_used")
        lora_hi = sem("lora_hi")
        lora_in = sem("lora_in")
        lora_lo = sem("lora_lo")
        kk_ready = sem("kk_ready")
        kk_sq = sem("kk_sq")
        kk_ss = sem("kk_ss")
        kk_max = sem("kk_max")
        kk_root = sem("kk_root")
        kk_inv = sem("kk_inv")
        kk_spread = sem("kk_spread")
        a_normed = sem("a_normed")
        logs_ready = sem("logs_ready")
        decays = sem("decays")
        r_decay = sem("r_decay")
        ends_ready = sem("ends_ready")
        a_scaled = sem("a_scaled")
        bk_scaled = sem("bk_scaled")
        rk_ready = sem("rk_ready")
        rk_sum = sem("rk_sum")
        rk_kept = sem("rk_kept")
        z_done = sem("z_done")
        z_ready = sem("z_ready")
        z_stored = sem("z_stored")
        g_loaded = sem("g_loaded")
        inv_dve = sem("inv_dve")
        inv_pool = sem("inv_pool")
        inv_stored = [sem(f"inv_stored{i}") for i in range(2)]
        tt_loaded = [sem(f"tt_loaded{i}") for i in range(2)]
        shift_ready = sem("shift_ready")

        def mix_sp(sp):
            load_phase(sp, "mix", 0, 14)
            load_slot(sp, "mix", 14)
            sp.wait_ge(shift_ready, 1)
            sp.dma_start(shift_out, shst[:].rearrange("p k n -> p (k n)")).then_inc(stored, 16)
            for i in range(2):
                sp.dma_start(wt[i][:, :], blockeye_dram).then_inc(g_loaded, 16)
            for p in range(PAIRS):
                sp.wait_ge(z_ready, 2 * p + 2)
                for hh in range(2):
                    rows = slice(HD * hh, HD * hh + C)
                    sp.dma_start(zt_dram[:, 2 * p + hh].rearrange("c s t -> s c t"),
                                 z[rows, p, :, 0:C]).then_inc(z_stored, 16)
            sp.wait_ge(z_stored, 16 * HEADS)
            sp.dma_start(gt[0][:, :], zt_dram[0:8].rearrange("c h s t -> (c h) (s t)")).then_inc(g_loaded, 16)
            sp.dma_start(gt[1][:REST, :], zt_dram[8:].rearrange("c h s t -> (c h) (s t)")).then_inc(g_loaded, 16)
            load_slot(sp, "mix", 15)
            load_slot(sp, "wo", 0)
            load_slot(sp, "wo", 1)
            sp.wait_ge(inv_dve, 2 * (C - 1))
            sp.dma_start(tt_dram[0:8].rearrange("c h s t -> (c h) (s t)"), wt[0][:, :]).then_inc(inv_stored[0], 16)

            def load_inverses(c):
                sp.wait_ge(inv_stored[c // 8], 16)
                if c >= 2:
                    sp.wait_ge(u_done, 2 * (c - 1))
                for hh in range(2):
                    sp.dma_start(ttc[c % 2][HD * hh:HD * hh + C, :, :],
                                 tt_dram[c].rearrange("(p two) s t -> two s p t", two=2)[hh]).then_inc(tt_loaded[c % 2], 16)

            load_inverses(0)
            load_inverses(1)
            sp.wait_ge(inv_pool, 2 * (C - 1))
            sp.dma_start(tt_dram[8:].rearrange("c h s t -> (c h) (s t)"), wt[1][:REST, :]).then_inc(inv_stored[1], 16)
            sp.wait_ge(rk_sum, PAIRS)
            for n in range(SEQS):
                if n == SPC:
                    sp.wait_ge(lo_pool, MIXB + 19)
                    sp.wait_ge(lo_dve, MIXB + 19)
                sp.dma_start(s0s[n // SPC][:, n % SPC].rearrange("p a b -> p (a b)"), wkv_dram[n]).then_inc(s0_loaded, 16)
            load_slot(sp, "wo", 3)
            for c in range(2, CHUNKS):
                load_inverses(c)
                if c == PCHUNKS:
                    sp.wait_ge(st_ready, 2 * PCHUNKS + 1)
                    sp.dma_start(wkvp_out, st[PCHUNKS % 2][:].rearrange("p a b -> p (a b)")).then_inc(final_stored, 16)
            for n in range(SEQS):
                sp.wait_ge(seq_ready, n + 1)
                sp.dma_start(wkvs_out[n], s0s[n // SPC][:, n % SPC].rearrange("p a b -> p (a b)")).then_inc(seq_stored, 16)
            sp.wait_ge(seq_stored, 16 * SEQS)
            load_slot(sp, "wo", 2)

        REST = (CHUNKS - 8) * HEADS
        MIX_STORES = 1
        s0_loaded = sem("s0_loaded")
        seq_ready = sem("seq_ready")
        seq_stored = sem("seq_stored")
        final_stored = sem("final_stored")
        x_done = sem("x_done")
        xs_ready = sem("xs_ready")
        u_done = sem("u_done")
        uv_dve = sem("uv_dve")
        uv_act = sem("uv_act")
        s_done = sem("s_done")
        st_ready = sem("st_ready")
        y_done = sem("y_done")
        y_evac = sem("y_evac")
        v_turned = sem("v_turned")
        kv_turned = sem("kv_turned")
        arm_ready = sem("arm_ready")
        kvm_ready = sem("kvm_ready")
        q_done = sem("q_done")

        def mix_pe(pe):
            norm_pe(pe, 1, 1, T)
            group = [0]

            def open_group():
                g = group[0]
                group[0] += 1
                if g == R_GROUP + 3:
                    pe.wait_ge(r_scaled, 2)
                elif g == R_GROUP + 4:
                    pe.wait_ge(z_ready, 2 * PAIRS - 4)
                elif g >= 2 and g not in (R_GROUP + 2, R_GROUP + 5, MIX_GROUPS - 2, MIX_GROUPS - 1):
                    pe.wait_ge(mix_evac, g - 1 - (4 if g - 2 >= R_GROUP else 0))
                return BANKS.get(g, 2 * (g % 2))

            def project(slot, ver, fresh, final=False, shift=0):
                pe_slot_wait(pe, MIXB + slot)
                b = open_group()
                w_hi, w_lo = whi[slot % 2], wlo[slot % 2]
                for k in range(KT):
                    if fresh:
                        pe.wait_ge(xlo_ready, 8 * ver + k + 1)
                    for j in range(2):
                        for i, (w, v) in enumerate(passes(w_hi, w_lo, xhi, xlo)):
                            last = pe.matmul(PS[:, b + j, shift:shift + T], w[:, (2 * k + j) * P:(2 * k + j + 1) * P],
                                             v[:, k, :], start=(k == 0 and i == 0), stop=(k == KT - 1 and i == 2))
                    if final and k < KT - 1:
                        last.then_inc(x_used, 1)
                last.then_inc(mix_out, 1)

            def lora_inner(slot, ver):
                pe_slot_wait(pe, MIXB + slot)
                b = open_group()
                for k in range(KT):
                    pe.wait_ge(xlo_ready, 8 * ver + k + 1)
                    for i, (w, v) in enumerate(passes(whi[slot % 2], wlo[slot % 2], xhi, xlo)):
                        last = pe.matmul(PS[:, b, :T], w[:, k * P:(k + 1) * P], v[:, k, :],
                                         start=(k == 0 and i == 0), stop=(k == KT - 1 and i == 2))
                    if k < KT - 1:
                        last.then_inc(x_used, 1)
                last.then_inc(mix_out, 1)

            def lora_out(slot, first_tile, inner, shift=0):
                for m in range(0, KT, 2):
                    b = open_group()
                    for j in range(2):
                        for n, k in enumerate(inner):
                            tile = first_tile + KT * n + m + j
                            for i, (w, v) in enumerate(passes(whi[slot % 2], wlo[slot % 2], thi, tlo)):
                                last = pe.matmul(PS[:, b + j, shift:shift + T], w[:, tile * P:(tile + 1) * P], v[:, k, :],
                                                 start=(n == 0 and i == 0), stop=(n == len(inner) - 1 and i == 2))
                    last.then_inc(mix_out, 1)

            for s in range(4):
                project(s, XK, s == 0, s == 3, PAD)
            lora_inner(4, XW)
            for p in range(PAIRS):
                pe.wait_ge(kk_sq, p + 1)
                last = pe.matmul(PS[0:HEADS, 6, :T], con[:, K_SEL + 16 * p:K_SEL + 16 * p + 16],
                                 tmp[SQUARES[p]][:, RD], start=(p == 0), stop=(p == PAIRS - 1))
                last.then_inc(kk_ss, 1)
            lora_inner(5, XA)
            pe.wait_ge(lora_lo, 1)
            lora_out(4, KT, (0,))
            pe.wait_ge(lora_lo, 2)
            lora_out(5, KT, (1,), PAD)
            project(6, XG, True, True)

            def spread(p):
                if p >= 2:
                    pe.wait_ge(a_normed, p - 1)
                pe.matmul(PS[:, 4 + p % 2, :T], con[0:HEADS, K_SELT + P * p:K_SELT + P * p + P], rstd[0:HEADS, :],
                          start=True, stop=True).then_inc(kk_spread, 1)

            pe.wait_ge(kk_inv, 1)
            for s in range(4):
                spread(2 * s)
                spread(2 * s + 1)
                project(7 + s, XR, s == 0, s == 3)
            pe.wait_ge(a_normed, PAIRS)

            def sum_rk(p):
                pe.wait_ge(rk_ready, p + 1)
                if p == 0:
                    pe.wait_ge(r_scaled, PAIRS)
                pe.matmul(PS[0:HEADS, 0, :T], con[:, K_SEL + 16 * p:K_SEL + 16 * p + 16], tmp[p % 2][:, RD],
                          start=(p == 0), stop=(p == PAIRS - 1)).then_inc(rk_sum, 1)

            for p in range(PAIRS):
                pe.wait_ge(a_scaled, p + 1)
                pe.wait_ge(bk_scaled, p + 1)
                pe.wait_ge(r_scaled, max(p + 1, 6 if p else 1))
                if p == 2:
                    pe.wait_ge(r_scaled, PAIRS)
                if p >= 3:
                    pe.wait_ge(z_ready, 2 * p - 4)
                for c in range(CHUNKS):
                    for hh in range(2):
                        rows = slice(HD * hh, HD * hh + HD)
                        last = pe.matmul(PS[rows, Z_BANKS[p % 3] + c // 8, (c % 8) * 64:(c % 8) * 64 + 64],
                                         bk[rows, p, c, :, :].rearrange("p h t -> p (h t)"),
                                         ar[rows, p, :, c * C:c * C + C], start=True, stop=True)
                last.then_inc(z_done, 1)
                if p >= 2:
                    sum_rk(p - 2)
            sum_rk(PAIRS - 2)
            sum_rk(PAIRS - 1)
            for s in range(4):
                if s == 1:
                    pe.wait_ge(rk_kept, 1)
                project(11 + s, XV, s == 0)
            pe_slot_wait(pe, MIXB + 15)
            pe.wait_ge(lora_lo, 4)
            pe.wait_ge(z_ready, 2 * PAIRS)
            lora_out(15, 0, (0, 1))
            chain_pe(pe)
            pe.wait_ge(y_evac, CHUNKS)
            for p in range(PAIRS):
                if p >= 2:
                    pe.wait_ge(yc_ready, p - 1)
                pe.matmul(PS[:, p % 2, :NY], con[:, K_BLOCK:K_BLOCK + P], yb[:, p, 14:], start=True, stop=True)\
                    .then_inc(mean_done, 1)
            for p in range(PAIRS):
                pe.wait_ge(yc_sq, p + 1)
                pe.matmul(PS[0:HEADS, 6, :NY], con[:, K_SEL + 16 * p:K_SEL + 16 * p + 16],
                          tmp[6 + p % 2][:, :NY], start=(p == 0), stop=(p == PAIRS - 1)).then_inc(var_done, 1)
            pe.wait_ge(gn_inv, 1)
            for p in range(PAIRS):
                if p >= 2:
                    pe.wait_ge(gn_used, p - 1)
                pe.matmul(PS[:, 4 + p % 2, :NY], con[0:HEADS, K_SELT + P * p:K_SELT + P * p + P], rstd[0:HEADS, :NY],
                          start=True, stop=True).then_inc(gn_spread, 1)
            project_pe(pe, "wo", 2, T - 14, 0)

        mean_done = sem("mean_done")
        rk_spread = sem("rk_spread")
        bonus_ready = sem("bonus_ready")
        yc_ready = sem("yc_ready")
        yc_sq = sem("yc_sq")
        var_done = sem("var_done")
        gn_root = sem("gn_root")
        gn_inv = sem("gn_inv")
        gn_spread = sem("gn_spread")
        gn_used = sem("gn_used")

        def chain_pe(pe):
            def step_x(c, g):
                pe.wait_ge(v_turned, c + 1)
                if c < PCHUNKS:
                    pe.wait_ge(st_ready, 2 * c + 1 if c == 0 else 2 * c + g)
                    if c == 0:
                        pe.wait_ge(mix_evac, 20)
                else:
                    pe.wait_ge(arm_ready, 2 * (c - PCHUNKS) + 1)
                    pe.wait_ge(s0_loaded, 16 * SPC * (c - PCHUNKS + 1))
                if c >= 1:
                    pe.wait_ge(xs_ready, 2 * (c - 1) + g + 1)
                for p in range(4 * g, 4 * g + 4):
                    for hh in range(2):
                        rows = slice(HD * hh, HD * hh + HD)
                        out = PS[HD * hh:HD * hh + C, g, (p - 4 * g) * HD:(p - 4 * g + 1) * HD]
                        if c < PCHUNKS:
                            pe.matmul(out, ar[rows, p, 0, c * C:c * C + C], st[c % 2][rows, p, :], start=True, stop=False)
                        else:
                            for q in range(SPC):
                                pe.matmul(out, arm[rows, q, p, :], s0s[c - PCHUNKS][rows, q, p, :],
                                          start=(q == 0), stop=False)
                        rows = slice(HD * hh + C, HD * hh + 2 * C)
                        last = pe.matmul(out, z[rows, p, c, 0:C], uv[c % 2][rows, p, :], start=False, stop=True)
                last.then_inc(x_done, 1)

            def step_u(c, g):
                if c == 0:
                    pe.wait_ge(mix_evac, 21)
                pe.wait_ge(tt_loaded[c % 2], 32 * (c // 2 + 1))
                pe.wait_ge(xs_ready, 2 * c + g + 1)
                if c >= 1:
                    pe.wait_ge(uv_dve, 2 * (c - 1) + g + 1)
                    pe.wait_ge(uv_act, 2 * (c - 1) + g + 1)
                for p in range(4 * g, 4 * g + 4):
                    for hh in range(2):
                        rows = slice(HD * hh, HD * hh + C)
                        last = pe.matmul(PS[rows, 2 + g, (p - 4 * g) * HD:(p - 4 * g + 1) * HD],
                                         ttc[c % 2][rows, p, :], xs[rows, p, :], start=True, stop=True)
                last.then_inc(u_done, 1)

            def step_s(c, g):
                pe.wait_ge(uv_dve, 2 * c + g + 1)
                pe.wait_ge(uv_act, 2 * c + g + 1)
                if c == 0:
                    pe.wait_ge(mix_evac, 22)
                pe.wait_ge(kv_turned, c + 1)
                if c >= 1:
                    pe.wait_ge(st_ready, 2 * c + g)
                for p in range(4 * g, 4 * g + 4):
                    for hh in range(2):
                        rows = slice(HD * hh, HD * hh + HD)
                        last = pe.matmul(PS[rows, 4 + g, (p - 4 * g) * HD:(p - 4 * g + 1) * HD],
                                         kv[c % 2][rows, p, :], uv[c % 2][rows, p, :], start=True, stop=True)
                last.then_inc(s_done, 1)

            def read_out(c):
                if c >= 1:
                    pe.wait_ge(y_evac, c)
                else:
                    pe.wait_ge(mix_evac, 23)
                if c >= PCHUNKS:
                    pe.wait_ge(arm_ready, 2 * (c - PCHUNKS) + 2)
                for p in range(PAIRS):
                    for hh in range(2):
                        rows = slice(HD * hh, HD * hh + HD)
                        out = PS[HD * hh:HD * hh + C, 7, p * HD:p * HD + HD]
                        if c < PCHUNKS:
                            pe.matmul(out, ar[rows, p, 1, c * C:c * C + C], st[c % 2][rows, p, :], start=True, stop=False)
                        else:
                            for q in range(SPC):
                                pe.matmul(out, rm[rows, q, p, :], s0s[c - PCHUNKS][rows, q, p, :],
                                          start=(q == 0), stop=False)
                        last = pe.matmul(out, z[rows, p, c, C:], uv[c % 2][rows, p, :], start=False, stop=True)
                last.then_inc(y_done, 1)

            def step_q(c):
                for q in range(SPC):
                    k = SPC * (c - PCHUNKS) + q
                    pe.wait_ge(kvm_ready, k + 1)
                    if k >= 2:
                        pe.wait_ge(seq_ready, k - 1)
                    for p in range(PAIRS):
                        for hh in range(2):
                            rows = slice(HD * hh, HD * hh + HD)
                            last = pe.matmul(PS[rows, 4 + q % 2, p * HD:p * HD + HD], st[q % 2][rows, p, :],
                                             uv[c % 2][rows, p, :], start=True, stop=True)
                    last.then_inc(q_done, 1)
                    if k >= 1:
                        pe.wait_ge(bonus_ready, k)
                    pe.matmul(PS[:, 6, :NY], con[0:HEADS, K_SELT + P * k:K_SELT + P * k + P], rks[:, 14:],
                              start=True, stop=True).then_inc(rk_spread, 1)

            for c in range(CHUNKS):
                step_x(c, 0)
                step_x(c, 1)
                step_u(c, 0)
                step_u(c, 1)
                if c < PCHUNKS:
                    step_s(c, 0)
                    step_s(c, 1)
                    read_out(c)
                else:
                    pe.wait_ge(uv_dve, 2 * c + 2)
                    pe.wait_ge(uv_act, 2 * c + 2)
                    read_out(c)
                    step_q(c)

        def mix_act(act):
            dn = used_base("down0")
            norm_act(act, 1, T)

            def split(k):
                split_act(act, (MIXB + k) // 2, k % 2, BIG, mix_out, LAST_GROUP[k - 2] + 1)

            def x_hi_tile(ver, k):
                act.wait_ge(xg_ready, 8 * ver + k + 1)
                if ver > XK:
                    if k < KT - 1:
                        act.wait_ge(x_used, (KT - 1) * (ver - 2) + k + 1)
                    else:
                        act.wait_ge(mix_out, VER_GROUP[ver - 1] + 1)
                act.activation(xhi[:, k, :], tmp[MIXED[ver][k % 4]][:, :T], ACT.Copy).then_inc(xhi_ready, 1)

            def x_hi(ver):
                for k in range(KT):
                    x_hi_tile(ver, k)

            def evac(g, outs):
                act.wait_ge(mix_out, g + 1)
                for j, (dst, func, bias, padded) in enumerate(outs):
                    kw = {} if bias is None else {"bias": bias}
                    src = PS[:, 2 * (g % 2) + j, :T]
                    if padded:
                        src = PS[:, 2 * (g % 2) + j, :TS].rearrange("p (c t) -> p c t", t=C)
                    last = act.activation(dst, src, func, **kw)
                last.then_inc(mix_evac, 1)

            def square_kk(p):
                act.wait_ge(kk_ready, p + 1)
                if p >= 6:
                    act.wait_ge(kk_ss, p - 5)
                act.activation(tmp[SQUARES[p]][:, RD], ar[:, p, 0, PAD:], ACT.Square).then_inc(kk_sq, 1)

            def decay(p):
                act.wait_ge(logs_ready, p + 1)
                if p >= 2:
                    act.wait_ge(a_scaled, p - 1)
                    act.wait_ge(bk_scaled, p - 1)
                act.activation(tmp[2 + p % 2][:, RD], sw[:, p, PAD:], ACT.Exp, scale=-E_HALF).then_inc(decays, 1)
                act.activation(tmp[6 + p % 2][:, RD], sw[:, p, PAD:], ACT.Exp, scale=E_HALF).then_inc(decays, 1)

            def decay_r(p):
                act.wait_ge(logs_ready, p + 1)
                if p >= 2:
                    act.wait_ge(r_scaled, p - 1)
                else:
                    act.wait_ge(xlo_ready, 8 * XR + KT)
                act.activation(tmp[p % 2][:, RD], sw[:, p, PAD:], ACT.Exp, scale=-E_HALF).then_inc(r_decay, 1)

            x_hi(XK)
            for s in range(4):
                if s == 3:
                    x_hi(XW)
                split(2 + s)
                evac(s, [(bk[:, m, :, 1, :], ACT.Copy, None, True) for m in (2 * s, 2 * s + 1)])
                if s:
                    square_kk(2 * s - 2)
                    square_kk(2 * s - 1)
            for k in range(KT):
                x_hi_tile(XA, k)
                if k in (0, 1):
                    square_kk(6 + k)
            act.wait_ge(mix_out, 5)
            act.wait_ge(kk_ss, PAIRS)
            act.activation(tmp[0][:, :T], PS[:, 0, :T], ACT.Tanh).then_inc(mix_evac, 1)
            act.wait_ge(mix_evac, 5)
            act.activation(thi[:, 0, :], tmp[0][:, :T], ACT.Copy).then_inc(lora_hi, 1)
            x_hi_tile(XG, 0)
            x_hi_tile(XG, 1)
            act.wait_ge(mix_out, 6)
            act.activation(tmp[1][:, :T], PS[:, 2, :T], ACT.Copy).then_inc(mix_evac, 1)
            act.wait_ge(mix_evac, 6)
            act.activation(thi[:, 1, :], tmp[1][:, :T], ACT.Copy).then_inc(lora_hi, 1)
            for s in range(4):
                x_hi_tile(XG, 2 + s)
                evac(6 + s, [(sw[:, m, PAD:], ACT.Sigmoid, vec[:, m, V_W0:V_W0 + 1], False) for m in (2 * s, 2 * s + 1)])
            split(6)
            x_hi_tile(XG, KT - 2)
            x_hi_tile(XG, KT - 1)
            for s in range(4):
                evac(10 + s, [(bk[:, m, :, 0, :], ACT.Sigmoid, vec[:, m, V_A0:V_A0 + 1], True) for m in (2 * s, 2 * s + 1)])
                if s == 1:
                    act.wait_ge(kk_max, 1)
                    act.activation(tmp[3][0:HEADS, :T], tmp[3][0:HEADS, :T], ACT.Sqrt).then_inc(kk_root, 1)
            split(7)
            x_hi(XR)
            split(8)
            act.wait_ge(mix_out, 15)
            act.wait_ge(kk_inv, 1)
            act.activation(tmp[2][:, :T], PS[:, 0, :T], ACT.Sigmoid).then_inc(lora_in, 1)
            act.activation(tmp[3][:, :T], PS[:, 1, :T], ACT.Sigmoid).then_inc(mix_evac, 1)
            act.wait_ge(mix_evac, 15)
            act.wait_ge(lora_in, 1)
            act.activation(thi[:, 0, :], tmp[2][:, :T], ACT.Copy).then_inc(lora_hi, 1)
            act.activation(thi[:, 1, :], tmp[3][:, :T], ACT.Copy).then_inc(lora_hi, 1)
            for p in range(PAIRS):
                if p in (3, 5, 7):
                    split(8 + p // 2)
                decay(p)
                if p >= 1:
                    decay_r(p - 1)
            for lo, hi, first, step in ((0, PCHUNKS, C - 1, C), (PCHUNKS, PCHUNKS + SEQS, PCHUNKS * C + STEPS - 1, STEPS)):
                act.activation(dend[:, :, lo:hi], sw[:, :, first:first + (hi - lo - 1) * step + 1:step], ACT.Exp,
                               scale=-E_HALF).then_inc(ends_ready, 1)
            decay_r(PAIRS - 1)
            x_hi(XV)
            split(12)
            act.wait_ge(rk_sum, PAIRS)
            act.activation(rks[:, :], PS[0:HEADS, 0, :T], ACT.Copy).then_inc(rk_kept, 1)
            for s in range(4):
                split(13 + s)
                evac(19 + s, [(vy[:, m, PAD:], ACT.Copy, None, False) for m in (2 * s, 2 * s + 1)])
            act.wait_ge(inv_stored[0], 16)
            act.wait_ge(mix_out, MIX_GROUPS)
            for s in (1, 0, 2, 3):
                act.activation(gate[:, 2 * s, :], PS[:, GATE_BANKS[s], :T], ACT.Copy)
                act.activation(gate[:, 2 * s + 1, :], PS[:, GATE_BANKS[s] + 1, :T], ACT.Copy).then_inc(mix_evac, 1)
            split(17)
            chain_act(act)
            for p in range(PAIRS):
                act.wait_ge(yc_ready, p + 1)
                if p >= 2:
                    act.wait_ge(var_done, p - 1)
                act.activation(tmp[6 + p % 2][:, :NY], yb[:, p, 14:], ACT.Square).then_inc(yc_sq, 1)
            act.wait_ge(var_done, PAIRS)
            act.activation(ms[0:HEADS, :NY], PS[0:HEADS, 6, :NY], ACT.Sqrt, bias=GN_EPS, scale=1.0 / HD)\
                .then_inc(gn_root, 1)
            for p in range(PAIRS):
                act.wait_ge(o_ready, p + 1)
                act.activation(ohi[:, p, :NY], tmp[2 + p % 4][:, :NY], ACT.Copy).then_inc(ohi_ready, 1)
            project_act(act, "wo", 2)

        def chain_act(act):
            for c in range(CHUNKS):
                for g in range(2):
                    act.wait_ge(x_done, 2 * c + g + 1)
                    if c >= 1:
                        act.wait_ge(u_done, 2 * (c - 1) + g + 1)
                    act.activation(xs[0:HD + C, 4 * g:4 * g + 4, :],
                                   PS[0:HD + C, g, 0:256].rearrange("p (a b) -> p a b", b=HD), ACT.Copy)\
                        .then_inc(xs_ready, 1)
                for g in range(2):
                    act.wait_ge(u_done, 2 * c + g + 1)
                    if c >= 2:
                        act.wait_ge(y_done, c - 1)
                    act.activation(uv[c % 2][HD:HD + C, 4 * g:4 * g + 4, :],
                                   PS[HD:HD + C, 2 + g, 0:256].rearrange("p (a b) -> p a b", b=HD), ACT.Copy)\
                        .then_inc(uv_act, 1)

        def mix_pool(pool):
            def split(k):
                split_pool(pool, (MIXB + k) // 2, k % 2, BIG, FEW if k in FEW_SLOTS else None)

            seqs = slice(TP, T, STEPS)
            for k in range(KT):
                pool.wait_ge(hc_ready, k + 1)
                pool.tensor_tensor(xx[:, k, 1:], hc[:, k, :T - 1], hc[:, k, 1:], ALU.subtract).then_inc(xx_all, 1)
                pool.tensor_scalar(xx[:, k, 0:1], hc[:, k, 0:1], -1.0, None, ALU.mult)
                pool.wait_ge(xx_all, k + 1)
                pool.tensor_tensor(xx[:, k, seqs], shin[:, SEQS * k:SEQS * k + SEQS], hc[:, k, seqs],
                                   ALU.subtract).then_inc(xx_ready, 1)
            def low(ver, k):
                pool.wait_ge(xhi_ready, 8 * ver + k + 1)
                pool.tensor_tensor(xlo[:, k, :], tmp[MIXED[ver][k % 4]][:, :T], xhi[:, k, :].bitcast(F32),
                                   ALU.subtract).then_inc(xlo_ready, 1)

            for k in range(2, 8):
                split(k)
            for k in range(KT):
                low(XR, k)
            split(8)
            for p in range(PAIRS):
                if p in (3, 5, 7):
                    split(8 + p // 2)
                pool.wait_ge(decays, 2 * p + 2)
                pool.wait_ge(b_ready, p + 1)
                e = tmp[6 + p % 2][:].rearrange("p (c one t) -> p c one t", one=1, t=C)
                pool.tensor_tensor(bk[:, p], bk[:, p], e.to_broadcast([P, CHUNKS, 2, C]), ALU.mult).then_inc(bk_scaled, 1)
            for k in range(KT):
                low(XV, k)
            split(12)
            pool.wait_ge(g_loaded, 64)
            inverse(pool, 1, REST, inv_pool, split)
            split(17)
            seq = con[:, K_SEQCOL:K_SEQCOL + SPC * C].rearrange("p (q t) -> p q t", t=C)
            pool.wait_ge(rk_sum, PAIRS)
            for c in range(PCHUNKS, CHUNKS):
                if c > PCHUNKS:
                    pool.wait_ge(x_done, 2 * c)
                for masked, part in ((arm, 0), (rm, 1)):
                    if c > PCHUNKS and part:
                        pool.wait_ge(y_done, c)
                    for q in range(SPC):
                        last = pool.tensor_tensor(masked[:, q], ar[:, :, part, c * C:c * C + C],
                                                  seq[:, q:q + 1, :].to_broadcast([P, PAIRS, C]), ALU.mult)
                    last.then_inc(arm_ready, 1)
            for p in range(PAIRS):
                pool.wait_ge(ohi_ready, p + 1)
                pool.tensor_tensor(olo[:, p, :NY], tmp[2 + p % 4][:, :NY], ohi[:, p, :NY].bitcast(F32),
                                   ALU.subtract).then_inc(olo_ready, 1)

        def inverse(eng, slot, rows, out_sem, split):
            g = gt[slot][:rows, :].rearrange("p (s t) -> p s t", t=C)
            w = wt[slot][:rows, :].rearrange("p (s t) -> p s t", t=C)
            done = 0
            split_rows = SPLIT_ROWS[slot]
            for r in range(C - 1, 0, -1):
                if r in split_rows:
                    split(split_rows[r])
                n = C - r
                o = outer[slot][:rows, :r * n].rearrange("p (s t) -> p s t", t=n)
                if done:
                    eng.wait_ge(out_sem, done)
                eng.tensor_tensor(o, g[:, 0:r, r:r + 1].to_broadcast([rows, r, n]),
                                  w[:, r:r + 1, r:].to_broadcast([rows, r, n]), ALU.mult).then_inc(out_sem, 1)
                eng.wait_ge(out_sem, done + 1)
                eng.tensor_tensor(w[:, 0:r, r:], w[:, 0:r, r:], o, ALU.add).then_inc(out_sem, 1)
                done += 2

        def mix_dve(dve):
            norm_dve(dve, 1, T)

            def split(k):
                split_dve(dve, (MIXB + k) // 2, k % 2, BIG, FEW if k in FEW_SLOTS else None)

            def mixed(ver, k):
                dve.wait_ge(xlo_ready, 8 * ver + (max(k - 3, 0) if ver in (XR, XV) else k - 1))
                dve.scalar_tensor_tensor(out=tmp[MIXED[ver][k % 4]][:, :T], in0=xx[:, k, :],
                                         scalar=vec[:, k, V_MU + MU[ver]:V_MU + MU[ver] + 1], in1=hc[:, k, :],
                                         op0=ALU.mult, op1=ALU.add).then_inc(xg_ready, 1)

            def low(ver, k):
                dve.wait_ge(xhi_ready, 8 * ver + k + 1)
                dve.tensor_tensor(xlo[:, k, :], tmp[MIXED[ver][k % 4]][:, :T], xhi[:, k, :].bitcast(F32),
                                  ALU.subtract).then_inc(xlo_ready, 1)

            def normed(k):
                dve.scalar_tensor_tensor(out=hc[:, k, :], in0=x[:, k, :], scalar=vec[:, k, V_MIX:V_MIX + 1],
                                         in1=rstd[:], op0=ALU.mult, op1=ALU.mult).then_inc(hc_ready, 1)

            def mix_version(ver):
                mixed(ver, 0)
                for k in range(KT):
                    if k + 1 < KT:
                        mixed(ver, k + 1)
                    low(ver, k)

            def kk(p):
                dve.wait_ge(mix_evac, p // 2 + 1)
                link(dve, dve.memset(bk[:, p, 0, 1, 0:PAD], 0.0))
                dve.tensor_scalar(ar[:, p, 0, :].rearrange("p (c t) -> p c t", t=C), bk[:, p, :, 1, :],
                                  vec[:, p, V_KK:V_KK + 1], None, ALU.mult).then_inc(kk_ready, 1)

            def lora_low(n, k):
                dve.wait_ge(lora_hi, n + 1)
                dve.tensor_tensor(tlo[:, k, :], tmp[n][:, :T], thi[:, k, :].bitcast(F32), ALU.subtract).then_inc(lora_lo, 1)

            def r_decayed(p):
                g = R_GROUP + p // 2
                dve.wait_ge(mix_out, g + 1)
                dve.wait_ge(r_decay, p + 1)
                dve.tensor_tensor(ar[:, p, 1, PAD:], PS[:, BANKS[g] + p % 2, :T], tmp[p % 2][:, RD],
                                  ALU.mult).then_inc(r_scaled, 1)

            normed(0)
            normed(1)
            for k in range(KT):
                if k + 2 < KT:
                    normed(k + 2)
                dve.wait_ge(xx_ready, k + 1)
                mixed(XK, k)
                if k:
                    low(XK, k - 1)
            low(XK, KT - 1)
            dve.tensor_copy(shst[:, :, 0:1], hc[:, :, TP - 1:TP])
            dve.tensor_copy(shst[:, :, 1:], hc[:, :, TP + STEPS - 1::STEPS]).then_inc(shift_ready, 1)
            dve.memset(ar[:, :, 1, 0:PAD], 0.0)
            for t in tmp[6:]:
                dve.memset(t[:, 0:PAD], 0.0)
            link(dve, dve.tensor_scalar(vec[:, :, V_OMKA:V_OMKA + 1], vec[:, :, V_KA:V_KA + 1], -1.0, 1.0,
                                        ALU.mult, ALU.add))
            for s in range(3):
                split(2 + s)
                kk(2 * s)
                kk(2 * s + 1)
            mix_version(XW)
            split(5)
            kk(PAIRS - 2)
            kk(PAIRS - 1)
            mix_version(XA)
            lora_low(0, 0)
            mixed(XG, 0)
            for k in range(KT):
                if k + 1 < KT:
                    mixed(XG, k + 1)
                low(XG, k)
                if k == 1:
                    lora_low(1, 1)
            dve.wait_ge(kk_ss, PAIRS)
            dve.tensor_scalar(tmp[3][0:HEADS, :T], PS[0:HEADS, 6, :T], 1e-24, None, ALU.max).then_inc(kk_max, 1)
            split(6)
            dve.wait_ge(kk_root, 1)
            dve.reciprocal(rstd[0:HEADS, :], tmp[3][0:HEADS, :T]).then_inc(kk_inv, 1)
            split(7)
            for k in range(KT):
                mixed(XR, k)
            split(8)
            lora_low(2, 0)
            lora_low(3, 1)
            dve.wait_ge(mix_evac, 14)
            for p in range(PAIRS):
                if p in (3, 5, 7):
                    split(8 + p // 2)
                pair_front(dve, p)
                if p:
                    pair_back(dve, p - 1)
                if p >= 3:
                    r_decayed(p - 3)
            pair_back(dve, PAIRS - 1)
            r_decayed(PAIRS - 3)
            dve.wait_ge(a_scaled, PAIRS)
            for k in range(KT):
                mixed(XV, k)
                if k in (3, 5):
                    r_decayed(PAIRS - 2 + k // 5)
            for p in range(PAIRS):
                dve.wait_ge(bk_scaled, p + 1)
                if p >= 2:
                    dve.wait_ge(rk_sum, p - 1)
                else:
                    dve.wait_ge(r_scaled, PAIRS)
                dve.scalar_tensor_tensor(out=tmp[p % 2][:].rearrange("p (c t) -> p c t", t=C),
                                         in0=ar[:, p, 1, :].rearrange("p (c t) -> p c t", t=C),
                                         scalar=vec[:, p, V_RK:V_RK + 1], in1=bk[:, p, :, 1, :],
                                         op0=ALU.mult, op1=ALU.mult).then_inc(rk_ready, 1)
                if p == 3:
                    split(12)
                dve.wait_ge(z_done, p + 1)
                if p == 0:
                    dve.wait_ge(ends_ready, 2)
                    dve.wait_ge(xlo_ready, 8 * XV + KT)
                for i, (c0, c1) in enumerate(((0, 8), (8, CHUNKS))):
                    n = (c1 - c0) * 2 * C
                    dve.tensor_tensor(z[:, p, c0:c1, :].rearrange("p c t -> p (c t)"), PS[:, Z_BANKS[p % 3] + i, :n],
                                      con[:, K_ZMASK + c0 * 2 * C:K_ZMASK + c1 * 2 * C], ALU.mult).then_inc(z_ready, 1)
            dve.memset(vy[:, :, 0:PAD], 0.0)
            dve.wait_ge(g_loaded, 64)
            inverse(dve, 0, P, inv_dve, split)
            chain_dve(dve, split)
            for p in range(PAIRS):
                dve.wait_ge(mean_done, p + 1)
                dve.scalar_tensor_tensor(out=yb[:, p, 14:], in0=PS[:, p % 2, :NY], scalar=-1.0 / HD, in1=yb[:, p, 14:],
                                         op0=ALU.mult, op1=ALU.add).then_inc(yc_ready, 1)
            dve.wait_ge(gn_root, 1)
            dve.reciprocal(rstd[0:HEADS, :NY], ms[0:HEADS, :NY]).then_inc(gn_inv, 1)
            dve.wait_ge(seq_stored, 16 * SEQS)
            for p in range(PAIRS):
                t = tmp[2 + p % 4][:, :NY]
                if p >= 4:
                    dve.wait_ge(olo_ready, p - 3)
                dve.wait_ge(gn_spread, p + 1)
                dve.wait_ge(yc_ready, PAIRS)
                dve.wait_ge(bonus_ready, PAIRS)
                dve.tensor_tensor(t, PS[:, 4 + p % 2, :NY], yb[:, p, 14:], ALU.mult).then_inc(gn_used, 1)
                dve.wait_ge(gn_used, p + 1)
                link(dve, dve.scalar_tensor_tensor(out=t, in0=t, scalar=vec[:, p, V_LNW:V_LNW + 1], in1=vy[:, p, YC:],
                                                   op0=ALU.mult, op1=ALU.add))
                dve.scalar_tensor_tensor(out=t, in0=t, scalar=vec[:, p, V_LNB:V_LNB + 1], in1=gate[:, p, 14:],
                                         op0=ALU.add, op1=ALU.mult).then_inc(o_ready, 1)
            project_dve(dve, "wo", 2)

        def pair_front(dve, p):
            a = ar[:, p, 0, :].rearrange("p (c t) -> p c t", t=C)
            factor = tmp[6 + p % 2][:].rearrange("p (c t) -> p c t", t=C)
            b, k = bk[:, p, :, 0, :], bk[:, p, :, 1, :]
            if p >= 2:
                dve.wait_ge(bk_scaled, p - 1)
            dve.tensor_scalar(factor, b, vec[:, p, V_KA:V_KA + 1], vec[:, p, V_OMKA:V_OMKA + 1],
                              ALU.mult, ALU.add)
            link(dve, dve.tensor_tensor_scan(sw[:, p, PAD:], con[:, K_SCAN + PAD:K_SCAN + TS], sw[:, p, PAD:], 0.0,
                                             ALU.mult, ALU.add))
            dve.wait_ge(kk_spread, p + 1)
            dve.tensor_tensor(ar[:, p, 0, PAD:], PS[:, 4 + p % 2, :T], ar[:, p, 0, PAD:], ALU.mult).then_inc(a_normed, 1)
            dve.tensor_tensor(k, k, factor, ALU.mult).then_inc(logs_ready, 1)
            dve.wait_ge(a_normed, p + 1)
            dve.scalar_tensor_tensor(out=b, in0=a, scalar=-1.0, in1=b, op0=ALU.mult, op1=ALU.mult).then_inc(b_ready, 1)

        def pair_back(dve, p):
            dve.wait_ge(decays, 2 * p + 1)
            dve.wait_ge(b_ready, p + 1)
            for a0, n, size in ((PAD, 1, C - PAD), (C, PCHUNKS - 1, C), (PCHUNKS * C, SEQS, STEPS)):
                e = tmp[2 + p % 2][:, a0:a0 + n * size].rearrange("p (n s) -> p n s", s=size)
                a = ar[:, p, 0, a0:a0 + n * size].rearrange("p (n s) -> p n s", s=size)
                last = dve.tensor_tensor(a[:, :, 1:], a[:, :, 1:], e[:, :, :size - 1], ALU.mult)
            last.then_inc(a_scaled, 1)

        b_ready = sem("b_ready")

        def chain_dve(dve, split):
            def turn(c):
                if c >= 2:
                    dve.wait_ge(y_done, c - 1)
                for hh in range(2):
                    for f in range(2):
                        src = slice(HD * hh + C * f, HD * hh + C * f + C)
                        last = dve.transpose(uv[c % 2][HD * hh + C:HD * hh + 2 * C, :, C * f:C * f + C],
                                             vy[src, :, c * C:c * C + C])
                last.then_inc(v_turned, 1)
                for hh in range(2):
                    for f in range(2):
                        src = slice(HD * hh + C * f, HD * hh + C * f + C)
                        for n in range(2):
                            last = dve.transpose(kv[c % 2][HD * hh + C * n:HD * hh + C * n + C, :, C * f:C * f + C],
                                                 bk[src, :, c, n, :])
                last.then_inc(kv_turned, 1)

            def bonus(p):
                dve.wait_ge(rk_spread, p + 1)
                dve.tensor_tensor(vy[:, p, YC:], PS[:, 6, :NY], vy[:, p, YC:], ALU.mult).then_inc(bonus_ready, 1)

            def turn_y(c):
                dve.wait_ge(y_done, c + 1)
                if c == 1:
                    dve.wait_ge(y_evac, 1)
                    dve.wait_ge(inv_stored[1], 16)
                for hh in range(2):
                    for f in range(2):
                        src = PS[HD * hh:HD * hh + C, 7, :].rearrange("p (a b) -> p a b", b=HD)[:, :, C * f:C * f + C]
                        dst = slice(HD * hh + C * f, HD * hh + C * f + C)
                        if c == 0:
                            last = dve.transpose(y0[dst, :, :], src)
                        else:
                            last = dve.transpose(yb[dst, :, c * C - PAD:c * C - PAD + C], src)
                last.then_inc(y_evac, 1)
                if c == 1:
                    dve.tensor_copy(yb[:, :, 0:C - PAD], y0[:, :, PAD:])

            dve.wait_ge(mix_evac, 19)
            dve.memset(st[0][:], 0.0).then_inc(st_ready, 1)
            turn(0)
            split(17)
            for c in range(CHUNKS):
                if 1 <= c <= PCHUNKS:
                    turn_y(c - 1)
                if c + 1 < CHUNKS:
                    turn(c + 1)
                for g in range(2):
                    dve.wait_ge(u_done, 2 * c + g + 1)
                    dve.tensor_copy(uv[c % 2][0:C, 4 * g:4 * g + 4, :],
                                    PS[0:C, 2 + g, 0:256].rearrange("p (a b) -> p a b", b=HD)).then_inc(uv_dve, 1)
                if c < PCHUNKS:
                    for g in range(2):
                        dve.wait_ge(s_done, 2 * c + g + 1)
                        if c >= 1:
                            dve.wait_ge(y_done, c)
                        ps = slice(4 * g, 4 * g + 4)
                        link(dve, dve.tensor_tensor(sd[:, ps, :], st[c % 2][:, ps, :],
                                                    PS[:, 4 + g, 0:256].rearrange("p (a b) -> p a b", b=HD), ALU.add))
                        dve.tensor_tensor(st[(c + 1) % 2][:, ps, :], sd[:, ps, :],
                                          dend[:, ps, c:c + 1].to_broadcast([P, 4, HD]), ALU.mult).then_inc(st_ready, 1)
                    continue
                if c == PCHUNKS:
                    dve.wait_ge(final_stored, 16)
                    dve.wait_ge(y_done, c)
                for q in range(SPC):
                    k = SPC * (c - PCHUNKS) + q
                    if k >= 2:
                        dve.wait_ge(q_done, k - 1)
                    dve.tensor_scalar(st[q % 2][:], kv[c % 2][:], con[:, K_SEQROW + q:K_SEQROW + q + 1], None,
                                      ALU.mult).then_inc(kvm_ready, 1)
                    if q == 1:
                        turn_y(c)
                    if q >= 1:
                        new_state(dve, c, q - 1)
                        bonus(k - 1)
                new_state(dve, c, SPC - 1)
                bonus(k)

        def new_state(dve, c, q):
            k = SPC * (c - PCHUNKS) + q
            state = s0s[c - PCHUNKS][:, q]
            dve.wait_ge(y_done, c + 1)
            dve.wait_ge(q_done, k + 1)
            link(dve, dve.tensor_tensor(state, state, PS[:, 4 + q % 2, :].rearrange("p (a b) -> p a b", b=HD), ALU.add))
            dve.tensor_tensor(state, state, dend[:, :, PCHUNKS + k:PCHUNKS + k + 1].to_broadcast([P, PAIRS, HD]),
                              ALU.mult).then_inc(seq_ready, 1)

        @block.sync
        def _(sp):
            sp.dma_start(x[:], x_dram).then_inc(loaded, 16)
            sp.dma_start(vec[:], vec_dram).then_inc(loaded, 16)
            load_slot(sp, "gu0", 0)
            load_slot(sp, "gu0", 1)
            sp.dma_start(con[:], const_dram).then_inc(con_loaded, 16)
            sp.dma_start(cin[:], conv_dram).then_inc(con_loaded, 16)
            sp.dma_start(shin[:], shift_dram).then_inc(con_loaded, 16)
            load_phase(sp, "gu0", 2)
            load_phase(sp, "down0")
            mix_sp(sp)
            for name in order[4:]:
                load_phase(sp, name)
            sp.wait_ge(conv_u, 1)
            sp.dma_start(convo_out, stage[:]).then_inc(stored, 16)
            for k in range(KT):
                sp.wait_ge(y_ready, k + 1)
                sp.dma_start(y_out[k], cv[:, k, :]).then_inc(stored, 16)
            sp.wait_ge(stored, 16 * (KT + 1 + MIX_STORES))

        @block.gpsimd
        def _(pool):
            for par in range(2):
                split_pool(pool, 0, par, BIG)
            for name in order:
                if name == "mix":
                    mix_pool(pool)
                else:
                    split_phase_pool(pool, name)

        @block.scalar
        def _(act):
            for par in range(2):
                split_act(act, 0, par, BIG, slot_used, 2)
            for m in range(KT):
                res_act(act, 0, m, m % 2, m >= 2)
            ffn_act(act, 0)
            mix_act(act)
            ffn_act(act, 1)
            ffn_act(act, 2)
            conv_act(act)
            ffn_act(act, 3)
            norm_act(act, 6, TN)

        @block.vector
        def _(dve):
            dve.memset(tmp[7][:, 0:1], 0.0).then_inc(slot_used, 2)
            dve.memset(tmp[7][:, 1:2], 0.0).then_inc(scaled, 2)
            dve.memset(tmp[7][:, 2:3], 0.0).then_inc(lo_pool, 2)
            dve.memset(tmp[7][:, 3:4], 0.0).then_inc(lo_dve, 2)
            dve.wait_ge(loaded, 16 * 2)
            dve.memset(tmp[7][:, 4:5], 0.0).then_inc(x_new, 8)
            dve.wait_ge(x_new, 8)
            for par in range(2):
                split_dve(dve, 0, par, BIG)
            for m in range(KT):
                res_dve(dve, 0, m, m % 2, None, None, None)
                res_dve_after(dve, 0, m, m % 2, m == 0)
            ffn_dve(dve, 0)
            mix_dve(dve)
            ffn_dve(dve, 1)
            ffn_dve(dve, 2)
            conv_dve(dve)
            ffn_dve(dve, 3)
            final_dve(dve)

        @block.tensor
        def _(pe):
            pe.wait_ge(con_loaded, 16 * 3)
            ffn_pe(pe, 0)
            mix_pe(pe)
            ffn_pe(pe, 1)
            ffn_pe(pe, 2)
            conv_pe(pe)
            ffn_pe(pe, 3)
            final_pe(pe)


def _slots(w, pairs):
    import numpy as np
    w = np.asarray(w).reshape(KT, P, -1, P)
    return np.stack([np.stack([w[:, :, m] for m in pair], 2).transpose(1, 0, 2, 3).reshape(P, -1) for pair in pairs])


def _constants():
    import numpy as np
    c = np.zeros((P, NCONST), np.float32)
    head = np.arange(P) // HD
    c[:, K_ONES:K_ONES + P] = 1.0
    c[:, K_BLOCK:K_BLOCK + P] = head[:, None] == head[None, :]
    c[:, K_EYE:K_EYE + HD] = (np.arange(P) % HD)[:, None] == np.arange(HD)[None, :]
    for p in range(PAIRS):
        c[:, K_SEL + 16 * p:K_SEL + 16 * p + 16] = (2 * p + head)[:, None] == np.arange(16)[None, :]
        c[:HEADS, K_SELT + P * p:K_SELT + P * p + P] = np.arange(HEADS)[:, None] == (2 * p + head)[None, :]
    col = np.arange(TS)
    starts = (col % C == 0) | ((col >= PCHUNKS * C) & (col % STEPS == 0))
    c[:, K_SCAN:K_SCAN + TS] = ~starts
    s, t = (np.arange(P) % C)[:, None], np.arange(C)[None, :]
    z = c[:, K_ZMASK:K_ZMASK + CHUNKS * 2 * C].reshape(P, CHUNKS, 2, C)
    for n in range(CHUNKS):
        same = (s // STEPS == t // STEPS) | (n < PCHUNKS)
        z[:, n, 0] = (s < t) & same
        z[:, n, 1] = (s <= t) & same
    c[:, K_SEQCOL:K_SEQCOL + SPC * C] = (np.arange(C)[None, :] // STEPS == np.arange(SPC)[:, None]).reshape(1, -1)
    c[:, K_SEQROW:K_SEQROW + SPC] = s // STEPS == np.arange(SPC)[None, :]
    return c


_INPUTS = ("x", "vec", "const", "shift", "conv", "wkv", "gu", "down", "mix", "wo", "scin", "scout", "eye")
_OUTPUTS = {"y": (KT, P, SEQ + SEQS * STEPS), "wkvp": (P, PAIRS * HD), "wkvs": (SEQS, P, PAIRS * HD),
            "shifto": (P, KT * (1 + SEQS)), "convo": (P, KT * (2 + 2 * SEQS))}


def kernel(**a):
    import numpy as np
    import concourse.bacc as bacc
    from concourse.bass_utils import run_bass_kernel_spmd

    a = {k: np.asarray(v) for k, v in a.items()}
    f32 = np.float32

    def tiles(v):
        return v.reshape(-1, KT, P).transpose(2, 1, 0)

    tokens = np.concatenate([a["meta"], a["x_prompt"][0], a["x_sample"].reshape(SEQS * STEPS, D)], 0)
    vectors = np.concatenate([
        a["ffn_norm"].reshape(4, D), a["mix_norm"], a["final_norm"][None], a["rk_mu"][0], a["rk_w0"], a["rk_a0"],
        a["rk_k_k"], a["rk_k_a"], a["rk_r_k"].reshape(1, D), a["rk_ln_w"], a["rk_ln_b"], a["sc_conv_w"][0],
        np.zeros((1, D), f32)], 0)
    gu = a["ffn_w_gu"].reshape(4, D, 2 * FF)
    down = a["ffn_w_down"].reshape(4, 2, SMALL, P, KT, P).transpose(0, 4, 1, 3, 2, 5)
    g1, g2 = a["rk_g1"][0], a["rk_g2"][0]
    gz = np.zeros((D, 2 * P - g1.shape[1]), f32)
    g1 = np.concatenate([g1[:, :P], gz, g1[:, P:]], 1)
    g2 = np.concatenate([g2[:P], np.concatenate([np.zeros((2 * P - g2.shape[0], D), f32), g2[P:]], 0)], 1)

    def lora(w_in, w_out):
        w_in = np.concatenate([w_in, np.zeros((D, P - w_in.shape[1]), f32)], 1)
        w_out = np.concatenate([w_out, np.zeros((P - w_out.shape[0], D), f32)], 0)
        return np.concatenate([w_in.reshape(KT, P, P).transpose(1, 0, 2).reshape(P, -1), w_out], 1)[None]

    straight = [(2 * s, 2 * s + 1) for s in range(4)]
    r, k, v = (_slots(a["rk_w_rkv"][0, i], straight) for i in range(3))
    mix = np.concatenate([k, lora(a["rk_w1"][0], a["rk_w2"][0]), lora(a["rk_a1"][0], a["rk_a2"][0]),
                          _slots(g1, [(0, 1)]), r, v, g2[None]], 0)
    arrays = {
        "x": tiles(tokens),
        "vec": tiles(vectors),
        "const": _constants(),
        "shift": tiles(a["state_shift"][0]).reshape(P, -1),
        "conv": tiles(a["state_conv"][0].reshape(2 * SEQS, D)).reshape(P, -1),
        "wkv": a["state_wkv"][0].reshape(SEQS, PAIRS, 2, HD, HD).transpose(0, 2, 4, 1, 3).reshape(SEQS, P, -1),
        "gu": np.stack([_slots(gu[f], [(s, FT + s) for s in range(FT)]) for f in range(4)]),
        "down": down.reshape(4, 2 * KT, P, SMALL * P),
        "mix": mix,
        "wo": _slots(a["rk_w_o"][0], straight),
        "scin": _slots(a["sc_w_in"][0], [(KT + s, 2 * KT + s) for s in range(KT)] + straight),
        "scout": _slots(a["sc_w_out"][0], straight),
        "eye": np.broadcast_to(np.eye(C, dtype=f32).reshape(1, -1), (P, C * C)),
    }
    nc = bacc.Bacc("TRN2", target_bir_lowering=False, num_devices=1)
    arrays = {n: np.ascontiguousarray(arrays[n], dtype=f32) for n in _INPUTS}
    aps = [nc.dram_tensor(f"in_{n}", arrays[n].shape, F32, kind="ExternalInput").ap() for n in _INPUTS]
    outs = [nc.dram_tensor(f"out_{n}", s, F32, kind="ExternalOutput").ap() for n, s in _OUTPUTS.items()]
    scratch = [nc.dram_tensor(n, (CHUNKS, HEADS, C, C), F32).ap() for n in ("couplings", "inverses")]
    build_program(nc, *aps, *outs, *scratch)
    got = run_bass_kernel_spmd(nc, [{f"in_{n}": v for n, v in arrays.items()}], core_ids=[0]).results[0]
    y, wkvp, wkvs, shifto, convo = (got[f"out_{n}"] for n in _OUTPUTS)
    y = y.reshape(D, -1).T
    shifto = shifto.reshape(P, KT, -1).transpose(2, 1, 0).reshape(-1, D)
    convo = convo.reshape(P, KT, -1).transpose(2, 1, 0).reshape(-1, D)

    def states(s):
        return s.reshape(-1, 2, HD, PAIRS, HD).transpose(0, 3, 1, 4, 2).reshape(1, -1, HEADS, HD, HD)

    return (y[:SEQ].reshape(1, SEQ, D), y[SEQ:].reshape(SEQS, STEPS, D), states(wkvp), shifto[None, :1],
            convo[None, None, :2], states(wkvs), shifto[None, 1:], convo[2:].reshape(1, SEQS, 2, D))
```
